# Optimizing a Trainium2 kernel written in Bass

```python
import math
import jax
import jax.numpy as jnp
from jax import lax
import numpy as np

D_MODEL = 1024
BATCH = 1
SEQ = 1024
DEPTH = 1
DEC_BATCH = 8
DEC_SEQ = 1
PAST_LEN = 2048
PAGE_SIZE = 128

HEAD_DIM = 64
A_HEADS = 8
KV_HEADS = 2
GROUP = A_HEADS // KV_HEADS
CMP_STRIDE = 16
CMP_LEN = 2 * CMP_STRIDE
SEL_BLOCK = 64
N_SELECT = 16
WINDOW = 512
Q_BLOCK = 128
ATTN_SCALE = HEAD_DIM ** -0.5
B_HEADS = 8
B_DK = 128
B_DV = 64
HGRN_CHUNK = 32
D_FF = 4 * D_MODEL
DEEPNORM_ALPHA = (2.0 * DEPTH) ** 0.25
DEEPNORM_BETA = (8.0 * DEPTH) ** -0.25
LN_EPS = 1e-5
NEG = -1e30
FORCE = 1e6
Q_A = A_HEADS * HEAD_DIM
KV_A = 2 * KV_HEADS * HEAD_DIM
GATE_A = 3 * A_HEADS
Q_B = B_HEADS * B_DK
F_B = B_HEADS * B_DK
I_B = B_HEADS * B_DV
G_B = B_HEADS * B_DV
MERGE = 2 * D_MODEL
SPLITS = (Q_A, KV_A, KV_A, KV_A, GATE_A, Q_B, F_B, I_B, G_B, MERGE)
D_IN = Q_A + 3 * KV_A + GATE_A + Q_B + F_B + I_B + G_B + MERGE

kernel_name = 'nsa_hgrn2_deepnorm_hybrid_step'

def layer_norm(x, g, b):
    xf = x.astype(jnp.float32)
    mu = jnp.mean(xf, axis=-1, keepdims=True)
    var = jnp.mean(jnp.square(xf - mu), axis=-1, keepdims=True)
    y = (xf - mu) * lax.rsqrt(var + LN_EPS) * g.astype(jnp.float32) + b.astype(jnp.float32)
    return y.astype(x.dtype)

def alibi_slopes():
    h = jnp.arange(1, A_HEADS + 1, dtype=jnp.float32)
    return jnp.exp2(-8.0 * h / A_HEADS).reshape(KV_HEADS, GROUP)

def masked_softmax(s, mask):
    s = jnp.where(mask, s.astype(jnp.float32), NEG)
    m = jnp.max(s, axis=-1, keepdims=True)
    p = jnp.where(mask, jnp.exp(s - m), 0.0)
    return p / jnp.maximum(jnp.sum(p, axis=-1, keepdims=True), 1e-30)

def split_projection(x, w_in):
    b, t = x.shape[:2]
    h = jnp.einsum('bsd,de->bse', x, w_in)
    parts = []
    off = 0
    for n in SPLITS:
        parts.append(h[..., off:off + n])
        off += n
    qa, kvc, kvs, kvw, gla, qb, fb, ib, gb, mg = parts
    kv = lambda a: a.reshape(b, t, 2, KV_HEADS, HEAD_DIM)
    return (qa.reshape(b, t, KV_HEADS, GROUP, HEAD_DIM), kv(kvc), kv(kvs), kv(kvw),
            gla.reshape(b, t, KV_HEADS, GROUP, 3), qb, fb, ib, gb, mg)

def chunk_parts(kv, cmp_w):
    b, L = kv.shape[:2]
    n_ch = L // CMP_STRIDE
    ch = kv[:, :n_ch * CMP_STRIDE].reshape(b, n_ch, CMP_STRIDE, 2, KV_HEADS, HEAD_DIM)
    w = cmp_w.reshape(2, CMP_LEN // CMP_STRIDE, CMP_STRIDE, HEAD_DIM, HEAD_DIM)
    return jnp.einsum('bnlcgd,cplde->bnpcge', ch, w)

def blocks_from_parts(parts, cmp_w, cmp_pos):
    bias = jnp.einsum('cld,clde->ce', cmp_pos, cmp_w)
    return parts[:, :-1, 0] + parts[:, 1:, 1] + bias[None, None, :, None, :]

def compressed_branch(qg, pos_q, kv_cmp, slopes):
    n = kv_cmp.shape[1]
    end = jnp.arange(n) * CMP_STRIDE + (CMP_LEN - 1)
    dist = (pos_q[:, None] - end[None, :]).astype(jnp.float32)
    s = jnp.einsum('bqgrd,bngd->bqgrn', qg, kv_cmp[:, :, 0]).astype(jnp.float32) * ATTN_SCALE
    s = s - slopes[:, :, None] * dist[None, :, None, None, :]
    p = masked_softmax(s, (dist >= 0)[None, :, None, None, :])
    o = jnp.einsum('bqgrn,bngd->bqgrd', p.astype(kv_cmp.dtype), kv_cmp[:, :, 1])
    return o, p

def select_blocks(p_cmp, pos_q, n_sel):
    imp = jnp.sum(p_cmp, axis=3)
    ratio = SEL_BLOCK // CMP_STRIDE
    imp = jnp.pad(imp, ((0, 0), (0, 0), (0, 0), (0, n_sel * ratio - imp.shape[-1])))
    imp = jnp.sum(imp.reshape(*imp.shape[:-1], n_sel, ratio), axis=-1)
    blk = jnp.arange(n_sel)
    cur = (pos_q // SEL_BLOCK)[:, None]
    forced = (blk[None, :] == 0) | (blk[None, :] == cur) | (blk[None, :] == cur - 1)
    allowed = blk[None, :] * SEL_BLOCK <= pos_q[:, None]
    score = jnp.where(forced[None, :, None, :], FORCE, imp)
    score = jnp.where(allowed[None, :, None, :], score, -FORCE)
    vals, idx = lax.top_k(score, min(N_SELECT, n_sel))
    return idx, vals > -0.5 * FORCE

def selected_branch(qg, pos_q, kv_g, idx, valid, slopes):
    b, q, g = qg.shape[:3]
    nk = idx.shape[-1] * SEL_BLOCK
    pos_k = (idx[..., None] * SEL_BLOCK + jnp.arange(SEL_BLOCK)).reshape(b, q, g, nk)
    dist = (pos_q[None, :, None, None] - pos_k).astype(jnp.float32)
    mask = jnp.repeat(valid, SEL_BLOCK, axis=-1) & (dist >= 0)
    k = kv_g[..., 0, :].reshape(b, q, g, nk, HEAD_DIM)
    v = kv_g[..., 1, :].reshape(b, q, g, nk, HEAD_DIM)
    s = jnp.einsum('bqgrd,bqgmd->bqgrm', qg, k).astype(jnp.float32) * ATTN_SCALE
    s = s - slopes[:, :, None] * dist[:, :, :, None, :]
    p = masked_softmax(s, mask[:, :, :, None, :])
    return jnp.einsum('bqgrm,bqgmd->bqgrd', p.astype(v.dtype), v)

def window_branch(qg, pos_q, kv_w, pos_k, slopes):
    dist = pos_q[:, None] - pos_k[None, :]
    mask = (dist >= 0) & (dist < WINDOW) & (pos_k[None, :] >= 0)
    s = jnp.einsum('bqgrd,bkgd->bqgrk', qg, kv_w[:, :, 0]).astype(jnp.float32) * ATTN_SCALE
    s = s - slopes[:, :, None] * dist.astype(jnp.float32)[None, :, None, None, :]
    p = masked_softmax(s, mask[None, :, None, None, :])
    return jnp.einsum('bqgrk,bkgd->bqgrd', p.astype(kv_w.dtype), kv_w[:, :, 1])

def gate_branches(gl, o_c, o_s, o_w):
    g = jax.nn.sigmoid(gl.astype(jnp.float32))
    o = g[..., 0:1] * o_c + g[..., 1:2] * o_s + g[..., 2:3] * o_w
    return o.astype(o_c.dtype)

def nsa_prompt(qg, kvc, kvs, kvw, gl, cmp_w, cmp_pos):
    b, t = qg.shape[:2]
    slopes = alibi_slopes()
    kv_cmp = blocks_from_parts(chunk_parts(kvc, cmp_w), cmp_w, cmp_pos)
    n_sel = -(-t // SEL_BLOCK)
    kv_sel_blk = kvs.reshape(b, n_sel, SEL_BLOCK, 2, KV_HEADS, HEAD_DIM)
    kv_w_pad = jnp.pad(kvw, ((0, 0), (WINDOW, 0), (0, 0), (0, 0), (0, 0)))
    b_ix = jnp.arange(b)[:, None, None, None]
    g_ix = jnp.arange(KV_HEADS)[None, None, :, None]

    def query_block(c):
        t0 = c * Q_BLOCK
        pos_q = t0 + jnp.arange(Q_BLOCK)
        qb = lax.dynamic_slice_in_dim(qg, t0, Q_BLOCK, axis=1)
        gb = lax.dynamic_slice_in_dim(gl, t0, Q_BLOCK, axis=1)
        o_c, p_c = compressed_branch(qb, pos_q, kv_cmp, slopes)
        idx, valid = select_blocks(p_c, pos_q, n_sel)
        kv_g = kv_sel_blk[b_ix, idx, :, :, g_ix]
        o_s = selected_branch(qb, pos_q, kv_g, idx, valid, slopes)
        kv_wb = lax.dynamic_slice_in_dim(kv_w_pad, t0, WINDOW + Q_BLOCK, axis=1)
        pos_k = t0 - WINDOW + jnp.arange(WINDOW + Q_BLOCK)
        o_w = window_branch(qb, pos_q, kv_wb, pos_k, slopes)
        return gate_branches(gb, o_c, o_s, o_w)

    out = lax.map(query_block, jnp.arange(t // Q_BLOCK))
    out = jnp.swapaxes(out, 0, 1).reshape(b, t, Q_A)
    new_win = kvw[:, -min(WINDOW, t):]
    return out, new_win

def nsa_sample(qg, kvc, kvs, kvw, gl, cache_cmp, cache_sel, cache_win, page_table, cmp_w, cmp_pos):
    b, t = qg.shape[:2]
    slopes = alibi_slopes()
    n_pages = page_table.shape[1]
    past = n_pages * PAGE_SIZE
    pos_q = past + jnp.arange(t)
    b_ix = jnp.arange(b)[:, None, None, None]
    g_ix = jnp.arange(KV_HEADS)[None, None, :, None]
    past_c = cache_cmp[page_table].reshape(b, past, 2, KV_HEADS, HEAD_DIM)
    parts = jnp.concatenate([chunk_parts(past_c, cmp_w), chunk_parts(kvc, cmp_w)], axis=1)
    kv_cmp = blocks_from_parts(parts, cmp_w, cmp_pos)
    o_c, p_c = compressed_branch(qg, pos_q, kv_cmp, slopes)
    n_sel = -(-(past + t) // SEL_BLOCK)
    idx, valid = select_blocks(p_c, pos_q, n_sel)
    n_past_blk = past // SEL_BLOCK
    blk_per_page = PAGE_SIZE // SEL_BLOCK
    in_past = idx < n_past_blk
    pblk = jnp.minimum(idx, n_past_blk - 1)
    phys = page_table[b_ix, pblk // blk_per_page]
    rows = (pblk % blk_per_page)[..., None] * SEL_BLOCK + jnp.arange(SEL_BLOCK)
    from_pool = cache_sel[phys[..., None], rows, :, g_ix[..., None]]
    n_new_blk = -(-t // SEL_BLOCK)
    tail = jnp.pad(kvs, ((0, 0), (0, n_new_blk * SEL_BLOCK - t), (0, 0), (0, 0), (0, 0)))
    tail = tail.reshape(b, n_new_blk, SEL_BLOCK, 2, KV_HEADS, HEAD_DIM)
    nblk = jnp.clip(idx - n_past_blk, 0, n_new_blk - 1)
    from_tail = tail[b_ix, nblk, :, :, g_ix]
    kv_g = jnp.where(in_past[..., None, None, None], from_pool, from_tail)
    o_s = selected_branch(qg, pos_q, kv_g, idx, valid, slopes)
    w_buf = cache_win.shape[1]
    kv_w = jnp.concatenate([cache_win.astype(kvw.dtype), kvw], axis=1)
    pos_k = past - w_buf + jnp.arange(w_buf + t)
    o_w = window_branch(qg, pos_q, kv_w, pos_k, slopes)
    out = gate_branches(gl, o_c, o_s, o_w).reshape(b, t, Q_A)
    new_win = kv_w[:, -min(WINDOW, w_buf + t):]
    return out, new_win

def hgrn_chunked(q, k, v, log_f, s0):
    b, t = q.shape[:2]
    nc = t // HGRN_CHUNK
    to_chunks = lambda a: jnp.swapaxes(a.reshape(b, nc, HGRN_CHUNK, *a.shape[2:]), 0, 1)
    tril = jnp.tril(jnp.ones((HGRN_CHUNK, HGRN_CHUNK), dtype=bool))

    def step(s, inp):
        qc, kc, vc, lf = inp
        lc = jnp.cumsum(lf, axis=1)
        qt = qc * jnp.exp(lc)
        kt = kc * jnp.exp(-lc)
        a = jnp.where(tril, jnp.einsum('bchk,bshk->bhcs', qt, kt), 0.0)
        o = jnp.einsum('bhcs,bshv->bchv', a, vc) + jnp.einsum('bchk,bhkv->bchv', qt, s)
        lend = lc[:, -1]
        s = jnp.exp(lend)[..., None] * s + jnp.einsum('bshk,bshv->bhkv', kc * jnp.exp(lend[:, None] - lc), vc)
        return s, o

    s, o = lax.scan(step, s0, (to_chunks(q), to_chunks(k), to_chunks(v), to_chunks(log_f)))
    return jnp.swapaxes(o, 0, 1).reshape(b, t, B_HEADS, B_DV), s

def hgrn_recurrent(q, k, v, log_f, s0):
    def step(s, inp):
        qt, kt, vt, lft = inp
        s = jnp.exp(lft)[..., None] * s + kt[..., None] * vt[..., None, :]
        return s, jnp.einsum('bhk,bhkv->bhv', qt, s)

    s, o = lax.scan(step, s0, (jnp.swapaxes(q, 0, 1), jnp.swapaxes(k, 0, 1),
                              jnp.swapaxes(v, 0, 1), jnp.swapaxes(log_f, 0, 1)))
    return jnp.swapaxes(o, 0, 1), s

def hgrn_mixer(qb, fb, ib, gb, lb, norm_g, s0, chunked):
    b, t = qb.shape[:2]
    f32 = jnp.float32
    q = qb.reshape(b, t, B_HEADS, B_DK).astype(f32)
    lbh = lb.reshape(B_HEADS, B_DK)
    f = lbh + (1.0 - lbh) * jax.nn.sigmoid(fb.reshape(b, t, B_HEADS, B_DK).astype(f32))
    log_f = jnp.log(f)
    k = 1.0 - f
    v = ib.reshape(b, t, B_HEADS, B_DV).astype(f32)
    if chunked:
        o, s = hgrn_chunked(q, k, v, log_f, s0.astype(f32))
    else:
        o, s = hgrn_recurrent(q, k, v, log_f, s0.astype(f32))
    o = o * lax.rsqrt(jnp.mean(jnp.square(o), axis=-1, keepdims=True) + LN_EPS) * norm_g.astype(f32)
    o = o.reshape(b, t, I_B) * jax.nn.silu(gb.astype(f32))
    return o.astype(qb.dtype), s

def merge_and_mlp(x, o_a, o_b, mg, w_br_a, w_br_b, w_out, ln1_g, ln1_b, w_up, w_down, ln2_g, ln2_b):
    br_a = jnp.einsum('bse,ed->bsd', o_a, w_br_a)
    br_b = jnp.einsum('bse,ed->bsd', o_b, w_br_b)
    merged = jax.nn.sigmoid(mg[..., :D_MODEL]) * br_a + jax.nn.sigmoid(mg[..., D_MODEL:]) * br_b
    mix = jnp.einsum('bsd,de->bse', merged, w_out)
    x1 = layer_norm(DEEPNORM_ALPHA * x + mix, ln1_g, ln1_b)
    h = jnp.einsum('bsf,fd->bsd', jnp.square(jax.nn.relu(jnp.einsum('bsd,df->bsf', x1, w_up))), w_down)
    return layer_norm(DEEPNORM_ALPHA * x1 + h, ln2_g, ln2_b)

def setup_inputs(seed: int = 0) -> dict:
    key = jax.random.key(seed)
    ks = jax.random.split(key, 24)
    f32 = jnp.float32
    nrm = lambda k, shape, scale: scale * jax.random.normal(k, shape, f32)
    n_pages = PAST_LEN // PAGE_SIZE
    n_pool = (5 * DEC_BATCH * n_pages) // 4
    win_buf = min(WINDOW, PAST_LEN)
    page_table = jax.random.permutation(ks[0], n_pool)[:DEC_BATCH * n_pages]
    page_table = page_table.reshape(DEC_BATCH, n_pages).astype(jnp.int32)
    return {
        'x_prompt': nrm(ks[1], (BATCH, SEQ, D_MODEL), 1.0),
        'x_sample': nrm(ks[2], (DEC_BATCH, DEC_SEQ, D_MODEL), 1.0),
        'cache_cmp_kv': nrm(ks[3], (DEPTH, n_pool, PAGE_SIZE, 2, KV_HEADS, HEAD_DIM), 1.0),
        'cache_sel_kv': nrm(ks[4], (DEPTH, n_pool, PAGE_SIZE, 2, KV_HEADS, HEAD_DIM), 1.0),
        'cache_win_kv': nrm(ks[5], (DEPTH, DEC_BATCH, win_buf, 2, KV_HEADS, HEAD_DIM), 1.0),
        'state_hgrn': nrm(ks[6], (DEPTH, DEC_BATCH, B_HEADS, B_DK, B_DV), 0.1),
        'page_table': page_table,
        'w_in': nrm(ks[7], (DEPTH, D_MODEL, D_IN), D_MODEL ** -0.5),
        'cmp_w': nrm(ks[8], (DEPTH, 2, CMP_LEN, HEAD_DIM, HEAD_DIM), (CMP_LEN * HEAD_DIM) ** -0.5),
        'cmp_pos': nrm(ks[9], (DEPTH, 2, CMP_LEN, HEAD_DIM), 0.5),
        'hgrn_lb_logits': nrm(ks[10], (DEPTH + 1, B_HEADS * B_DK), 0.5),
        'hgrn_norm_g': 1.0 + nrm(ks[11], (DEPTH, B_DV), 0.02),
        'w_br_a': nrm(ks[12], (DEPTH, Q_A, D_MODEL), DEEPNORM_BETA * Q_A ** -0.5),
        'w_br_b': nrm(ks[13], (DEPTH, I_B, D_MODEL), DEEPNORM_BETA * I_B ** -0.5),
        'w_out': nrm(ks[14], (DEPTH, D_MODEL, D_MODEL), DEEPNORM_BETA * D_MODEL ** -0.5),
        'ln1_g': 1.0 + nrm(ks[15], (DEPTH, D_MODEL), 0.02),
        'ln1_b': nrm(ks[16], (DEPTH, D_MODEL), 0.02),
        'w_up': nrm(ks[17], (DEPTH, D_MODEL, D_FF), DEEPNORM_BETA * D_MODEL ** -0.5),
        'w_down': nrm(ks[18], (DEPTH, D_FF, D_MODEL), DEEPNORM_BETA * D_FF ** -0.5),
        'ln2_g': 1.0 + nrm(ks[19], (DEPTH, D_MODEL), 0.02),
        'ln2_b': nrm(ks[20], (DEPTH, D_MODEL), 0.02),
    }

def reference(x_prompt, x_sample, cache_cmp_kv, cache_sel_kv, cache_win_kv, state_hgrn, page_table,
              w_in, cmp_w, cmp_pos, hgrn_lb_logits, hgrn_norm_g, w_br_a, w_br_b, w_out,
              ln1_g, ln1_b, w_up, w_down, ln2_g, ln2_b):
    lb_all = jnp.cumsum(jax.nn.softmax(hgrn_lb_logits.astype(jnp.float32), axis=0), axis=0)
    xp, xs = x_prompt, x_sample
    cmp_p, sel_p, win_p, hg_p = [], [], [], []
    cmp_s, sel_s, win_s, hg_s = [], [], [], []
    for l in range(DEPTH):
        qa, kvc, kvs, kvw, gla, qb, fb, ib, gb, mg = split_projection(xp, w_in[l])
        o_a, nw = nsa_prompt(qa, kvc, kvs, kvw, gla, cmp_w[l], cmp_pos[l])
        s0 = jnp.zeros((xp.shape[0], B_HEADS, B_DK, B_DV), jnp.float32)
        o_b, s_end = hgrn_mixer(qb, fb, ib, gb, lb_all[l], hgrn_norm_g[l], s0, True)
        xp = merge_and_mlp(xp, o_a, o_b, mg, w_br_a[l], w_br_b[l], w_out[l], ln1_g[l], ln1_b[l],
                           w_up[l], w_down[l], ln2_g[l], ln2_b[l])
        cmp_p.append(kvc)
        sel_p.append(kvs)
        win_p.append(nw)
        hg_p.append(s_end.astype(x_prompt.dtype))
        qa, kvc, kvs, kvw, gla, qb, fb, ib, gb, mg = split_projection(xs, w_in[l])
        o_a, nw = nsa_sample(qa, kvc, kvs, kvw, gla, cache_cmp_kv[l], cache_sel_kv[l], cache_win_kv[l],
                             page_table, cmp_w[l], cmp_pos[l])
        o_b, s_end = hgrn_mixer(qb, fb, ib, gb, lb_all[l], hgrn_norm_g[l], state_hgrn[l], False)
        xs = merge_and_mlp(xs, o_a, o_b, mg, w_br_a[l], w_br_b[l], w_out[l], ln1_g[l], ln1_b[l],
                           w_up[l], w_down[l], ln2_g[l], ln2_b[l])
        cmp_s.append(kvc)
        sel_s.append(kvs)
        win_s.append(nw)
        hg_s.append(s_end.astype(x_sample.dtype))
    return (xp, xs,
            jnp.stack(cmp_p), jnp.stack(sel_p), jnp.stack(win_p), jnp.stack(hg_p),
            jnp.stack(cmp_s), jnp.stack(sel_s), jnp.stack(win_s), jnp.stack(hg_s))


_drawn_inputs = setup_inputs


def setup_inputs(seed=0):
    import zlib

    import numpy as np

    out = dict(_drawn_inputs(seed))
    spreads = {}
    factors = {'cache_sel_kv': 2.897,
     'hgrn_norm_g': 34.294,
     'ln1_g': 7.776,
     'ln1_b': 7.728,
     'ln2_g': 22.982,
     'ln2_b': 23.749,
     'cache_cmp_kv': 2.855,
     'cmp_pos': 3.538}
    for name, (base, spread) in spreads.items():
        noise = np.random.default_rng([zlib.crc32(name.encode()), seed]).standard_normal(out[name].shape)
        drawn = base * np.exp(spread * noise) if base else spread * noise
        out[name] = jnp.asarray(drawn.astype(out[name].dtype))
    for name, factor in factors.items():
        out[name] = (out[name] * factor).astype(out[name].dtype)
    return out
```

```python
from contextlib import ExitStack

import numpy as np

import concourse.bass as bass
from concourse import mybir

F32 = mybir.dt.float32
I32 = mybir.dt.int32
U32 = mybir.dt.uint32
ALU = mybir.AluOpType
ACT = mybir.ActivationFunctionType
AX = mybir.AxisListType

P = 128
D = 1024
KD = D // P
SEQ = 1024
NQ = SEQ // P
NB = 8
T = SEQ + NB
HD = 64
GROUPS = 2
PAGES = 16
PAST = 2048
STRIDE = 16
NCMP_P = SEQ // STRIDE
NCMP_S = PAST // STRIDE
CMP_LEN = 32
WINDOW = 512
SEL_BLOCK = 64
N_SELECT = 16
NBLK_S = PAST // SEL_BLOCK + 1
HG = 8
DV = 64
CH = 32
NCH = SEQ // CH
F_FF = 4096
NEG = -1e30
FORCE = 1e6
LN_EPS = 1e-5
ALPHA = 2.0 ** 0.25
NROW = NB * 8

C_QA, C_KV, C_GLA, C_QB = 0, 512, 1280, 1304
C_FB, C_IB, C_GB, C_MG = C_QB + 1024, C_QB + 2048, C_QB + 2560, C_QB + 3072

CONSTS = {}


def constants():
    parts = {}

    def put(name, a):
        full = np.zeros((P, int(np.prod(a.shape[1:]))), np.float32)
        full[:a.shape[0]] = a.reshape(a.shape[0], -1)
        parts[name] = full

    p = np.arange(P)
    put("ident", np.eye(P))
    put("causal", np.where(p[None, :] <= p[:, None], 0.0, NEG))
    put("winlow", np.where(p[None, :] > p[:, None], 0.0, NEG))
    n = np.arange(NCMP_P)
    end = STRIDE * n + CMP_LEN - 1
    pos = P * np.arange(NQ)[None, :, None] + p[:, None, None]
    put("cmpmask", np.where((n < NCMP_P - 1) & (end <= pos), 0.0, NEG))
    put("hgmask", ((p[:, None] // CH == p[None, :] // CH) & (p[:, None] <= p[None, :])).astype(np.float32))
    put("fresh", np.broadcast_to((np.arange(SEQ) % CH != 0).astype(np.float32), (P, SEQ)))
    row = np.arange(NROW)
    put("gsum", (row[:, None] // 4 == np.arange(16)[None, :]).astype(np.float32))
    put("gspread", (row[None, :] // 4 == np.arange(16)[:, None]).astype(np.float32))
    b = np.arange(NBLK_S)
    put("below", np.broadcast_to((b[None, None, :] < b[None, :, None]), (16, NBLK_S, NBLK_S)).astype(np.float32))
    forced = (b == 0) | (b == NBLK_S - 1) | (b == NBLK_S - 2)
    put("free", np.broadcast_to(np.where(forced, 0.0, 1.0), (16, NBLK_S)))
    put("forced", np.broadcast_to(np.where(forced, FORCE, 0.0), (16, NBLK_S)))
    put("ownT", (row[None, :] // 8 == np.arange(NB)[:, None]).astype(np.float32))
    put("headsel", (row[:, None] % 8 == np.arange(8)[None, :]).astype(np.float32))
    put("pagespread", (p[None, :] // 8 == np.arange(PAGES)[:, None]).astype(np.float32))
    put("own", (row[:, None] // 8 == np.arange(NB)[None, :]).astype(np.float32))
    put("rowb", np.repeat(np.eye(NB)[:, :, None], P, axis=2))
    put("half", np.stack([2.0 * (p % 8), 2.0 * (p % 8) + 1], axis=1))
    at, out = 0, []
    for name, a in parts.items():
        CONSTS[name] = (at, a.shape[1])
        at += a.shape[1]
        out.append(a)
    return np.concatenate(out, axis=1)


def positions():
    end = STRIDE * np.arange(NCMP_P) + CMP_LEN - 1
    return np.concatenate([np.arange(SEQ), end, end]).astype(np.float32)[None, :]


def decode_biases():
    slope = 2.0 ** -(np.arange(NROW) % 8 + 1.0)
    l, c = np.arange(STRIDE), np.arange(NCMP_S)
    sel = slope[:, None, None] * (STRIDE * c[None, None, :] + l[None, :, None] - PAST)
    wpos = PAST - WINDOW + 4 * np.arange(P)[None, None, :] + np.arange(4)[None, :, None]
    win = np.where(PAST - wpos < WINDOW, slope[:, None, None] * (wpos - PAST), NEG)
    cmp = np.where(c < NCMP_S - 1, slope[:, None] * (STRIDE * c + CMP_LEN - 1 - PAST), NEG)
    zero = np.zeros((NROW, 1))
    return np.concatenate([sel.reshape(NROW, -1), zero, win.reshape(NROW, -1), zero, cmp], axis=1).astype(np.float32)


class Steps:

    def __init__(self, eng, sem):
        self.eng, self.sem, self.n = eng, sem, 0

    def __call__(self, ins):
        ins.then_inc(self.sem, 1)
        self.n += 1
        self.eng.wait_ge(self.sem, self.n)


def hybrid_step(nc, x_p, x_s, c_cmp, c_sel, c_win, state, table, w_in, cmp_w, cmp_pos, lb_logits, norm_g,
                w_br_a, w_br_b, w_out, ln1_g, ln1_b, w_up, w_down, ln2_g, ln2_b, consts, kpos, dbias,
                y_p, y_s_out, cmp_p, sel_p, win_p, hg_p, cmp_s, sel_s, win_s, hg_s):
    with ExitStack() as ctx:
        def sb(name, shape, dt=F32):
            return ctx.enter_context(nc.sbuf_tensor(name, shape, dt))

        def sem(name):
            return ctx.enter_context(nc.semaphore(name))

        NC_ = consts.shape[1]
        K = sb("consts_sb", [P, NC_])

        def const(name, rows=P):
            at, n = CONSTS[name]
            return K[0:rows, at:at + n]

        ident = const("ident")
        xT = sb("xT", [P, KD, T])
        aT = sb("aT", [P, 4, T])
        WR = 4
        wring = sb("wring", [P, WR, KD, P])
        ARENA = 32200
        arena = sb("arena", [P, ARENA])
        PS = ctx.enter_context(nc.psum_tensor("PS", [P, 8, 512], F32))

        def view(at, *dims, rows=P, base=0):
            n = int(np.prod(dims))
            assert at + n <= ARENA, (at, n)
            v = arena[base:base + rows, at:at + n]
            names = "abcd"[:len(dims)]
            if len(dims) > 1:
                v = v.rearrange(f"p ({' '.join(names)}) -> p {' '.join(names)}",
                                **{names[i]: dims[i] for i in range(1, len(dims))})
            return v

        o = 0
        gates = view(o, NQ + 1, 24); o += (NQ + 1) * 24
        cw2 = view(o, 2, 8, P); o += 2 * 8 * P
        cpos = view(o, 2, 16); o += 32
        cb = view(o, 2); o += 2
        small = view(o, 64); o += 64
        kvd = view(o, 768, rows=NB); o += 768
        qbd = view(o, NB, NROW); o += NB * NROW
        knew = view(o, 2, NB); o += 2 * NB
        o_kept = o
        hA = view(o, 10, T); o += 10 * T
        kvtok = view(o, NQ, 768); o += NQ * 768
        kcA = view(o, 2, NCMP_P, rows=65); o += 2 * NCMP_P
        vcN = view(o, 2, HD, rows=NCMP_P); o += 2 * HD
        cw64 = view(o, 2, STRIDE, P)
        kA = view(o, 2, 2, SEQ, rows=65); o += 4 * SEQ
        hG = view(o, T, rows=24)
        cmpT = view(o, 4, NCMP_P, rows=HD)
        cmpK = view(o + 256, 4, NCMP_P, rows=HD)
        PT = view(o, 2, 2, 512)
        o += 4 * 512
        qS = view(o, 2, SEQ, rows=65); o += 2 * SEQ
        pr = view(o, 2, SEQ); o += 2 * SEQ
        xs = view(o - 3 * SEQ, 3, D)

        ph = sem("phase_done")
        c_in = sem("consts_loaded")
        x_in = [sem(f"x_in{i}") for i in range(3)]
        xt_ps, xt_act, xt_dve = sem("xt_turned"), sem("xt_copied_act"), sem("xt_copied_dve")
        w_in_s = [sem(f"w_loaded{i}") for i in range(WR)]
        u_ps, u_act = sem("unit_chunk_ready"), sem("unit_chunk_copied")
        kt_ps, kt_dve = sem("kv_turned"), sem("kv_copied")
        kv_out, shift_out = sem("kv_stored"), sem("window_shifted")
        cw_in = sem("cmp_weights_loaded")
        cp_ps, cp_act, cp_dve = sem("cmp_parts_ready"), sem("cmp_copied_act"), sem("cmp_steps_dve")
        ka_s = sem("k_staged")
        q_s, ss_ps, e_act, m_dve, p_dve, q_row = (sem("q_staged"), sem("scores_ready"), sem("exp_done"), sem("max_done"),
                                      sem("probs_scaled"), sem("slope_row_set"))
        dch = sem("dve_steps")
        t_ps, t_act, t_dve, pv_ps, o_act = (sem("probs_turned"), sem("probs_copied_act"), sem("probs_copied_dve"),
                                            sem("pv_groups_done"), sem("attn_out_copied"))

        def toks(t):
            return P if t < NQ else NB

        wv = w_in[0].rearrange("(k p) c -> p k c", p=P)
        units = [(wv, C_QA + P * i, P, hA[:, i, :], ACT.Copy) for i in range(10)]
        units += [(wv, C_GLA, 24, hG, ACT.Sigmoid)]
        NU_ATT = len(units)
        CHUNKS = [(0, 512), (512, 512), (SEQ, NB)]

        def unit_out(n, ci, m):
            return PS[0:m, 2 * (n % 2) + ci, :] if ci < 2 else PS[0:m, 4, 0:NB]

        heads = [(h, i) for h in range(8) for i in range(NQ)]
        NJ = 2 * len(heads)

        def job(j):
            h, i = heads[j // 2]
            return h, i, j % 2

        def blocks(j):
            h, i, wc = job(j)
            if not wc:
                return [(0, P * b, P, P * b) for b in range(i + 1)]
            lo = max(0, i - 4)
            return [(1, P * b, P, P * (b - lo)) for b in range(lo, i + 1)] + [(2, 0, NCMP_P, 640)]

        def groups(j):
            bl = blocks(j)
            return [bl[:4]] + ([bl[4:]] if len(bl) > 4 else [])

        first_group = [0]
        second_groups = [0]
        for j in range(NJ):
            first_group.append(first_group[-1] + len(groups(j)))
            second_groups.append(second_groups[-1] + len(groups(j)) - 1)

        def evacuations(gr):
            full = sum(n == P for _, _, n, _ in gr)
            return [(P, 0, P * full)] * (full > 0) + [(NCMP_P, P * full, P * (full + 1))] * (full < len(gr))

        def exps(j):
            return 3 * (j // 2) + (1 if j % 2 == 0 else 3)

        NSEL, NWIN = PAST + 1, WINDOW + 1
        o = o_kept
        raw = view(o, 2, 8 * 256); o += 2 * 8 * 256
        raww = view(o - 4096, NB, 4, P)
        ktd = view(o, 2, 512); o += 1024
        Prow = view(o, NSEL + NWIN + NCMP_S, rows=NROW)
        rk1 = view(o, NBLK_S, NBLK_S, rows=16)
        rk2 = view(o + NBLK_S * NBLK_S, NBLK_S, NBLK_S, rows=16)
        o += NSEL + NWIN + NCMP_S
        P_sel, P_win, P_cmp = Prow[:, 0:NSEL], Prow[:, NSEL:NSEL + NWIN], Prow[:, NSEL + NWIN:]
        cmpbias = view(o, NCMP_S, rows=NROW); o += NCMP_S
        kcd = view(o, NB, NCMP_S); o += NB * NCMP_S
        vcd = view(o, NB, P); o += NB * P
        g64 = view(o, 24, rows=NROW); o += 24
        grow = view(o, 4, rows=NROW); o += 4
        idx = view(o, 2, NB).bitcast(U32); o += 16
        tabi = view(o, NB, rows=PAGES).bitcast(I32); o += NB
        tabf = view(o, NB, rows=PAGES); o += NB
        dsm = view(o, 32, rows=NROW); o += 32
        blkm = view(o, 4, NBLK_S, rows=16); o += 4 * NBLK_S
        mb64 = view(o, NBLK_S - 1, rows=NROW); o += NBLK_S - 1
        pnew = view(o, 2, NB, rows=NROW); o += 16
        pnewT = view(o, 2, NROW, rows=NB); o += 128
        xt2 = view(o, 2, 2048)
        tmp1 = view(o + 4096, 2, 2, NCMP_S, rows=HD)
        vct = view(o + 4608, 2, NCMP_S)
        vall = view(o, NB, STRIDE, P)
        o += NB * STRIDE * P
        ptdv = view(o, 21, NROW)
        tb_in, ix_s = sem("table_loaded"), sem("row_index_ready")
        raw_in = [sem(f"pages_loaded{i}") for i in range(2)]
        cx_act, cx_dve = sem("chunks_copied_act"), sem("chunks_copied_dve")

        def xt_of(n, c, par, g):
            return xt2[HD * par:HD * (par + 1), n % 2, 1024 * c:1024 * (c + 1)].rearrange(
                "p (q g n) -> p q g n", q=4, g=2)[:, :, g, :]

        d_ps, d_act, d_dve = sem("turned_pages"), sem("turned_copied_act"), sem("turned_copied_dve")
        dc_ps, kv_a, kv_d = sem("cmp_products"), sem("cmp_part1_copied"), sem("cmp_blocks_built")
        vc_ps, vc_s = sem("cmp_v_turned"), sem("cmp_v_copied")
        pe_r, act_r, dve_r, v_s = (sem("pe_results"), sem("act_results"), sem("dve_results"), sem("v_copied"))
        bias_in, rank_s, wv_in = sem("bias_loaded"), sem("rank_done"), sem("window_v_loaded")
        wraw_in = [sem(f"window_loaded{i}") for i in range(2)]
        sc_ps, dst2 = sem("decode_scores"), sem("decode_steps")
        o = 0
        rT = view(o, 4, T); o += 4 * T
        gbs = view(o, 4, T); o += 4 * T
        vt = view(o, NQ, 512); o += NQ * 512
        vdec = view(o, 512, rows=NB); o += 512
        fT = view(o, 2, T); o += 2 * T
        qT = view(o, 2, T); o += 2 * T
        kf = view(o, T); o += T
        lfb = view(o, SEQ); o += SEQ
        lcb = view(o, SEQ); o += SEQ
        kkt = view(o, NQ, P); o += NQ * P
        atm = view(o, NQ, P); o += NQ * P
        ibT = view(o, 4, T)
        stt = view(o, NB, HG, DV)
        Ub = view(o, NCH, DV); o += NCH * DV
        Sb = view(o, NCH, DV); o += NCH * DV
        o += 32
        vbd = view(o, NQ, 4, DV); o += NQ * 4 * DV
        onb = view(o, NQ, P); o += NQ * P
        osb = view(o, NQ, DV); o += NQ * DV
        sqb = view(o, NQ, DV); o += NQ * DV
        dec = view(o, NCH); o += NCH
        hsm = view(o, 96); o += 96
        lbt = view(o, 6, HG); o += 6 * HG
        ngt = view(o, 1); o += 1
        dfk = view(o, 3, HG, NB); o += 3 * HG * NB
        qz = view(o, HG, NB, NB); o += HG * NB * NB
        units += [(wv, C_IB + P * i, P, ibT[:, i, :], ACT.Copy) for i in range(4)]
        units += [(wv, C_GB + P * i, P, gbs[:, i, :], ACT.Silu) for i in range(4)]
        for h in range(HG):
            units += [(wv, C_FB + P * h, P, fT[:, h % 2, :], ACT.Sigmoid), (wv, C_QB + P * h, P, qT[:, h % 2, :], ACT.Copy)]
        U_IB, U_H = NU_ATT, NU_ATT + 8
        small_in = sem("hgrn_small_loaded")
        vt_ps, vt_dve = sem("v_turned"), sem("v_tokens_copied")
        hf, hl, hs, he, hk = (sem("forget_ready"), sem("log_done"), sem("cumulated"), sem("decay_exp_done"), sem("keys_ready"))
        w_ps, w_act, w_dve = sem("hgrn_products"), sem("hgrn_copied_act"), sem("hgrn_copied_dve")
        vb_s, s_s, r_act, on_s = sem("v_diagonal_set"), sem("states_done"), sem("rms_done"), sem("normed_out")
        hd, lb_act, lb_s = sem("hgrn_dve_steps"), sem("lb_exp_done"), sem("rms_sum_done")
        st_in, hg_out = sem("states_loaded"), sem("states_stored")
        hgs_out = sem("decode_states_stored")
        zd = sem("diagonal_cleared")
        dg_ps, dg_dve, dg_act = sem("decode_v_spread"), sem("decode_state_steps"), sem("decode_rms_done")

        BY_ACT = (0, 1, 4, 5, 6, 7)

        def wstep(h, s):
            return 20 * (h // 2) + 9 * (h % 2) + s

        wsteps = [(h, s) for h in range(HG) for s in range(11 if h % 2 else 9)]
        for i, (h, s) in enumerate(wsteps):
            assert wstep(h, s) == i

        def copied(i):
            mine = wsteps[i][1] in BY_ACT
            return (w_act if mine else w_dve), sum((s in BY_ACT) == mine for _, s in wsteps[:i + 1])

        mT = view(4 * T, KD, T)
        o = 4 * T + KD * T
        wo = view(o, KD, D); o += KD * D
        o_x1 = o
        wba = view(o, 4, D); o += 4 * D
        wbb = view(o, 4, D); o += 4 * D
        sgb = view(o, 2, 2, 512); o += 2048
        x1 = view(o_x1, NQ + 1, D)
        o = max(o, o_x1 + (NQ + 1) * D)
        stats = view(o, 2, 6); o += 12
        mv = view(o, 2); o += 2
        rstd = view(o, 2); o += 2
        epsb = view(o, 1); o += 1
        assert o <= ARENA
        lng = view(0, 2, D)
        xr = view(2 * D, 2, D)
        uT = view(4 * T, 2, 4, T)
        wdn = view(4 * T + 8 * T, 2, 4, D)
        NG = F_FF // (4 * P)
        U_M = len(units)
        for i in range(KD):
            units += [(wv, C_MG + P * i, P, None, None), (wv, C_MG + D + P * i, P, None, None)]
        U_U = len(units)
        wupv = w_up[0].rearrange("(k p) c -> p k c", p=P)
        for i in range(F_FF // P):
            units += [(wupv, P * i, P, uT[:, (i // 4) % 2, i % 4, :], None)]
        NM = 3 * KD
        wb_in, wo_in, g_ps, m_act, m_dve2 = (sem("branch_weights_loaded"), sem("w_out_loaded"), sem("merge_products"),
                                             sem("merge_gates"), sem("merged"))
        me_s = sem("merge_dve_steps")
        ln_in, ln2_in = sem("ln1_loaded"), sem("ln2_loaded")
        xr_in = [sem(f"x_again{i}") for i in range(2)]
        f_ps, f_dve, ln_v, ln_r, ln_c = (sem("mix_ready"), sem("residual_done"), sem("variance_ready"), sem("rstd_ready"),
                                         sem("ln_steps"))
        x1_s, xt1_ps, xt1_act, x1_sc = sem("x1_ready"), sem("x1_turned"), sem("x1_copied"), sem("x1_scaled")
        sq_act, wd_in, dn_ps, dn_dve = sem("squared"), [sem(f"w_down{i}") for i in range(2)], sem("mlp_out"), sem("mlp_added")
        y_s, y_out = sem("y_ready"), sem("y_stored")

        def unit_done(n):
            if n < U_M:
                return u_ps, 3 * (n + 1)
            if n < U_U:
                i, ab = (n - U_M) // 2, (n - U_M) % 2
                return g_ps, 4 * (3 * i + 2) + ab + 1
            return u_ps, 3 * (n + 1 - (U_U - U_M))

        block = ctx.enter_context(nc.Block())

        @block.sync
        def _(sp):
            sp.dma_start(K[:, :], consts).then_inc(c_in, 16)
            for t in range(NQ + 1):
                if t >= 3:
                    sp.wait_ge(xt_ps, 2 * (t - 2))
                src = x_p[0, P * t:P * (t + 1), :] if t < NQ else x_s[:, 0, :]
                sp.dma_start(xs[0:toks(t), t % 3, :], src).then_inc(x_in[t % 3], 16)
                if t < WR:
                    v, c, m, _, _ = units[t]
                    sp.dma_start(wring[:, t, :, 0:m], v[:, :, c:c + m]).then_inc(w_in_s[t], 16)

            def load_unit(n):
                v, c, m, _, _ = units[n]
                sp.wait_ge(*unit_done(n - WR))
                sp.dma_start(wring[:, n % WR, :, 0:m], v[:, :, c:c + m]).then_inc(w_in_s[n % WR], 16)

            for n in range(WR, NU_ATT):
                load_unit(n)
            sp.wait_ge(xt_ps, 2 * (NQ + 1))
            for c in range(2):
                for part in range(2):
                    sp.dma_start(cw2[:, c, :, HD * part:HD * (part + 1)],
                                 cmp_w[0, c, STRIDE * part:STRIDE * (part + 1)].rearrange(
                                     "(q two) d e -> (two d) q e", two=2)).then_inc(cw_in, 16)
                    for half in range(2):
                        sp.dma_start(cw64[HD * half:HD * (half + 1), c, :, HD * part:HD * (part + 1)],
                                     cmp_w[0, c, STRIDE * part:STRIDE * (part + 1)].rearrange("l d e -> d l e")
                                     ).then_inc(cw_in, 16)
                for two in range(2):
                    sp.dma_start(cpos[HD * two:HD * (two + 1), c, :],
                                 cmp_pos[0, c].rearrange("(q two) d -> two d q", two=2)[two],
                                 allow_slow_non_contiguous=True).then_inc(cw_in, 16)
            sp.dma_start(kcA[64:65, :, :], kpos[:, SEQ:SEQ + 2 * NCMP_P].rearrange("a (g n) -> a g n", g=2)).then_inc(cw_in, 16)
            sp.wait_ge(kt_dve, 3 * (NQ + 1))
            for i, (dst, dst_s) in enumerate(((cmp_p, cmp_s), (sel_p, sel_s))):
                sp.dma_start(dst[0, 0].rearrange("(t p) c g d -> p t (c g d)", p=P),
                             kvtok[:, 0:NQ, 256 * i:256 * (i + 1)]).then_inc(kv_out, 16)
                sp.dma_start(dst_s[0, :, 0].rearrange("b c g d -> b (c g d)"),
                             kvd[:, 256 * i:256 * (i + 1)]).then_inc(kv_out, 16)
            sp.dma_start(win_p[0, 0].rearrange("(t p) c g d -> p t (c g d)", p=P),
                         kvtok[:, NQ - WINDOW // P:NQ, 512:768]).then_inc(kv_out, 16)
            sp.dma_start(win_s[0, :, WINDOW - 1].rearrange("b c g d -> b (c g d)"),
                         kvd[:, 512:768]).then_inc(kv_out, 16)
            sp.dma_start(win_s[0, :, 0:WINDOW - 1].rearrange("b l c g d -> b (l c g d)"),
                         c_win[0, :, 1:WINDOW].rearrange("b l c g d -> b (l c g d)")).then_inc(shift_out, 16)
            sp.wait_ge(cp_ps, 2)
            sp.wait_ge(cp_dve, 3)
            for br in range(2):
                for g in range(2):
                    sp.dma_start(kA[64:65, br, g, :], kpos[:, 0:SEQ]).then_inc(ka_s, 16)
            sp.wait_ge(kv_out, 6 * 16)

            for n in range(NU_ATT, NU_ATT + WR):
                load_unit(n)
            sp.wait_ge(ph, 3)
            sp.dma_start(tabi, table.rearrange("b j -> j b"), allow_slow_non_contiguous=True).then_inc(tb_in, 16)
            sp.dma_start(cmpbias, dbias[:, NSEL + NWIN:]).then_inc(tb_in, 16)
            sp.wait_ge(rank_s, 1)
            sp.dma_start(Prow[:, 0:NSEL + NWIN], dbias[:, 0:NSEL + NWIN]).then_inc(bias_in, 16)
            for b in range(NB):
                n = 32 + b
                if b < 2:
                    sp.wait_ge(v_s, 15 + b)
                    sp.wait_ge(d_ps, 2 * 16 * 2 + 2 * (15 + b))
                else:
                    sp.wait_ge(d_ps, 96 + b - 1)
                sp.dma_start(raw[:, b % 2, 0:1024].rearrange("p (l c) -> p l c", l=4),
                             c_win[0, b].rearrange("(p l) c g d -> p l (c g d)", l=4)).then_inc(wraw_in[b % 2], 16)
            sp.wait_ge(d_ps, 96 + NB)
            for b in range(NB):
                sp.dma_start(raww[:, b, :, :],
                             c_win[0, b].rearrange("(p l) c g d -> p l c (g d)", l=4)[:, :, 1, :]).then_inc(wv_in, 16)
            sp.wait_ge(ph, 6)
            for i in range(2):
                sp.dma_start(lbt[:, i, :], lb_logits[i].rearrange("(h p) -> p h", p=P),
                             allow_slow_non_contiguous=True).then_inc(small_in, 16)
            for i in range(2):
                sp.dma_start(ngt[DV * i:DV * (i + 1), :], norm_g.rearrange("a v -> v a"),
                             allow_slow_non_contiguous=True).then_inc(small_in, 16)
            for n in range(NU_ATT + WR, U_H + 2 * HG):
                load_unit(n)
            sp.wait_ge(w_ps, wstep(HG - 1, 8) + 1)
            sp.wait_ge(hg_out, 16 * HG)
            sp.dma_start(stt, state[0].rearrange("b h k v -> k b h v")).then_inc(st_in, 16)
            sp.wait_ge(dg_dve, 3 * NB)
            sp.dma_start(hg_s[0].rearrange("b h k v -> k b h v"), stt).then_inc(hgs_out, 16)
            sp.wait_ge(hgs_out, 16)
            sp.wait_ge(shift_out, 16)
            for n in range(U_M, U_M + WR):
                load_unit(n)
            sp.wait_ge(ph, 9)
            for src, dst in ((w_br_a, wba), (w_br_b, wbb)):
                sp.dma_start(dst, src[0].rearrange("(k p) c -> p k c", p=P)).then_inc(wb_in, 16)
            sp.dma_start(wo, w_out[0].rearrange("(k p) c -> p k c", p=P)).then_inc(wo_in, 16)
            for n in range(U_M + WR, U_U + WR):
                load_unit(n)
            sp.wait_ge(g_ps, 4 * NM)
            sp.dma_start(lng[:, 0, :], ln1_g.to_broadcast([P, D])).then_inc(ln_in, 16)
            sp.dma_start(lng[:, 1, :], ln1_b.to_broadcast([P, D])).then_inc(ln_in, 16)
            for t in range(NQ + 1):
                if t >= 2:
                    sp.wait_ge(f_dve, t - 1)
                src = x_p[0, P * t:P * (t + 1), :] if t < NQ else x_s[:, 0, :]
                sp.dma_start(xr[0:toks(t), t % 2, :], src).then_inc(xr_in[t % 2], 16)
            for g in range(NG):
                for n in range(U_U + 4 * (g + 1), U_U + 4 * (g + 2)):
                    if n < len(units):
                        load_unit(n)
                if g == 0:
                    sp.wait_ge(f_ps, NQ + 1)
                if g >= 2:
                    sp.wait_ge(dn_ps, 18 * (g - 1))
                sp.dma_start(wdn[:, g % 2, :, :], w_down[0, 4 * P * g:4 * P * (g + 1), :].rearrange("(j p) c -> p j c", p=P)
                             ).then_inc(wd_in[g % 2], 16)
                if g == 0:
                    sp.wait_ge(x1_s, NQ + 1)
                    sp.dma_start(lng[:, 0, :], ln2_g.to_broadcast([P, D])).then_inc(ln2_in, 16)
                    sp.dma_start(lng[:, 1, :], ln2_b.to_broadcast([P, D])).then_inc(ln2_in, 16)
            for t in range(NQ + 1):
                sp.wait_ge(y_s, t + 1)
                dst = y_p[0, P * t:P * (t + 1), :] if t < NQ else y_s_out[:, 0, :]
                sp.dma_start(dst, x1[0:toks(t), t, :]).then_inc(y_out, 16)
            sp.wait_ge(y_out, 16 * (NQ + 1))

        def unit_matmuls(pe, n):
            v, c, m, _, _ = units[n]
            pe.wait_ge(w_in_s[n % WR], 16 * (n // WR + 1))
            for ci, (c0, cn) in enumerate(CHUNKS):
                if ci < 2 and n >= 2:
                    pe.wait_ge(u_act, 3 * (n - 2) + ci + 1)
                if ci == 2 and n >= 1:
                    pe.wait_ge(u_act, 3 * n)
                for k in range(KD):
                    mm = pe.matmul(unit_out(n, ci, m), wring[:, n % WR, k, 0:m], xT[:, k, c0:c0 + cn],
                                   start=(k == 0), stop=(k == KD - 1))
                mm.then_inc(u_ps, 1)

        @block.tensor
        def _(pe):
            pe.wait_ge(c_in, 16)
            for t in range(NQ + 1):
                n = toks(t)
                pe.wait_ge(x_in[t % 3], 16 * (t // 3 + 1))
                for half, done in enumerate((xt_act, xt_dve)):
                    if t >= 1:
                        pe.wait_ge(done, t)
                    for j in range(4):
                        k = 4 * half + j
                        mm = pe.transpose(PS[:, half, P * j:P * j + n], xs[0:n, t % 3, P * k:P * (k + 1)],
                                          ident[0:n, 0:n])
                    mm.then_inc(xt_ps, 1)
            pe.wait_ge(xt_act, NQ + 1)
            pe.wait_ge(xt_dve, NQ + 1)
            for n in range(NU_ATT):
                unit_matmuls(pe, n)
            pe.wait_ge(u_act, 3 * NU_ATT)
            for t in range(NQ + 1):
                n = toks(t)
                if t >= 1:
                    pe.wait_ge(kt_dve, 3 * t)
                for j in range(6):
                    mm = pe.transpose(PS[0:n, 6 + j // 4, P * (j % 4):P * (j % 4 + 1)],
                                      hA[:, 4 + j, P * t:P * t + n], ident)
                    if j == 3:
                        mm.then_inc(kt_ps, 1)
                pe.transpose(PS[0:n, 7, 256:280], hG[0:24, P * t:P * t + n], ident[0:24, 0:24]).then_inc(kt_ps, 1)
            pe.wait_ge(cw_in, 16 * 17)
            for c in range(2):
                for g in range(2):
                    for l in range(STRIDE):
                        mm = pe.matmul(PS[:, 4 + g, c * NCMP_P:(c + 1) * NCMP_P],
                                       cw64[HD * g:HD * (g + 1), c, l, :],
                                       hA[HD * g:HD * (g + 1), 4 + c, l:SEQ:STRIDE],
                                       start=(l == 0), stop=(l == STRIDE - 1))
            for c in range(2):
                for half in range(2):
                    for q in range(16):
                        mm = pe.matmul(PS[HD * half:HD * (half + 1), 2, c:c + 1],
                                       cw2[:, c, q % 8, HD * (q // 8):HD * (q // 8 + 1)], cpos[:, c, q:q + 1],
                                       start=(q == 0), stop=(q == 15))
            mm.then_inc(cp_ps, 1)
            pe.wait_ge(cp_dve, 3)
            for g in range(2):
                mm = pe.transpose(PS[0:NCMP_P, 3, HD * g:HD * (g + 1)], cmpK[:, 2 + g, :], ident[0:HD, 0:HD])
            mm.then_inc(cp_ps, 1)

            def scores(j):
                h, i, wc = job(j)
                if j % 16 == 0:
                    pe.wait_ge(q_s, h + 1)
                    pe.wait_ge(q_row, h + 1)
                if j >= 2:
                    pe.wait_ge(e_act, exps(j - 2))
                q = qS[:, h % 2, P * i:P * (i + 1)]
                g = h // 4
                if not wc:
                    spans = [(0, g, k0, min(512, P * (i + 1) - k0), k0) for k0 in range(0, P * (i + 1), 512)]
                else:
                    lo, n = P * max(0, i - 4), P * min(i + 1, 5)
                    spans = [(1, g, lo + k0, min(512, n - k0), k0) for k0 in range(0, n, 512)]
                for br, g, k0, n, col in spans:
                    mm = pe.matmul(PS[:, 2 * wc + col // 512, col % 512:col % 512 + n], q, kA[:, br, g, k0:k0 + n],
                                   start=True, stop=True)
                if wc:
                    mm = pe.matmul(PS[:, 3, 128:128 + NCMP_P], q, kcA[:, g, :], start=True, stop=True)
                mm.then_inc(ss_ps, 1)

            def turn(j, gi):
                h, i, wc = job(j)
                if gi == 0:
                    pe.wait_ge(p_dve, j + 1)
                    if j >= 1:
                        pe.wait_ge(t_act, j)
                else:
                    if second_groups[j] >= 1:
                        pe.wait_ge(t_dve, second_groups[j])
                for b, (br, k0, n, col) in enumerate(groups(j)[gi]):
                    mm = pe.transpose(PS[0:n, 4 + gi, P * b:P * (b + 1)], pr[:, j % 2, col:col + n], ident)
                mm.then_inc(t_ps, 1)

            def pv(j, gi):
                h, i, wc = job(j)
                g = h // 4
                if gi == 0:
                    pe.wait_ge(t_act, j + 1)
                    if j % 2 == 0 and j >= 4:
                        pe.wait_ge(o_act, j // 2 - 1)
                else:
                    pe.wait_ge(t_dve, second_groups[j] + 1)
                last_g = gi == len(groups(j)) - 1
                for b, (br, k0, n, col) in enumerate(groups(j)[gi]):
                    if br == 2:
                        v = vcN[:, g, :]
                    else:
                        at = 384 + 256 * br + HD * g
                        v = kvtok[:, k0 // P, at:at + HD]
                    first = wc == 0 and gi == 0 and b == 0
                    last = wc == 1 and last_g and b == len(groups(j)[gi]) - 1
                    mm = pe.matmul(PS[HD * (h % 2):HD * (h % 2 + 1), 6 + i % 2, 0:P], v[0:n, :], PT[0:n, j % 2, gi, P * b:P * (b + 1)],
                                   start=first, stop=last)
                mm.then_inc(pv_ps, 1)

            pe.wait_ge(ka_s, 16 * 4 + 4)
            scores(0)
            scores(1)
            for j in range(NJ + 1):
                if j + 2 < NJ:
                    scores(j + 2)
                if j < NJ:
                    for gi in range(len(groups(j))):
                        turn(j, gi)
                if j >= 1:
                    for gi in range(len(groups(j - 1))):
                        pv(j - 1, gi)

            pe.drain().then_inc(ph, 1)
            pe.wait_ge(ph, 3)
            pe.wait_ge(dve_r, 1)
            pe.matmul(PS[:, 7, 0:NB], const("pagespread", PAGES), tabf, start=True, stop=True).then_inc(pe_r, 1)
            pe.matmul(PS[0:NROW, 6, 0:24], const("ownT", NB), gates[0:NB, NQ, :], start=True, stop=True).then_inc(pe_r, 1)

            def cmp_turn(n):
                pe.wait_ge(raw_in[n % 2], 16 * (n // 2 + 1))
                for a, (c, par, q) in enumerate((c, par, q) for c in range(2) for par in range(2) for q in range(4)):
                    if a % 4 == 0 and n >= 1:
                        pe.wait_ge((cx_act, cx_dve)[c], 4 * (n - 1) + 2 * (par + 1))
                    at = 256 * (2 * q + par) + P * c
                    mm = pe.transpose(PS[:, a // 4, P * (a % 4):P * (a % 4 + 1)], raw[:, n % 2, at:at + P], ident)
                    if a % 4 == 3:
                        mm.then_inc(d_ps, 1)

            def cmp_products(n):
                b, half = n // 2, n % 2
                pe.wait_ge(cx_act, 4 * (n + 1))
                pe.wait_ge(cx_dve, 4 * (n + 1))
                if half == 0 and b >= 2:
                    pe.wait_ge(vc_s, b - 1)
                for c in range(2):
                    for q in range(4):
                        mm = pe.matmul(PS[:, 4 + 2 * (b % 2) + c, 0:256], cw2[:, c, 4 * half + q, :],
                                       xt2[:, n % 2, 256 * (4 * c + q):256 * (4 * c + q + 1)],
                                       start=(half == 0 and q == 0), stop=(half == 1 and q == 3))
                mm.then_inc(dc_ps, 1)

            pe.wait_ge(dve_r, 3)
            for n in range(18):
                if n < 16:
                    cmp_turn(n)
                if 1 <= n < 17:
                    cmp_products(n - 1)
                if n >= 3 and n % 2:
                    b = (n - 3) // 2
                    pe.wait_ge(kv_d, b + 1)
                    pe.transpose(PS[:, 4 + 2 * (b % 2), 256:384], vct[:, b % 2, :], ident).then_inc(vc_ps, 1)
            pe.wait_ge(kv_d, NB)
            pe.wait_ge(dve_r, 4)
            for b in range(NB):
                mm = pe.matmul(PS[0:NROW, 0, 0:NCMP_S], qbd[:, b, :], kcd[:, b, :], start=(b == 0), stop=(b == NB - 1))
            mm.then_inc(pe_r, 1)
            pe.wait_ge(dve_r, 5)
            pe.matmul(PS[0:16, 1, 0:NCMP_S], const("gsum", NROW), P_cmp, start=True, stop=True).then_inc(pe_r, 1)
            pe.wait_ge(rank_s, 1)
            pe.matmul(PS[0:NROW, 6, 0:NBLK_S], const("gspread", 16), blkm[:, 3, :], start=True, stop=True).then_inc(pe_r, 1)
            pe.wait_ge(dve_r, 6)

            def sel_turn(n):
                m = n - 16
                pe.wait_ge(raw_in[n % 2], 16 * (n // 2 + 1))
                for a in range(8):
                    if a % 4 == 0:
                        if m >= 1:
                            pe.wait_ge((d_act, d_dve)[a // 4], m)
                    mm = pe.transpose(PS[:, 4 + a // 4, P * (a % 4):P * (a % 4 + 1)],
                                      raw[:, n % 2, 256 * a:256 * a + P], ident)
                    if a % 4 == 3:
                        mm.then_inc(d_ps, 1)

            def sel_scores(m):
                b, half = m // 2, m % 2
                for s in range(2):
                    pe.wait_ge((d_act, d_dve)[s], m + 1)
                    pe.matmul(PS[0:NROW, 2 * half + s, :], qbd[:, b, :], ktd[:, s, :], start=(b == 0),
                              stop=(b == NB - 1)).then_inc(sc_ps, 1)

            for n in range(16, 32):
                sel_turn(n)
                sel_scores(n - 16)
            for b in range(NB):
                pe.wait_ge(wraw_in[b % 2], 16 * (b // 2 + 1))
                done, bank = ((d_act, 4), (d_dve, 5))[b % 2]
                pe.wait_ge(done, 16 + b // 2)
                for a in range(4):
                    mm = pe.transpose(PS[:, bank, P * a:P * (a + 1)], raw[:, b % 2, 256 * a:256 * a + P], ident)
                mm.then_inc(d_ps, 1)
                pe.wait_ge(done, 16 + b // 2 + 1)
                pe.matmul(PS[0:NROW, 6, :], qbd[:, b, :], ktd[:, b % 2, :], start=(b == 0), stop=(b == NB - 1)
                          ).then_inc(sc_ps, 1)
            for s in range(2):
                for b in range(NB):
                    mm = pe.matmul(PS[0:NROW, 7, s:s + 1], qbd[:, b, :], knew[:, s, b:b + 1], start=(b == 0),
                                   stop=(b == NB - 1))
            mm.then_inc(sc_ps, 1)
            pe.wait_ge(dve_r, 10)
            for a in range(16):
                pe.transpose(PS[:, a // 8, NROW * (a % 8):NROW * (a % 8 + 1)], P_sel[:, P * a:P * (a + 1)],
                             ident[0:NROW, 0:NROW])
            for a in range(4):
                pe.transpose(PS[:, 2, NROW * a:NROW * (a + 1)], P_win[:, P * a:P * (a + 1)], ident[0:NROW, 0:NROW])
            pe.transpose(PS[:, 2, 4 * NROW:5 * NROW], P_cmp, ident[0:NROW, 0:NROW])
            for s in range(2):
                mm = pe.transpose(PS[0:NB, 3, NROW * s:NROW * (s + 1)], pnew[:, s, :], ident[0:NROW, 0:NROW])
            mm.then_inc(pe_r, 1)
            pe.wait_ge(dve_r, 12)
            pe.wait_ge(v_s, 16)
            pe.wait_ge(wv_in, 16 * NB)
            for s in range(2):
                pe.matmul(PS[:, 4, 0:NROW], kvd[:, 384 + 256 * s:512 + 256 * s], pnewT[:, s, :], start=(s == 0), stop=False,
                          skip_group_check=True)
            for b in range(NB):
                cols = slice(8 * b, 8 * b + 8)
                for a in range(16):
                    pe.matmul(PS[:, 4, cols], vall[:, b, a, :], ptdv[:, a, cols], start=False, stop=False,
                              skip_group_check=True)
                for a in range(4):
                    pe.matmul(PS[:, 4, cols], raww[:, b, a, :], ptdv[:, 16 + a, cols], start=False, stop=False,
                              skip_group_check=True)
                mm = pe.matmul(PS[:, 4, cols], vcd[:, b, :], ptdv[:, 20, cols], start=False, stop=(b == NB - 1),
                               skip_group_check=True)
            mm.then_inc(pe_r, 1)
            pe.drain().then_inc(ph, 1)
            pe.wait_ge(ph, 6)
            for n in range(U_IB, U_IB + 4):
                unit_matmuls(pe, n)
            unit_matmuls(pe, U_IB + 4)
            for t in range(NQ + 1):
                n = toks(t)
                if t >= 3:
                    pe.wait_ge(vt_dve, t - 2)
                pe.wait_ge(u_act, 3 * (U_IB + 4))
                for j in range(4):
                    mm = pe.transpose(PS[0:n, 5 + t % 3, P * j:P * (j + 1)], ibT[:, j, P * t:P * t + n], ident)
                mm.then_inc(vt_ps, 1)
            for n in range(U_IB + 5, U_H):
                unit_matmuls(pe, n)
            unit_matmuls(pe, U_H)
            unit_matmuls(pe, U_H + 1)
            pe.wait_ge(vt_dve, NQ + 1)

            def wbank(h, s):
                i = wstep(h, s)
                if i >= 3:
                    pe.wait_ge(*copied(i - 3))
                return 5 + i % 3

            def turn_out(h):
                pe.wait_ge(on_s, h + 1)
                for s in (9, 10):
                    bank = wbank(h, s)
                    for j in range(4):
                        mm = pe.transpose(PS[:, bank, P * j:P * (j + 1)], onb[:, 4 * (s - 9) + j, :], ident)
                    mm.then_inc(w_ps, 1)

            for h in range(HG):
                if h + 1 < HG:
                    unit_matmuls(pe, U_H + 2 * (h + 1))
                if h >= 1 and h % 2 == 0:
                    turn_out(h - 1)
                pe.wait_ge(hk, h + 1)
                for s in (0, 1):
                    bank = wbank(h, s)
                    for j in range(4):
                        t = 4 * s + j
                        mm = pe.transpose(PS[:, bank, P * j:P * (j + 1)], lcb[:, P * t:P * (t + 1)], ident)
                    mm.then_inc(w_ps, 1)
                for s in (2, 3):
                    bank = wbank(h, s)
                    for j in range(4):
                        t = 4 * (s - 2) + j
                        mm = pe.matmul(PS[:, bank, P * j:P * (j + 1)], kf[:, P * t:P * (t + 1)],
                                       qT[:, h % 2, P * t:P * (t + 1)], start=True, stop=True)
                    mm.then_inc(w_ps, 1)
                pe.wait_ge(vb_s, 4 * (h + 1))
                pe.wait_ge(*copied(wstep(h, 1)))
                for s in (4, 5, 6, 7):
                    bank = wbank(h, s)
                    for j in range(2):
                        t = 2 * (s - 4) + j
                        mm = pe.matmul(PS[:, bank, 256 * j:256 * (j + 1)], kkt[:, t, :],
                                       vbd[:, t, :, :].rearrange("p j v -> p (j v)"), start=True, stop=True)
                    mm.then_inc(w_ps, 1)
                if h + 1 < HG:
                    unit_matmuls(pe, U_H + 2 * (h + 1) + 1)
                pe.wait_ge(*copied(wstep(h, 3)))
                pe.wait_ge(s_s, NCH * (h + 1) - 1)
                bank = wbank(h, 8)
                for t in range(NQ):
                    out = PS[:, bank, DV * t:DV * (t + 1)]
                    pe.matmul(out, atm[:, t, :], vt[:, t, DV * h:DV * (h + 1)], start=True, stop=False,
                              skip_group_check=True)
                    for j in range(4):
                        c = 4 * t + j
                        if c:
                            mm = pe.matmul(out[CH * j:CH * (j + 1), :], qT[:, h % 2, CH * c:CH * (c + 1)], Sb[:, c - 1, :],
                                           start=False, stop=True, skip_group_check=True)
                mm.then_inc(w_ps, 1)
            turn_out(HG - 1)
            for b in range(NB):
                pe.wait_ge(*copied(len(wsteps) - 1))
                if b >= 3:
                    pe.wait_ge(dg_dve, 3 * (b - 2))
                pe.matmul(PS[:, 5 + b % 3, :], const("rowb", NB).rearrange("p (b n) -> p b n", b=NB)[:, b, :], vdec,
                          start=True, stop=True).then_inc(dg_ps, 1)
            pe.wait_ge(dg_dve, 3 * NB)
            for h in range(HG):
                for b in range(NB):
                    mm = pe.matmul(PS[0:NB, 5, DV * h:DV * (h + 1)], qz[:, h, b, :], stt[:, b, h, :], start=(b == 0),
                                   stop=(b == NB - 1))
            mm.then_inc(dg_ps, 1)
            pe.wait_ge(dg_dve, 3 * NB + 4)
            for j in range(4):
                mm = pe.transpose(PS[:, 6, NB * j:NB * (j + 1)], onb[0:NB, j, :], ident[0:NB, 0:NB])
            mm.then_inc(dg_ps, 1)
            pe.drain().then_inc(ph, 1)
            pe.wait_ge(ph, 9)
            for s in range(NM):
                i, ci = s // 3, s % 3
                c0, cn = CHUNKS[ci]
                if s >= 2:
                    pe.wait_ge(m_dve2, s - 1)
                if s == 0:
                    pe.wait_ge(u_act, 3 * U_M)
                for ab in range(2):
                    n = U_M + 2 * i + ab
                    pe.wait_ge(w_in_s[n % WR], 16 * (n // WR + 1))
                    for k in range(KD):
                        mm = pe.matmul(PS[:, 4 * (s % 2) + ab, 0:cn], wring[:, n % WR, k, :], xT[:, k, c0:c0 + cn],
                                       start=(k == 0), stop=(k == KD - 1))
                    mm.then_inc(g_ps, 1)
                pe.wait_ge(wb_in, 32)
                for ab, (w, a) in enumerate(((wba, aT), (wbb, rT))):
                    for k in range(4):
                        mm = pe.matmul(PS[:, 4 * (s % 2) + 2 + ab, 0:cn], w[:, k, P * i:P * (i + 1)], a[:, k, c0:c0 + cn],
                                       start=(k == 0), stop=(k == 3))
                    mm.then_inc(g_ps, 1)
            pe.wait_ge(m_dve2, NM)
            pe.wait_ge(wo_in, 16)

            def turn_x1(t):
                n = toks(t)
                pe.wait_ge(x1_s, t + 1)
                for half in range(2):
                    if t >= 2:
                        pe.wait_ge(xt1_act, 2 * (t - 2) + half + 1)
                    for j in range(4):
                        k = 4 * half + j
                        mm = pe.transpose(PS[:, 4 + 2 * (t % 2) + half, P * j:P * j + n], x1[0:n, t, P * k:P * (k + 1)],
                                          ident[0:n, 0:n])
                    mm.then_inc(xt1_ps, 1)

            for t in range(NQ + 1):
                n = toks(t)
                if t >= 2:
                    pe.wait_ge(f_dve, t - 1)
                for half in range(2):
                    for k in range(KD):
                        mm = pe.matmul(PS[0:n, 2 * (t % 2) + half, :], mT[:, k, P * t:P * t + n],
                                       wo[:, k, 512 * half:512 * (half + 1)], start=(k == 0), stop=(k == KD - 1))
                mm.then_inc(f_ps, 1)
                if t >= 1:
                    turn_x1(t - 1)
            turn_x1(NQ)
            pe.wait_ge(xt1_act, 2 * (NQ + 1))

            def up(i):
                n = U_U + i
                pe.wait_ge(w_in_s[n % WR], 16 * (n // WR + 1))
                for ci, (c0, cn) in enumerate(CHUNKS):
                    m = n - (U_U - U_M)
                    if i >= 2 or ci == 2 and i >= 1:
                        pe.wait_ge(u_act, 3 * (m - 2) + ci + 1 if ci < 2 else 3 * m)
                    for k in range(KD):
                        mm = pe.matmul(unit_out(n, ci, P), wring[:, n % WR, k, :], xT[:, k, c0:c0 + cn],
                                       start=(k == 0), stop=(k == KD - 1))
                    mm.then_inc(u_ps, 1)

            def down(g):
                pe.wait_ge(wd_in[g % 2], 16 * (g // 2 + 1))
                pe.wait_ge(sq_act, 12 * (g + 1))
                for t in range(NQ + 1):
                    n = toks(t)
                    for half in range(2):
                        d = 18 * g + 2 * t + half
                        if d >= 3:
                            pe.wait_ge(dn_dve, d - 2)
                        for j in range(4):
                            mm = pe.matmul(PS[0:n, 5 + d % 3, :], uT[:, g % 2, j, P * t:P * t + n],
                                           wdn[:, g % 2, j, 512 * half:512 * (half + 1)], start=(j == 0), stop=(j == 3))
                        mm.then_inc(dn_ps, 1)

            for g in range(NG):
                for i in range(4 * g, 4 * g + 4):
                    up(i)
                if g >= 1:
                    down(g - 1)
            down(NG - 1)

        @block.scalar
        def _(act):
            for t in range(NQ + 1):
                n = toks(t)
                act.wait_ge(xt_ps, 2 * t + 1)
                act.activation(xT[:, 0:4, P * t:P * t + n],
                               PS[:, 0, :].rearrange("p (j n) -> p j n", j=4)[:, :, 0:n], ACT.Copy).then_inc(xt_act, 1)
            def unit_copy(n):
                v, c, m, dst, fn = units[n]
                for ci, (c0, cn) in enumerate(CHUNKS):
                    act.wait_ge(u_ps, 3 * n + ci + 1)
                    act.activation(dst[0:m, c0:c0 + cn], unit_out(n, ci, m), fn).then_inc(u_act, 1)
            act.wait_ge(xt_ps, 2 * (NQ + 1))
            for n in range(NU_ATT):
                unit_copy(n)
            act.wait_ge(cp_ps, 1)
            act.wait_ge(kt_ps, 2 * (NQ + 1))
            act.activation(cmpT.rearrange("p (c g) n -> p g c n", c=2),
                           PS[HD:P, 4:6, 0:2 * NCMP_P].rearrange("p g (c n) -> p g c n", c=2), ACT.Copy
                           ).then_inc(cp_act, 1)

            def exp(j):
                h, i, wc = job(j)
                act.wait_ge(m_dve, j + 1)
                if j >= 2:
                    act.wait_ge(t_ps, first_group[j - 1])
                if not wc:
                    n = P * (i + 1)
                    act.activation(pr[:, 0, 0:n], PS[:, 0:2, :].rearrange("p a n -> p (a n)")[:, 0:n], ACT.Exp,
                                   bias=small[:, 16 * (j % 4):16 * (j % 4) + 1],
                                   accum_out=small[:, 16 * (j % 4) + 4:16 * (j % 4) + 5]).then_inc(e_act, 1)
                else:
                    for w, (c0, n) in enumerate(((0, P * min(i + 1, 5)), (640, NCMP_P))):
                        act.activation(pr[:, 1, c0:c0 + n], PS[:, 2:4, :].rearrange("p a n -> p (a n)")[:, c0:c0 + n],
                                       ACT.Exp, bias=small[:, 16 * (j % 4) + w:16 * (j % 4) + w + 1],
                                       accum_out=small[:, 16 * (j % 4) + 4 + w:16 * (j % 4) + 5 + w]).then_inc(e_act, 1)

            def stage_q(h):
                if h >= 2:
                    act.wait_ge(ss_ps, 16 * (h - 1))
                act.activation(qS[0:HD, h % 2, :], hA[HD * (h % 2):HD * (h % 2 + 1), h // 2, 0:SEQ], ACT.Copy,
                               scale=HD ** -0.5).then_inc(q_s, 1)

            def out(n):
                h, i = heads[n]
                act.wait_ge(pv_ps, first_group[2 * n + 2])
                act.activation(aT[HD * (h % 2):HD * (h % 2 + 1), h // 2, P * i:P * (i + 1)],
                               PS[HD * (h % 2):HD * (h % 2 + 1), 6 + i % 2, 0:P], ACT.Copy).then_inc(o_act, 1)

            act.wait_ge(kt_ps, 2 * (NQ + 1))
            act.wait_ge(cp_ps, 2)
            act.wait_ge(cp_dve, 5)
            stage_q(0)
            exp(0)
            exp(1)
            for j in range(NJ):
                act.wait_ge(t_ps, first_group[j] + 1)
                if j >= 2:
                    act.wait_ge(pv_ps, first_group[j - 1])
                ev = evacuations(groups(j)[0])
                for e, (r, c0, c1) in enumerate(ev):
                    ins = act.activation(PT[0:r, j % 2, 0, c0:c1], PS[0:r, 4, c0:c1], ACT.Copy)
                    if e == len(ev) - 1:
                        ins.then_inc(t_act, 1)
                if j + 2 < NJ:
                    exp(j + 2)
                if j % 2 == 0 and j >= 2:
                    out(j // 2 - 1)
                if j % 16 == 4 and j // 16 + 1 < 8:
                    stage_q(j // 16 + 1)
            out(len(heads) - 1)

            act.drain().then_inc(ph, 1)
            act.wait_ge(ph, 3)

            def part1(b):
                act.wait_ge(dc_ps, 2 * b + 2)
                if b >= 1:
                    act.wait_ge(kv_d, b)
                act.activation(tmp1, PS[HD:P, 4 + 2 * (b % 2):6 + 2 * (b % 2), 0:256].rearrange(
                    "p c (g n) -> p c g n", g=2), ACT.Copy).then_inc(kv_a, 1)

            for n in range(16):
                for s in range(2):
                    act.wait_ge(d_ps, 4 * n + s + 1)
                    if n >= 2:
                        act.wait_ge(dc_ps, n - 1)
                    for g in range(2):
                        act.activation(xt_of(n, 0, s, g), PS[HD * g:HD * (g + 1), s, :].rearrange("p (q n) -> p q n", q=4),
                                       ACT.Copy).then_inc(cx_act, 1)
                if n >= 2 and n % 2 == 0:
                    part1(n // 2 - 1)
            part1(NB - 1)
            act.wait_ge(dve_r, 4)
            ast = Steps(act, act_r)
            act.wait_ge(dst2, 4)
            ast(act.activation(P_cmp, P_cmp, ACT.Exp, bias=dsm[:, 0:1], accum_out=dsm[:, 3:4]))
            for m in range(16):
                act.wait_ge(d_ps, 64 + 2 * m + 1)
                if m >= 1:
                    act.wait_ge(sc_ps, 2 * m - 1)
                act.activation(ktd[:, 0, :], PS[:, 4, :], ACT.Copy).then_inc(d_act, 1)
            for b in range(0, NB, 2):
                act.wait_ge(d_ps, 96 + b + 1)
                act.wait_ge(sc_ps, 31 if b == 0 else 32 + b - 1)
                act.activation(ktd[:, 0, :], PS[:, 4, :], ACT.Copy).then_inc(d_act, 1)
            act.wait_ge(dve_r, 8)
            ast(act.activation(P_sel, P_sel, ACT.Exp, bias=dsm[:, 1:2], accum_out=dsm[:, 4:5]))
            ast(act.activation(P_win, P_win, ACT.Exp, bias=dsm[:, 2:3], accum_out=dsm[:, 5:6]))
            act.drain().then_inc(ph, 1)
            act.wait_ge(ph, 6)
            act.wait_ge(small_in, 64)
            act.wait_ge(hd, 3)
            act.activation(lbt[:, 3, :], lbt[:, 3, :], ACT.Exp).then_inc(lb_act, 1)
            act.activation(lbt[:, 4, :], lbt[:, 4, :], ACT.Exp).then_inc(lb_act, 1)
            for n in range(U_IB, U_H + 2):
                if n == U_H:
                    act.wait_ge(lb_act, 2)
                unit_copy(n)

            def step_copy(h, s):
                i = wstep(h, s)
                act.wait_ge(w_ps, i + 1)
                dst = kkt[:, 4 * s:4 * s + 4, :] if s < 2 else Ub[:, 8 * (s - 4):8 * (s - 3), :]
                if s == 0 and h >= 1:
                    act.wait_ge(w_ps, wstep(h - 1, 7) + 1)
                if s == 4:
                    act.wait_ge(vt_ps, NQ + 1)
                    if h >= 1:
                        act.wait_ge(s_s, NCH * h)
                act.activation(dst, PS[:, 5 + i % 3, :].rearrange("p (a n) -> p a n", n=dst.shape[2]), ACT.Copy
                               ).then_inc(w_act, 1)

            ra = Steps(act, r_act)

            def decay(h):
                act.wait_ge(hf, h + 1)
                if h >= 1:
                    act.wait_ge(hk, h)
                act.activation(lfb, fT[:, h % 2, 0:SEQ], ACT.Ln).then_inc(hl, 1)
                act.wait_ge(hs, h + 1)
                act.activation(lfb, lcb, ACT.Exp, scale=-1.0).then_inc(he, 1)
                act.wait_ge(he, 2 * h + 1)
                act.activation(lcb, lcb, ACT.Exp).then_inc(he, 1)

            decay(0)
            for h in range(HG):
                if h + 1 < HG:
                    if h >= 1:
                        act.wait_ge(hk, h)
                    unit_copy(U_H + 2 * (h + 1))
                for s in (0, 1, 4, 5, 6, 7):
                    step_copy(h, s)
                if h + 1 < HG:
                    if h >= 1:
                        act.wait_ge(w_ps, wstep(h - 1, 8) + 1)
                    unit_copy(U_H + 2 * (h + 1) + 1)
                    decay(h + 1)
                act.wait_ge(lb_s, h + 1)
                ra(act.activation(hsm[:, 8:16], hsm[:, 0:8], ACT.Ln, scale=1.0 / DV, bias=hsm[:, 95:96]))
                ra(act.activation(hsm[:, 16:24], hsm[:, 8:16], ACT.Exp, scale=-0.5))
            act.wait_ge(dg_dve, 3 * NB + 3)
            ra(act.activation(hsm[0:NB, 8:16], hsm[0:NB, 0:8], ACT.Ln, scale=1.0 / DV, bias=hsm[0:NB, 95:96]))
            ra(act.activation(hsm[0:NB, 16:24], hsm[0:NB, 8:16], ACT.Exp, scale=-0.5))
            act.drain().then_inc(ph, 1)
            act.wait_ge(ph, 9)
            for s in range(NM):
                cn = CHUNKS[s % 3][1]
                for ab in range(2):
                    act.wait_ge(g_ps, 4 * s + ab + 1)
                    if s >= 2:
                        act.wait_ge(m_dve2, s - 1)
                    act.activation(sgb[:, s % 2, ab, 0:cn], PS[:, 4 * (s % 2) + ab, 0:cn], ACT.Sigmoid).then_inc(m_act, 1)

            ra2 = Steps(act, ln_r)

            def rstd_of(t, lnum):
                n = toks(t)
                act.wait_ge(ln_v, (NQ + 1) * lnum + t + 1)
                ra2(act.activation(rstd[0:n, 0:1], mv[0:n, 1:2], ACT.Ln, bias=epsb[0:n, :]))
                ra2(act.activation(rstd[0:n, 1:2], rstd[0:n, 0:1], ACT.Exp, scale=-0.5))

            for t in range(NQ + 1):
                n = toks(t)
                rstd_of(t, 0)
                for half in range(2):
                    act.wait_ge(xt1_ps, 2 * t + half + 1)
                    act.activation(xT[:, 4 * half:4 * half + 4, P * t:P * t + n],
                                   PS[:, 4 + 2 * (t % 2) + half, :].rearrange("p (j n) -> p j n", j=4)[:, :, 0:n], ACT.Copy
                                   ).then_inc(xt1_act, 1)
            for i in range(F_FF // P):
                n = U_U + i
                dst = units[n][3]
                if i == 0:
                    act.wait_ge(f_ps, NQ + 1)
                if i >= 8:
                    act.wait_ge(dn_ps, 18 * (i // 4 - 1))
                for ci, (c0, cn) in enumerate(CHUNKS):
                    m = n - (U_U - U_M)
                    act.wait_ge(u_ps, 3 * m + ci + 1)
                    act.activation(dst[:, c0:c0 + cn], unit_out(n, ci, P), ACT.Relu).then_inc(u_act, 1)
                    act.wait_ge(u_act, 3 * m + ci + 1)
                    act.activation(dst[:, c0:c0 + cn], dst[:, c0:c0 + cn], ACT.Square).then_inc(sq_act, 1)
            for t in range(NQ + 1):
                rstd_of(t, 1)

        @block.vector
        def _(dve):
            for t in range(NQ + 1):
                n = toks(t)
                dve.wait_ge(xt_ps, 2 * t + 2)
                dve.tensor_copy(xT[:, 4:8, P * t:P * t + n],
                                PS[:, 1, :].rearrange("p (j n) -> p j n", j=4)[:, :, 0:n]).then_inc(xt_dve, 1)
            for t in range(NQ + 1):
                n = toks(t)
                dve.wait_ge(kt_ps, 2 * t + 1)
                kv = kvtok[:, t, :] if t < NQ else kvd
                dve.tensor_copy(kv[0:n, 0:512], PS[0:n, 6, :]).then_inc(kt_dve, 1)
                dve.wait_ge(kt_ps, 2 * t + 2)
                dve.tensor_copy(kv[0:n, 512:768], PS[0:n, 7, 0:256]).then_inc(kt_dve, 1)
                dve.tensor_copy(gates[0:n, t, :], PS[0:n, 7, 256:280]).then_inc(kt_dve, 1)
            cps = Steps(dve, cp_dve)
            dve.wait_ge(cp_act, 1)
            cps(dve.tensor_copy(cb[:, 0:2], PS[:, 2, 0:2]))
            cps(dve.memset(cmpK[:, :, :], 0.0))
            for c in range(2):
                s = slice(2 * c, 2 * c + 2)
                ins = dve.scalar_tensor_tensor(
                    out=cmpK[:, s, 0:NCMP_P - 1],
                    in0=PS[0:HD, 4:6, c * NCMP_P:(c + 1) * NCMP_P - 1],
                    scalar=cb[0:HD, c:c + 1], in1=cmpT[:, s, 1:NCMP_P], op0=ALU.add, op1=ALU.add)
                if c:
                    cps(ins)
            dve.wait_ge(cp_ps, 2)
            cps(dve.tensor_copy(vcN, PS[0:NCMP_P, 3, 0:P].rearrange("p (g e) -> p g e", g=2)))
            cps(dve.tensor_copy(kcA[0:HD, :, :], cmpK[:, 0:2, :]))
            dve.wait_ge(ka_s, 16 * 4)
            for br in range(2):
                for g in range(2):
                    dve.tensor_copy(kA[0:HD, br, g, :], hA[HD * g:HD * (g + 1), 6 + 2 * br, 0:SEQ]).then_inc(ka_s, 1)
            steps = Steps(dve, dch)

            def slope_row(h):
                if h >= 2:
                    dve.wait_ge(ss_ps, 16 * (h - 1))
                dve.memset(qS[64:65, h % 2, :], 2.0 ** -(h + 1)).then_inc(q_row, 1)

            def maxima(j):
                h, i, wc = job(j)
                dve.wait_ge(ss_ps, j + 1)
                sc = PS[:, 2 * wc:2 * wc + 2, :].rearrange("p a n -> p (a n)")
                nm = small[:, 16 * (j % 4):16 * (j % 4) + 4]
                n = P * (i + 1) if not wc else P * min(i + 1, 5)
                own = sc[:, n - P:n]
                steps(dve.tensor_tensor(own, own, const("causal"), ALU.add))
                if wc and i >= 4:
                    steps(dve.tensor_tensor(sc[:, 0:P], sc[:, 0:P], const("winlow"), ALU.add))
                if wc:
                    cm = const("cmpmask").rearrange("p (t n) -> p t n", t=NQ)[:, i, :]
                    steps(dve.tensor_tensor(sc[:, 640:704], sc[:, 640:704], cm, ALU.add))
                    steps(dve.tensor_reduce(nm[:, 1:2], sc[:, 640:704], AX.X, ALU.max, negate=True))
                    if i == 0:
                        steps(dve.tensor_scalar(nm[:, 1:2], nm[:, 1:2], 1e29, None, ALU.min))
                dve.tensor_reduce(nm[:, 0:1], sc[:, 0:n], AX.X, ALU.max, negate=True).then_inc(m_dve, 1)

            def scale(j):
                h, i, wc = job(j)
                dve.wait_ge(e_act, exps(j))
                sm = small[:, 16 * (j % 4):16 * (j % 4) + 16]
                w = 2 if wc else 1
                if wc:
                    steps(dve.tensor_scalar(sm[:, 5:6], sm[:, 5:6], 1e-30, None, ALU.max))
                steps(dve.reciprocal(sm[:, 8:8 + w], sm[:, 4:4 + w]))
                gt = gates[:, i, :].rearrange("p (h c) -> p h c", c=3)[:, h, :]
                gt = gt[:, 1:2] if not wc else gt[:, 2:3]
                steps(dve.tensor_tensor(sm[:, 12:13], sm[:, 8:9], gt, ALU.mult))
                if wc:
                    steps(dve.tensor_tensor(sm[:, 13:14], sm[:, 9:10],
                                            gates[:, i, 3 * h:3 * h + 1], ALU.mult))
                    dve.tensor_scalar(pr[:, 1, 640:704], pr[:, 1, 640:704], sm[:, 13:14], None, ALU.mult)
                n = P * (i + 1) if not wc else P * min(i + 1, 5)
                dve.tensor_scalar(pr[:, wc, 0:n], pr[:, wc, 0:n], sm[:, 12:13], None, ALU.mult).then_inc(p_dve, 1)

            def second(j):
                if len(groups(j)) < 2:
                    return
                dve.wait_ge(t_ps, first_group[j] + 2)
                if j >= 2:
                    dve.wait_ge(pv_ps, first_group[j - 1])
                ev = evacuations(groups(j)[1])
                for e, (r, c0, c1) in enumerate(ev):
                    ins = dve.tensor_copy(PT[0:r, j % 2, 1, c0:c1], PS[0:r, 5, c0:c1])
                    if e == len(ev) - 1:
                        ins.then_inc(t_dve, 1)

            slope_row(0)
            maxima(0)
            maxima(1)
            scale(0)
            for j in range(NJ):
                if j + 2 < NJ:
                    maxima(j + 2)
                second(j)
                if j + 1 < NJ:
                    scale(j + 1)
                if j % 16 == 4 and j // 16 + 1 < 8:
                    slope_row(j // 16 + 1)
            ds = Steps(dve, dst2)
            ds(dve.memset(qbd[:, :, :], 0.0))
            qf = qbd.rearrange("p b r -> p (b r)")
            for g in range(2):
                for r in range(4):
                    h = 4 * g + r
                    dve.tensor_scalar(qf[HD * g:HD * (g + 1), h:h + 72 * (NB - 1) + 1:72],
                                      hA[HD * (h % 2):HD * (h % 2 + 1), h // 2, SEQ:T], HD ** -0.5, None, ALU.mult)
            dve.tensor_copy(knew[:, 0, :], hA[:, 6, SEQ:T])
            dve.tensor_copy(knew[:, 1, :], hA[:, 8, SEQ:T])
            dve.drain().then_inc(ph, 1)
            dve.wait_ge(ph, 3)
            rs = Steps(dve, dve_r)
            dve.wait_ge(tb_in, 32)
            rs(dve.tensor_copy(tabf, tabi))
            for half in range(2):
                dve.wait_ge(pe_r, 1)
                dve.tensor_scalar(idx[:, half, :], PS[:, 7, 0:NB], 16.0, const("half")[:, half:half + 1],
                                  ALU.mult, ALU.add).then_inc(ix_s, 1)
            dve.wait_ge(pe_r, 2)
            rs(dve.tensor_tensor(g64, PS[0:NROW, 6, 0:24],
                                 const("headsel", NROW).unsqueeze(2).to_broadcast([NROW, 8, 3]), ALU.mult))
            rs(dve.tensor_reduce(grow[:, 0:3], g64.rearrange("p (h c) -> p c h", c=3), AX.X, ALU.add))
            dve.memset(kcd[:, :, NCMP_S - 1:NCMP_S], 0.0)
            ds(dve.memset(vct[:, :, NCMP_S - 1:NCMP_S], 0.0))

            def blocks_of(b):
                dve.wait_ge(kv_a, b + 1)
                if b >= 2:
                    dve.wait_ge(vc_ps, b - 1)
                for c in range(2):
                    for g in range(2):
                        dst = kcd[:, b, :] if c == 0 else vct[:, b % 2, :]
                        ins = dve.scalar_tensor_tensor(
                            out=dst[HD * g:HD * (g + 1), 0:NCMP_S - 1],
                            in0=PS[0:HD, 4 + 2 * (b % 2) + c, NCMP_S * g:NCMP_S * (g + 1) - 1],
                            scalar=cb[0:HD, c:c + 1], in1=tmp1[:, c, g, 1:NCMP_S], op0=ALU.add, op1=ALU.add)
                ins.then_inc(kv_d, 1)

            def cmp_v(b):
                dve.wait_ge(vc_ps, b + 1)
                dve.tensor_copy(vcd[:, b, :], PS[:, 4 + 2 * (b % 2), 256:384]).then_inc(vc_s, 1)

            for n in range(18):
                if n < 16:
                    for s in range(2):
                        dve.wait_ge(d_ps, 4 * n + s + 3)
                        if n >= 2:
                            dve.wait_ge(dc_ps, n - 1)
                        for g in range(2):
                            dve.tensor_copy(xt_of(n, 1, s, g), PS[HD * g:HD * (g + 1), 2 + s, :].rearrange(
                                "p (q n) -> p q n", q=4)).then_inc(cx_dve, 1)
                if n >= 2 and n % 2 == 0:
                    blocks_of(n // 2 - 1)
                if n >= 3 and n % 2:
                    cmp_v((n - 3) // 2)
            rs(dve.memset(dsm[:, 31:32], 0.0))
            dve.wait_ge(pe_r, 3)
            dve.wait_ge(tb_in, 32)
            ds(dve.tensor_tensor(P_cmp, PS[0:NROW, 0, 0:NCMP_S], cmpbias, ALU.add))
            ds(dve.tensor_reduce(dsm[:, 0:1], P_cmp, AX.X, ALU.max, negate=True))
            dve.wait_ge(act_r, 1)
            ds(dve.tensor_scalar(dsm[:, 6:7], dsm[:, 3:4], 1e-30, None, ALU.max))
            ds(dve.reciprocal(dsm[:, 7:8], dsm[:, 6:7]))
            rs(dve.tensor_scalar(P_cmp, P_cmp, dsm[:, 7:8], None, ALU.mult))
            dve.wait_ge(pe_r, 4)
            ds(dve.memset(blkm[:, 0, :], 0.0))
            ds(dve.tensor_reduce(blkm[:, 0, 0:NBLK_S - 1], PS[0:16, 1, 0:NCMP_S].rearrange("p (b r) -> p b r", r=4),
                                 AX.X, ALU.add))
            ds(dve.tensor_tensor(blkm[:, 1, :], blkm[:, 0, :], const("free", 16), ALU.mult))
            ds(dve.tensor_tensor(blkm[:, 2, :], blkm[:, 1, :], const("forced", 16), ALU.add))
            other = blkm[:, 2, :].unsqueeze(1).to_broadcast([16, NBLK_S, NBLK_S])
            own_ = blkm[:, 2, :].unsqueeze(2).to_broadcast([16, NBLK_S, NBLK_S])
            ds(dve.tensor_tensor(rk1, other, own_, ALU.is_gt))
            ds(dve.tensor_tensor(rk2, other, own_, ALU.is_equal))
            ds(dve.tensor_tensor(rk2, rk2, const("below", 16).rearrange("p (a b) -> p a b", a=NBLK_S), ALU.mult))
            ds(dve.tensor_tensor(rk1, rk1, rk2, ALU.add))
            ds(dve.tensor_reduce(blkm[:, 1, :], rk1, AX.X, ALU.add))
            dve.tensor_scalar(blkm[:, 3, :], blkm[:, 1, :], N_SELECT - 0.5, NEG, ALU.is_gt, ALU.mult).then_inc(rank_s, 1)
            dve.wait_ge(pe_r, 5)
            rs(dve.tensor_copy(mb64, PS[0:NROW, 6, 0:NBLK_S - 1]))
            for m in range(16):
                dve.wait_ge(d_ps, 64 + 2 * m + 2)
                if m >= 1:
                    dve.wait_ge(sc_ps, 2 * m)
                dve.tensor_copy(ktd[:, 1, :], PS[:, 5, :]).then_inc(d_dve, 1)
            for b in range(1, NB, 2):
                dve.wait_ge(d_ps, 96 + b + 1)
                dve.wait_ge(sc_ps, 32 if b == 1 else 32 + b - 1)
                dve.tensor_copy(ktd[:, 1, :], PS[:, 5, :]).then_inc(d_dve, 1)
            dve.wait_ge(bias_in, 16)
            dve.wait_ge(sc_ps, 32 + NB + 1)
            ds(dve.tensor_tensor(P_sel[:, 0:PAST], P_sel[:, 0:PAST], PS[0:NROW, 0:4, :].rearrange("p a n -> p (a n)"), ALU.add))
            ps4 = P_sel[:, 0:PAST].rearrange("p (l k f) -> p l k f", l=STRIDE, f=4)
            ds(dve.tensor_tensor(ps4, ps4, mb64.unsqueeze(1).unsqueeze(3).to_broadcast([NROW, STRIDE, NBLK_S - 1, 4]), ALU.add))
            ds(dve.tensor_copy(P_sel[:, PAST:NSEL], PS[0:NROW, 7, 0:1]))
            rs(dve.tensor_reduce(dsm[:, 1:2], P_sel, AX.X, ALU.max, negate=True))
            ds(dve.tensor_tensor(P_win[:, 0:WINDOW], P_win[:, 0:WINDOW], PS[0:NROW, 6, :], ALU.add))
            ds(dve.tensor_copy(P_win[:, WINDOW:NWIN], PS[0:NROW, 7, 1:2]))
            rs(dve.tensor_reduce(dsm[:, 2:3], P_win, AX.X, ALU.max, negate=True))
            dve.wait_ge(act_r, 3)
            ds(dve.reciprocal(dsm[:, 8:10], dsm[:, 4:6]))
            ds(dve.tensor_tensor(dsm[:, 10:12], dsm[:, 8:10], grow[:, 1:3], ALU.mult))
            ds(dve.tensor_scalar(P_sel, P_sel, dsm[:, 10:11], None, ALU.mult))
            ds(dve.tensor_scalar(P_win, P_win, dsm[:, 11:12], None, ALU.mult))
            ds(dve.tensor_scalar(pnew[:, 0, :], const("own", NROW), P_sel[:, PAST:NSEL], None, ALU.mult))
            rs(dve.tensor_scalar(pnew[:, 1, :], const("own", NROW), P_win[:, WINDOW:NWIN], None, ALU.mult))
            rs(dve.tensor_scalar(P_cmp, P_cmp, grow[:, 0:1], None, ALU.mult))
            dve.wait_ge(pe_r, 6)
            rs(dve.tensor_copy(ptdv[:, :, :], PS[:, 0:3, :].rearrange("p a n -> p (a n)")[:, 0:21 * NROW].rearrange(
                "p (a n) -> p a n", a=21)))
            rs(dve.tensor_copy(pnewT, PS[0:NB, 3, 0:2 * NROW].rearrange("p (s n) -> p s n", s=2)))
            dve.wait_ge(pe_r, 7)
            acc = PS[:, 4, 0:NROW].rearrange("p (b r) -> p b r", b=NB)
            for g in range(2):
                for r in range(4):
                    h = 4 * g + r
                    ins = dve.tensor_copy(aT[HD * (h % 2):HD * (h % 2 + 1), h // 2, SEQ:T], acc[HD * g:HD * (g + 1), :, h])
            dve.drain().then_inc(ph, 1)
            dve.wait_ge(ph, 6)
            hv = Steps(dve, hd)
            dve.wait_ge(small_in, 64)
            hv(dve.tensor_tensor(lbt[:, 2, :], lbt[:, 0, :], lbt[:, 1, :], ALU.max))
            hv(dve.tensor_tensor(lbt[:, 3, :], lbt[:, 0, :], lbt[:, 2, :], ALU.subtract))
            hv(dve.tensor_tensor(lbt[:, 4, :], lbt[:, 1, :], lbt[:, 2, :], ALU.subtract))
            dve.wait_ge(lb_act, 2)
            hv(dve.tensor_tensor(lbt[:, 5, :], lbt[:, 3, :], lbt[:, 4, :], ALU.add))
            hv(dve.reciprocal(lbt[:, 2, :], lbt[:, 5, :]))
            hv(dve.tensor_tensor(lbt[:, 0, :], lbt[:, 3, :], lbt[:, 2, :], ALU.mult))
            hv(dve.tensor_scalar(lbt[:, 1, :], lbt[:, 0, :], -1.0, 1.0, ALU.mult, ALU.add))
            hv(dve.memset(atm, 0.0))
            hv(dve.memset(qz, 0.0))
            hv(dve.memset(hsm[:, 95:96], LN_EPS))
            for t in range(NQ + 1):
                n = toks(t)
                dve.wait_ge(vt_ps, t + 1)
                dve.tensor_copy(vt[:, t, :] if t < NQ else vdec, PS[0:n, 5 + t % 3, :]).then_inc(vt_dve, 1)
            maskb = const("hgmask").bitcast(U32)

            def turned_out(h):
                for s in (9, 10):
                    i = wstep(h, s)
                    dve.wait_ge(w_ps, i + 1)
                    c0 = 512 * (s - 9)
                    dve.scalar_tensor_tensor(out=rT[:, h // 2, c0:c0 + 512], in0=PS[:, 5 + i % 3, :], scalar=ngt[:, 0:1],
                                             in1=gbs[:, h // 2, c0:c0 + 512], op0=ALU.mult, op1=ALU.mult
                                             ).then_inc(w_dve, 1)

            def prepare(h):
                par = h % 2
                dve.wait_ge(u_act, 3 * (U_H + 2 * h + 1))
                dve.tensor_scalar(fT[:, par, :], fT[:, par, :], lbt[:, 1, h:h + 1], lbt[:, 0, h:h + 1], ALU.mult, ALU.add
                                  ).then_inc(hf, 1)
                dve.wait_ge(hf, h + 1)
                if h >= 1:
                    dve.wait_ge(w_ps, wstep(h - 1, 3) + 1)
                hv(dve.tensor_scalar(kf, fT[:, par, :], -1.0, 1.0, ALU.mult, ALU.add))
                hv(dve.tensor_copy(dfk[:, 0, h, :], fT[:, par, SEQ:T]))
                hv(dve.tensor_copy(dfk[:, 1, h, :], kf[:, SEQ:T]))
                dve.wait_ge(hl, h + 1)
                dve.tensor_tensor_scan(lcb, const("fresh"), lfb, 0.0, ALU.mult, ALU.add).then_inc(hs, 1)
                dve.wait_ge(he, 2 * h + 2)
                dve.wait_ge(u_act, 3 * (U_H + 2 * h + 2))
                hv(dve.tensor_copy(dfk[:, 2, h, :], qT[:, par, SEQ:T]))
                hv(dve.tensor_tensor(qT[:, par, 0:SEQ], qT[:, par, 0:SEQ], lcb, ALU.mult))
                hv(dve.tensor_copy(dec, lcb[:, CH - 1:SEQ:CH]))
                hv(dve.tensor_tensor(kf[:, 0:SEQ], kf[:, 0:SEQ], lfb, ALU.mult))
                dve.tensor_tensor(lcb.rearrange("p (c i) -> p c i", c=NCH), kf[:, 0:SEQ].rearrange("p (c i) -> p c i", c=NCH),
                                  dec.unsqueeze(2).to_broadcast([P, NCH, CH]), ALU.mult).then_inc(hk, 1)
                dve.wait_ge(hk, h + 1)

            prepare(0)
            for h in range(HG):
                if h >= 1 and h % 2 == 0:
                    turned_out(h - 1)
                for s in (2, 3):
                    i = wstep(h, s)
                    dve.wait_ge(w_ps, i + 1)
                    for j in range(4):
                        ins = dve.copy_predicated(atm[:, 4 * (s - 2) + j, :], maskb, PS[:, 5 + i % 3, P * j:P * (j + 1)])
                    ins.then_inc(w_dve, 1)
                for c in range(NCH):
                    if c % 8 == 0:
                        dve.wait_ge(*copied(wstep(h, 4 + c // 8)))
                        if h >= 1 and c == 0:
                            dve.wait_ge(hg_out, 16 * h)
                    if c == 0:
                        ins = dve.tensor_copy(Sb[:, 0, :], Ub[:, 0, :])
                    else:
                        ins = dve.scalar_tensor_tensor(out=Sb[:, c, :], in0=Sb[:, c - 1, :], scalar=dec[:, c:c + 1],
                                                       in1=Ub[:, c, :], op0=ALU.mult, op1=ALU.add)
                    ins.then_inc(s_s, 1)
                    dve.wait_ge(s_s, NCH * h + c + 1)
                if h + 1 < HG:
                    prepare(h + 1)
                i = wstep(h, 8)
                dve.wait_ge(w_ps, i + 1)
                dve.tensor_copy(osb, PS[:, 5 + i % 3, :].rearrange("p (t v) -> p t v", t=NQ)).then_inc(w_dve, 1)
                dve.wait_ge(*copied(i))
                hv(dve.tensor_tensor(sqb, osb, osb, ALU.mult))
                dve.tensor_reduce(hsm[:, 0:8], sqb, AX.X, ALU.add).then_inc(lb_s, 1)
                dve.wait_ge(r_act, 2 * (h + 1))
                if h % 2 == 0 and h >= 2:
                    dve.wait_ge(w_ps, wstep(h - 1, 10) + 1)
                dve.tensor_tensor(onb[:, :, DV * (h % 2):DV * (h % 2 + 1)], osb,
                                  hsm[:, 16:24].unsqueeze(2).to_broadcast([P, NQ, DV]), ALU.mult).then_inc(on_s, 1)
                dve.wait_ge(on_s, h + 1)
            turned_out(HG - 1)
            dv = Steps(dve, dg_dve)
            for h in range(HG):
                dve.tensor_copy(qz[:, h, :, :].rearrange("p a b -> p (a b)")[:, 0:NB * NB:NB + 1], dfk[:, 2, h, :])
            dve.wait_ge(st_in, 16)
            for b in range(NB):
                dve.wait_ge(dg_ps, b + 1)
                dv(dve.tensor_tensor(sqb, PS[:, 5 + b % 3, :].rearrange("p (h v) -> p h v", h=HG),
                                     dfk[:, 1, :, b:b + 1].to_broadcast([P, HG, DV]), ALU.mult))
                dv(dve.tensor_tensor(stt[:, b, :, :], stt[:, b, :, :],
                                     dfk[:, 0, :, b:b + 1].to_broadcast([P, HG, DV]), ALU.mult))
                dv(dve.tensor_tensor(stt[:, b, :, :], stt[:, b, :, :], sqb, ALU.add))
            dve.wait_ge(dg_ps, NB + 1)
            dv(dve.tensor_copy(osb[0:NB], PS[0:NB, 5, :].rearrange("p (t v) -> p t v", t=HG)))
            dv(dve.tensor_tensor(sqb[0:NB], osb[0:NB], osb[0:NB], ALU.mult))
            dv(dve.tensor_reduce(hsm[0:NB, 0:8], sqb[0:NB], AX.X, ALU.add))
            dve.wait_ge(r_act, 2 * HG + 2)
            dve.wait_ge(w_ps, len(wsteps))
            dv(dve.tensor_tensor(onb[0:NB, 0:4, :].rearrange("p a b -> p (a b)").rearrange("p (h v) -> p h v", h=HG), osb[0:NB],
                                 hsm[0:NB, 16:24].unsqueeze(2).to_broadcast([NB, HG, DV]), ALU.mult))
            dve.wait_ge(dg_ps, NB + 2)
            for j in range(4):
                dve.scalar_tensor_tensor(out=rT[:, j, SEQ:T], in0=PS[:, 6, NB * j:NB * (j + 1)], scalar=ngt[:, 0:1],
                                         in1=gbs[:, j, SEQ:T], op0=ALU.mult, op1=ALU.mult)
            dve.drain().then_inc(ph, 1)
            dve.wait_ge(ph, 9)
            ms = Steps(dve, me_s)
            ms(dve.memset(epsb, LN_EPS))
            for s in range(NM):
                i, ci = s // 3, s % 3
                c0, cn = CHUNKS[ci]
                dve.wait_ge(m_act, 2 * s + 2)
                dve.wait_ge(g_ps, 4 * s + 4)
                for ab in range(2):
                    ms(dve.tensor_tensor(sgb[:, s % 2, ab, 0:cn], sgb[:, s % 2, ab, 0:cn], PS[:, 4 * (s % 2) + 2 + ab, 0:cn],
                                         ALU.mult))
                dve.tensor_tensor(mT[:, i, c0:c0 + cn], sgb[:, s % 2, 0, 0:cn], sgb[:, s % 2, 1, 0:cn], ALU.add
                                  ).then_inc(m_dve2, 1)
            lc = Steps(dve, ln_c)

            def norm(t, lnum, done):
                n = toks(t)
                y = x1[0:n, t, :]
                lc(dve.bn_stats(stats[0:n, 0, :], y[:, 0:512]))
                lc(dve.bn_stats(stats[0:n, 1, :], y[:, 512:D]))
                dve.bn_aggr(mv[0:n, :], stats[0:n, :, :]).then_inc(ln_v, 1)
                k = (NQ + 1) * lnum + t + 1
                dve.wait_ge(ln_r, 2 * k)
                lc(dve.tensor_scalar(y, y, mv[0:n, 0:1], rstd[0:n, 1:2], ALU.subtract, ALU.mult))
                lc(dve.tensor_tensor(y, y, lng[0:n, 0, :], ALU.mult))
                dve.tensor_tensor(y, y, lng[0:n, 1, :], ALU.add).then_inc(done, 1)

            dve.wait_ge(ln_in, 32)
            for t in range(NQ + 1):
                n = toks(t)
                dve.wait_ge(f_ps, t + 1)
                dve.wait_ge(xr_in[t % 2], 16 * (t // 2 + 1))
                dve.scalar_tensor_tensor(out=x1[0:n, t, :], in0=xr[0:n, t % 2, :], scalar=ALPHA,
                                         in1=PS[0:n, 2 * (t % 2):2 * (t % 2) + 2, :].rearrange("p a n -> p (a n)"),
                                         op0=ALU.mult, op1=ALU.add).then_inc(f_dve, 1)
                dve.wait_ge(f_dve, t + 1)
                norm(t, 0, x1_s)
                if t >= 1:
                    m = toks(t - 1)
                    dve.wait_ge(xt1_ps, 2 * t)
                    dve.tensor_scalar(x1[0:m, t - 1, :], x1[0:m, t - 1, :], ALPHA, None, ALU.mult).then_inc(x1_sc, 1)
            dve.wait_ge(xt1_ps, 2 * (NQ + 1))
            dve.wait_ge(x1_s, NQ + 1)
            dve.tensor_scalar(x1[0:NB, NQ, :], x1[0:NB, NQ, :], ALPHA, None, ALU.mult).then_inc(x1_sc, 1)
            dve.wait_ge(x1_sc, NQ + 1)
            dve.wait_ge(ln2_in, 32)
            for g in range(NG):
                for t in range(NQ + 1):
                    n = toks(t)
                    for half in range(2):
                        d = 18 * g + 2 * t + half
                        dve.wait_ge(dn_ps, d + 1)
                        if g:
                            dve.wait_ge(dn_dve, d - 17)
                        y = x1[0:n, t, 512 * half:512 * (half + 1)]
                        dve.tensor_tensor(y, y, PS[0:n, 5 + d % 3, :], ALU.add).then_inc(dn_dve, 1)
                    if g == NG - 1:
                        dve.wait_ge(dn_dve, d + 1)
                        norm(t, 1, y_s)
                        dve.wait_ge(y_s, t + 1)

        @block.gpsimd
        def _(pool):
            pass
            pool.wait_ge(ix_s, 2)
            for n in range(32):
                src = (c_cmp if n < 16 else c_sel)[0].rearrange("n (r l) c g d -> (n r) (l c g d)", l=8)
                b, half = (n % 16) // 2, n % 2
                if n >= 2:
                    pool.wait_ge(d_ps, 4 * (n - 1) if n <= 17 else 64 + 2 * (n - 17))
                if n >= 18:
                    pool.wait_ge(v_s, n - 17)
                pool.indirect_dma_start(out=raw[:, n % 2, :], out_offset=None, in_=src,
                                        in_offset=bass.IndirectOffsetOnAxis(ap=idx[:, half, b:b + 1], axis=0)
                                        ).then_inc(raw_in[n % 2], 16)
                if n >= 17:
                    m = n - 17
                    pool.wait_ge(raw_in[(m + 16) % 2], 16 * ((m + 16) // 2 + 1))
                    if m == 0:
                        pool.wait_ge(vc_s, NB)
                    pool.tensor_copy(vall[:, m // 2, 8 * (m % 2):8 * (m % 2) + 8, :],
                                     raw[:, m % 2, :].rearrange("p (l c) -> p l c", l=8)[:, :, P:2 * P]).then_inc(v_s, 1)
            m = 15
            pool.wait_ge(raw_in[1], 16 * 16)
            pool.tensor_copy(vall[:, m // 2, 8 * (m % 2):8 * (m % 2) + 8, :],
                             raw[:, m % 2, :].rearrange("p (l c) -> p l c", l=8)[:, :, P:2 * P]).then_inc(v_s, 1)
            pool.wait_ge(ph, 6)
            pool.memset(vbd, 0.0).then_inc(zd, 1)
            pool.wait_ge(zd, 1)
            pool.wait_ge(vt_dve, NQ + 1)
            for h in range(HG + 1):
                if h < HG:
                    if h >= 1:
                        pool.wait_ge(w_ps, wstep(h - 1, 7) + 1)
                    for j in range(4):
                        pool.tensor_copy(vbd[CH * j:CH * (j + 1), :, j, :],
                                         vt[CH * j:CH * (j + 1), :, DV * h:DV * (h + 1)]).then_inc(vb_s, 1)
                if h >= 1:
                    pool.wait_ge(s_s, NCH * h)
                    pool.dma_start(hg_p[0, 0, h - 1], Sb[:, NCH - 1, :]).then_inc(hg_out, 16)


_INS = ['x_prompt', 'x_sample', 'cache_cmp_kv', 'cache_sel_kv', 'cache_win_kv', 'state_hgrn', 'page_table', 'w_in',
        'cmp_w', 'cmp_pos', 'hgrn_lb_logits', 'hgrn_norm_g', 'w_br_a', 'w_br_b', 'w_out', 'ln1_g', 'ln1_b', 'w_up',
        'w_down', 'ln2_g', 'ln2_b']
_KV = (2, GROUPS, HD)
_OUTS = [(1, SEQ, D), (NB, 1, D), (1, 1, SEQ) + _KV, (1, 1, SEQ) + _KV, (1, 1, WINDOW) + _KV, (1, 1, HG, P, DV),
         (1, NB, 1) + _KV, (1, NB, 1) + _KV, (1, NB, WINDOW) + _KV, (1, NB, HG, P, DV)]


def kernel(**inputs):
    import concourse.bacc as _bacc
    from concourse.bass_utils import run_bass_kernel_spmd as _run

    nc = _bacc.Bacc("TRN2", target_bir_lowering=False, num_devices=1)
    arrays, args = {}, []
    given = {name: np.ascontiguousarray(inputs[name]) for name in _INS}
    given["consts"], given["kpos"], given["dbias"] = constants(), positions(), decode_biases()
    for name, a in given.items():
        arrays[f"in_{name}"] = a
        args.append(nc.dram_tensor(f"in_{name}", a.shape, mybir.dt.from_np(a.dtype), kind="ExternalInput").ap())
    for i, shape in enumerate(_OUTS):
        args.append(nc.dram_tensor(f"out_{i}", shape, F32, kind="ExternalOutput").ap())
    hybrid_step(nc, *args)
    r = _run(nc, [arrays], core_ids=[0])
    return tuple(r.results[0][f"out_{i}"] for i in range(len(_OUTS)))
```

```python
from contextlib import ExitStack

import numpy as np

import concourse.bass as bass
from concourse import mybir

F32 = mybir.dt.float32
F32R = mybir.dt.float32r
I32 = mybir.dt.int32
U32 = mybir.dt.uint32
ALU = mybir.AluOpType
ACT = mybir.ActivationFunctionType
AX = mybir.AxisListType

P = 128
D = 1024
KD = D // P
SEQ = 1024
NQ = SEQ // P
NB = 8
T = SEQ + NB
HD = 64
GROUPS = 2
PAGES = 16
PAST = 2048
STRIDE = 16
NCMP_P = SEQ // STRIDE
NCMP_S = PAST // STRIDE
CMP_LEN = 32
WINDOW = 512
SEL_BLOCK = 64
N_SELECT = 16
NBLK_S = PAST // SEL_BLOCK + 1
HG = 8
DV = 64
CH = 32
NCH = SEQ // CH
F_FF = 4096
NEG = -1e30
FORCE = 1e6
LN_EPS = 1e-5
ALPHA = 2.0 ** 0.25
NROW = NB * 8

C_QA, C_KV, C_GLA, C_QB = 0, 512, 1280, 1304
C_FB, C_IB, C_GB, C_MG = C_QB + 1024, C_QB + 2048, C_QB + 2560, C_QB + 3072

CONSTS = {}


def constants():
    parts = {}

    def put(name, a):
        full = np.zeros((P, int(np.prod(a.shape[1:]))), np.float32)
        full[:a.shape[0]] = a.reshape(a.shape[0], -1)
        parts[name] = full

    p = np.arange(P)
    put("ident", np.eye(P))
    put("causal", np.where(p[None, :] <= p[:, None], 0.0, NEG))
    put("winlow", np.where(p[None, :] > p[:, None], 0.0, NEG))
    n = np.arange(NCMP_P)
    end = STRIDE * n + CMP_LEN - 1
    pos = P * np.arange(NQ)[None, :, None] + p[:, None, None]
    put("cmpmask", np.where((n < NCMP_P - 1) & (end <= pos), 0.0, NEG))
    put("hgmask", ((p[:, None] // CH == p[None, :] // CH) & (p[:, None] <= p[None, :])).astype(np.float32))
    put("fresh", np.broadcast_to((np.arange(SEQ) % CH != 0).astype(np.float32), (P, SEQ)))
    row = np.arange(NROW)
    put("gsum", (row[:, None] // 4 == np.arange(16)[None, :]).astype(np.float32))
    put("gspread", (row[None, :] // 4 == np.arange(16)[:, None]).astype(np.float32))
    b = np.arange(NBLK_S)
    put("below", np.broadcast_to((b[None, None, :] < b[None, :, None]), (16, NBLK_S, NBLK_S)).astype(np.float32))
    forced = (b == 0) | (b == NBLK_S - 1) | (b == NBLK_S - 2)
    put("free", np.broadcast_to(np.where(forced, 0.0, 1.0), (16, NBLK_S)))
    put("forced", np.broadcast_to(np.where(forced, FORCE, 0.0), (16, NBLK_S)))
    put("ownT", (row[None, :] // 8 == np.arange(NB)[:, None]).astype(np.float32))
    put("headsel", (row[:, None] % 8 == np.arange(8)[None, :]).astype(np.float32))
    put("pagespread", (p[None, :] // 8 == np.arange(PAGES)[:, None]).astype(np.float32))
    put("own", (row[:, None] // 8 == np.arange(NB)[None, :]).astype(np.float32))
    put("rowb", np.repeat(np.eye(NB)[:, :, None], P, axis=2))
    put("half", np.stack([2.0 * (p % 8), 2.0 * (p % 8) + 1], axis=1))
    at, out = 0, []
    for name, a in parts.items():
        CONSTS[name] = (at, a.shape[1])
        at += a.shape[1]
        out.append(a)
    return np.concatenate(out, axis=1)


def positions():
    end = STRIDE * np.arange(NCMP_P) + CMP_LEN - 1
    return np.concatenate([np.arange(SEQ), end, end]).astype(np.float32)[None, :]


def decode_biases():
    slope = 2.0 ** -(np.arange(NROW) % 8 + 1.0)
    l, c = np.arange(STRIDE), np.arange(NCMP_S)
    sel = slope[:, None, None] * (STRIDE * c[None, None, :] + l[None, :, None] - PAST)
    wpos = PAST - WINDOW + 4 * np.arange(P)[None, None, :] + np.arange(4)[None, :, None]
    win = np.where(PAST - wpos < WINDOW, slope[:, None, None] * (wpos - PAST), NEG)
    cmp = np.where(c < NCMP_S - 1, slope[:, None] * (STRIDE * c + CMP_LEN - 1 - PAST), NEG)
    zero = np.zeros((NROW, 1))
    return np.concatenate([sel.reshape(NROW, -1), zero, win.reshape(NROW, -1), zero, cmp], axis=1).astype(np.float32)


class Steps:

    def __init__(self, eng, sem):
        self.eng, self.sem, self.n = eng, sem, 0

    def __call__(self, ins):
        ins.then_inc(self.sem, 1)
        self.n += 1
        self.eng.wait_ge(self.sem, self.n)


def hybrid_step(nc, x_p, x_s, c_cmp, c_sel, c_win, state, table, w_in, cmp_w, cmp_pos, lb_logits, norm_g,
                w_br_a, w_br_b, w_out, ln1_g, ln1_b, w_up, w_down, ln2_g, ln2_b, consts, kpos, dbias,
                y_p, y_s_out, cmp_p, sel_p, win_p, hg_p, cmp_s, sel_s, win_s, hg_s):
    with ExitStack() as ctx:
        def sb(name, shape, dt=F32):
            return ctx.enter_context(nc.sbuf_tensor(name, shape, dt))

        def sem(name):
            return ctx.enter_context(nc.semaphore(name))

        NC_ = consts.shape[1]
        K = sb("consts_sb", [P, NC_])

        def const(name, rows=P):
            at, n = CONSTS[name]
            return K[0:rows, at:at + n]

        ident = const("ident")
        xT_at = (nc.sbuf_base + 31) // 32 * 32
        xT = sb("xT", [P, KD, T])
        aT_at = (nc.sbuf_base + 31) // 32 * 32
        aT = sb("aT", [P, 4, T])
        WR = 4
        wring_at = (nc.sbuf_base + 31) // 32 * 32
        wring = sb("wring", [P, WR, KD, P])
        ARENA = 32200
        arena_at = (nc.sbuf_base + 31) // 32 * 32
        arena = sb("arena", [P, ARENA])
        PS = ctx.enter_context(nc.psum_tensor("PS", [P, 8, 512], F32))

        def rounded(name, base, at, *dims):
            assert base + 4 * (at + int(np.prod(dims))) <= arena_at + 4 * ARENA
            return nc.alloc_sbuf_tensor_at(name, [P, *dims], F32R, offset=base + 4 * at)

        def view(at, *dims, rows=P, base=0):
            n = int(np.prod(dims))
            assert at + n <= ARENA, (at, n)
            v = arena[base:base + rows, at:at + n]
            names = "abcd"[:len(dims)]
            if len(dims) > 1:
                v = v.rearrange(f"p ({' '.join(names)}) -> p {' '.join(names)}",
                                **{names[i]: dims[i] for i in range(1, len(dims))})
            return v

        o = 0
        gates = view(o, NQ + 1, 24); o += (NQ + 1) * 24
        cw2 = view(o, 2, 8, P); o += 2 * 8 * P
        cpos = view(o, 2, 16); o += 32
        cb = view(o, 2); o += 2
        small = view(o, 64); o += 64
        kvd = view(o, 768, rows=NB); o += 768
        qbd = view(o, NB, NROW); o += NB * NROW
        knew = view(o, 2, NB); o += 2 * NB
        o_kept = o = (o + 7) // 8 * 8
        hA = view(o, 10, T); o += 10 * T
        kvtok = view(o, NQ, 768); o += NQ * 768
        kcA = view(o, 2, NCMP_P, rows=65); o += 2 * NCMP_P
        vcN = view(o, 2, HD, rows=NCMP_P); o += 2 * HD
        kA = view(o, 2, 2, SEQ, rows=65); o += 4 * SEQ
        hG = view(o, T, rows=24)
        cmpT = view(o, 4, NCMP_P, rows=HD)
        cmpK = view(o + 256, 4, NCMP_P, rows=HD)
        PT = view(o, 2, 2, 512)
        o += 4 * 512
        qS = view(o, 2, SEQ, rows=65); o += 2 * SEQ
        pr = view(o, 2, SEQ); o += 2 * SEQ
        xs = view(o - 3 * SEQ, 3, D)
        cw64 = view(o - 4 * SEQ, 2, STRIDE, P)
        o_kvtok = o_kept + 10 * T
        xhA = rounded("x_high_att", arena_at, o_kvtok, KD, T)
        xl = rounded("x_low", xT_at, 0, KD, T)
        whA = rounded("w_high_att", arena_at, o_kvtok + KD * T, 2, KD, P)
        wl = rounded("w_low", wring_at, 0, WR, KD, P)

        ph = sem("phase_done")
        c_in = sem("consts_loaded")
        x_in = [sem(f"x_in{i}") for i in range(3)]
        xt_ps, xt_act, xt_dve = sem("xt_turned"), sem("xt_copied_act"), sem("xt_copied_dve")
        w_in_s = [sem(f"w_loaded{i}") for i in range(WR)]
        u_ps, u_act = sem("unit_chunk_ready"), sem("unit_chunk_copied")
        wh_act, wl_dve = sem("weight_high_parts"), sem("weight_low_parts")
        x_dve, x_pool = sem("x_whole_again_dve"), sem("x_whole_again_pool")
        kt_ps, kt_dve = sem("kv_turned"), sem("kv_copied")
        kv_out, shift_out = sem("kv_stored"), sem("window_shifted")
        cw_in = sem("cmp_weights_loaded")
        cp_ps, cp_act, cp_dve = sem("cmp_parts_ready"), sem("cmp_copied_act"), sem("cmp_steps_dve")
        ka_s = sem("k_staged")
        q_s, ss_ps, e_act, m_dve, p_dve, q_row = (sem("q_staged"), sem("scores_ready"), sem("exp_done"), sem("max_done"),
                                      sem("probs_scaled"), sem("slope_row_set"))
        dch = sem("dve_steps")
        t_ps, t_act, t_dve, pv_ps, o_act = (sem("probs_turned"), sem("probs_copied_act"), sem("probs_copied_dve"),
                                            sem("pv_groups_done"), sem("attn_out_copied"))

        def toks(t):
            return P if t < NQ else NB

        wv = w_in[0].rearrange("(k p) c -> p k c", p=P)
        wv = (wv[:, 0:4], wv[:, 4:8])
        units = [(wv, C_QA + P * i, P, hA[:, i, :], ACT.Copy) for i in range(10)]
        units += [(wv, C_GLA, 24, hG, ACT.Sigmoid)]
        NU_ATT = len(units)
        CHUNKS = [(T // 3 * i, T // 3) for i in range(3)]

        def unit_out(x, m, cn):
            return PS[0:m, x % 5, 0:cn]

        heads = [(h, i) for h in range(8) for i in range(NQ)]
        NJ = 2 * len(heads)

        def job(j):
            h, i = heads[j // 2]
            return h, i, j % 2

        def blocks(j):
            h, i, wc = job(j)
            if not wc:
                return [(0, P * b, P, P * b) for b in range(i + 1)]
            lo = max(0, i - 4)
            return [(1, P * b, P, P * (b - lo)) for b in range(lo, i + 1)] + [(2, 0, NCMP_P, 640)]

        def groups(j):
            bl = blocks(j)
            return [bl[:4]] + ([bl[4:]] if len(bl) > 4 else [])

        first_group = [0]
        second_groups = [0]
        for j in range(NJ):
            first_group.append(first_group[-1] + len(groups(j)))
            second_groups.append(second_groups[-1] + len(groups(j)) - 1)

        def evacuations(gr):
            full = sum(n == P for _, _, n, _ in gr)
            return [(P, 0, P * full)] * (full > 0) + [(NCMP_P, P * full, P * (full + 1))] * (full < len(gr))

        def exps(j):
            return 3 * (j // 2) + (1 if j % 2 == 0 else 3)

        NSEL, NWIN = PAST + 1, WINDOW + 1
        o = o_kept
        raw = view(o, 2, 8 * 256); o += 2 * 8 * 256
        raww = view(o - 4096, NB, 4, P)
        ktd = view(o, 2, 512); o += 1024
        Prow = view(o, NSEL + NWIN + NCMP_S, rows=NROW)
        rk1 = view(o, NBLK_S, NBLK_S, rows=16)
        rk2 = view(o + NBLK_S * NBLK_S, NBLK_S, NBLK_S, rows=16)
        o += NSEL + NWIN + NCMP_S
        P_sel, P_win, P_cmp = Prow[:, 0:NSEL], Prow[:, NSEL:NSEL + NWIN], Prow[:, NSEL + NWIN:]
        cmpbias = view(o, NCMP_S, rows=NROW); o += NCMP_S
        kcd = view(o, NB, NCMP_S); o += NB * NCMP_S
        vcd = view(o, NB, P); o += NB * P
        g64 = view(o, 24, rows=NROW); o += 24
        grow = view(o, 4, rows=NROW); o += 4
        idx = view(o, 2, NB).bitcast(U32); o += 16
        tabi = view(o, NB, rows=PAGES).bitcast(I32); o += NB
        tabf = view(o, NB, rows=PAGES); o += NB
        dsm = view(o, 32, rows=NROW); o += 32
        blkm = view(o, 4, NBLK_S, rows=16); o += 4 * NBLK_S
        mb64 = view(o, NBLK_S - 1, rows=NROW); o += NBLK_S - 1
        pnew = view(o, 2, NB, rows=NROW); o += 16
        pnewT = view(o, 2, NROW, rows=NB); o += 128
        xt2 = view(o, 2, 2048)
        tmp1 = view(o + 4096, 2, 2, NCMP_S, rows=HD)
        vct = view(o + 4608, 2, NCMP_S)
        vall = view(o, NB, STRIDE, P)
        o += NB * STRIDE * P
        ptdv = view(o, 21, NROW)
        tb_in, ix_s = sem("table_loaded"), sem("row_index_ready")
        raw_in = [sem(f"pages_loaded{i}") for i in range(2)]
        cx_act, cx_dve = sem("chunks_copied_act"), sem("chunks_copied_dve")

        def xt_of(n, c, par, g):
            return xt2[HD * par:HD * (par + 1), n % 2, 1024 * c:1024 * (c + 1)].rearrange(
                "p (q g n) -> p q g n", q=4, g=2)[:, :, g, :]

        d_ps, d_act, d_dve = sem("turned_pages"), sem("turned_copied_act"), sem("turned_copied_dve")
        dc_ps, kv_a, kv_d = sem("cmp_products"), sem("cmp_part1_copied"), sem("cmp_blocks_built")
        vc_ps, vc_s = sem("cmp_v_turned"), sem("cmp_v_copied")
        pe_r, act_r, dve_r, v_s = (sem("pe_results"), sem("act_results"), sem("dve_results"), sem("v_copied"))
        bias_in, rank_s, wv_in = sem("bias_loaded"), sem("rank_done"), sem("window_v_loaded")
        wraw_in = [sem(f"window_loaded{i}") for i in range(2)]
        sc_ps, dst2 = sem("decode_scores"), sem("decode_steps")
        o = 0
        rT = view(o, 4, T); o += 4 * T
        gbs = view(o, 4, T); o += 4 * T
        vt = view(o, NQ, 512); o += NQ * 512
        vdec = view(o, 512, rows=NB); o += 512
        fT = view(o, 2, T); o += 2 * T
        qT = view(o, 2, T); o += 2 * T
        kf = view(o, T); o += T
        lfb = view(o, SEQ); o += SEQ
        lcb = view(o, SEQ); o += SEQ
        kkt = view(o, NQ, P); o += NQ * P
        atm = view(o, NQ, P); o += NQ * P
        ibT = view(o, 4, T)
        stt = view(o, NB, HG, DV)
        Ub = view(o, NCH, DV); o += NCH * DV
        Sb = view(o, NCH, DV); o += NCH * DV
        o += 32
        vbd = view(o, NQ, 4, DV); o += NQ * 4 * DV
        onb = view(o, NQ, P); o += NQ * P
        osb = view(o, NQ, DV); o += NQ * DV
        sqb = view(o, NQ, DV); o += NQ * DV
        dec = view(o, NCH); o += NCH
        hsm = view(o, 96); o += 96
        lbt = view(o, 6, HG); o += 6 * HG
        ngt = view(o, 1); o += 1
        dfk = view(o, 3, HG, NB); o += 3 * HG * NB
        qz = view(o, HG, NB, NB); o += HG * NB * NB
        units += [(wv, C_IB + P * i, P, ibT[:, i, :], ACT.Copy) for i in range(4)]
        units += [(wv, C_GB + P * i, P, gbs[:, i, :], ACT.Silu) for i in range(4)]
        for h in range(HG):
            units += [(wv, C_FB + P * h, P, fT[:, h % 2, :], ACT.Sigmoid), (wv, C_QB + P * h, P, qT[:, h % 2, :], ACT.Copy)]
        U_IB, U_H = NU_ATT, NU_ATT + 8
        small_in = sem("hgrn_small_loaded")
        vt_ps, vt_dve = sem("v_turned"), sem("v_tokens_copied")
        hf, hl, hs, he, hk = (sem("forget_ready"), sem("log_done"), sem("cumulated"), sem("decay_exp_done"), sem("keys_ready"))
        w_ps, w_act, w_dve = sem("hgrn_products"), sem("hgrn_copied_act"), sem("hgrn_copied_dve")
        vb_s, s_s, r_act, on_s = sem("v_diagonal_set"), sem("states_done"), sem("rms_done"), sem("normed_out")
        hd, lb_act, lb_s = sem("hgrn_dve_steps"), sem("lb_exp_done"), sem("rms_sum_done")
        st_in, hg_out = sem("states_loaded"), sem("states_stored")
        hgs_out = sem("decode_states_stored")
        zd = sem("diagonal_cleared")
        dg_ps, dg_dve, dg_act = sem("decode_v_spread"), sem("decode_state_steps"), sem("decode_rms_done")

        BY_ACT = (0, 1, 4, 5, 6, 7)

        def wstep(h, s):
            return 20 * (h // 2) + 9 * (h % 2) + s

        wsteps = [(h, s) for h in range(HG) for s in range(11 if h % 2 else 9)]
        for i, (h, s) in enumerate(wsteps):
            assert wstep(h, s) == i

        def copied(i):
            mine = wsteps[i][1] in BY_ACT
            return (w_act if mine else w_dve), sum((s in BY_ACT) == mine for _, s in wsteps[:i + 1])

        xr = view(0, 2, D)
        mT = view(4 * T, KD, T)
        x1h = rounded("x1_high", arena_at, 4 * T, KD, T)
        o = 4 * T + KD * T
        whM = rounded("w_high_mlp", arena_at, o, 4, KD, P)
        wo = view(o, KD, D)
        wdn = view(o + 2 * KD * P, 2, 2, D)
        wdl = rounded("w_down_low", arena_at, o + 2 * KD * P, 2, 2, D)
        wdh = rounded("w_down_high", arena_at, o + 2 * KD * P + 4 * D, 2, D)
        o += KD * D
        xhM = rounded("x_high_merge", arena_at, o, KD, T)
        sgb = view(o + KD * T, 2, 2, 512)
        x1 = view(o, NQ + 1, D)
        o += (NQ + 1) * D
        lng = view(o, 2, D); o += 2 * D
        o = max(o, 12 * T + KD * D + KD * T + 4 * 512)
        stats = view(o, 2, 6); o += 12
        mv = view(o, 2); o += 2
        rstd = view(o, 2); o += 2
        epsb = view(o, 1); o += 1
        uT = [aT[:, :, :].rearrange("p (j s) t -> p j s t", s=2), view(0, 2, 2, T)]
        uR = [rounded("hidden0", aT_at, 0, 2, 2, T), rounded("hidden1", arena_at, 0, 2, 2, T)]
        NG = F_FF // (2 * P)
        U_M = len(units)
        wbr = tuple(w[0].rearrange("(k p) c -> p k c", p=P) for w in (w_br_a, w_br_b))
        for i in range(KD):
            units += [(wv, C_MG + P * i, P, None, None), (wv, C_MG + D + P * i, P, None, None),
                      (wbr, P * i, P, None, None)]
        U_U = len(units)
        wupv = w_up[0].rearrange("(k p) c -> p k c", p=P)
        wupv = (wupv[:, 0:4], wupv[:, 4:8])
        for i in range(F_FF // P):
            units += [(wupv, P * i, P, None, None)]
        NM = 3 * KD
        wo_in, g_ps, m_act, m_dve2 = [sem(f"w_out_loaded{i}") for i in range(2)], sem("merge_products"), sem("merge_gates"), sem("merged")
        xh_act, xl_dve = sem("x_high_parts"), sem("x_low_parts")
        me_s = sem("merge_dve_steps")
        ln_in, ln2_in = sem("ln1_loaded"), sem("ln2_loaded")
        xr_in = [sem(f"x_again{i}") for i in range(2)]
        f_ps, f_dve, ln_v, ln_r, ln_c = (sem("mix_ready"), sem("residual_done"), sem("variance_ready"), sem("rstd_ready"),
                                         sem("ln_steps"))
        x1_s, xt1_ps, xt1_act, x1_sc = sem("x1_ready"), sem("x1_turned"), sem("x1_copied"), sem("x1_scaled")
        x1l_dve = sem("x1_low_parts")
        wd_in, wdh_act, wdl_dve = [sem(f"w_down{i}") for i in range(2)], sem("w_down_high"), sem("w_down_low")
        relu_act, sq_dve, uh_act, ul_dve = sem("relu_done"), sem("squared"), sem("hidden_high"), sem("hidden_low")
        dn_ps, dn_dve = sem("mlp_out"), sem("mlp_added")
        y_s, y_out = sem("y_ready"), sem("y_stored")

        def unit_done(n):
            if n < U_M:
                return u_ps, 3 * (n + 1)
            if n < U_U:
                i, part = (n - U_M) // 3, (n - U_M) % 3
                return g_ps, 4 * (3 * i + 2) + (1, 2, 4)[part]
            return u_ps, 3 * (n + 1 - (U_U - U_M))

        SPLITS_M, SPLITS_U = NU_ATT, NU_ATT + 2 * KD

        block = ctx.enter_context(nc.Block())

        @block.sync
        def _(sp):
            def load_unit(n):
                v, c, m, _, _ = units[n]
                if n >= WR:
                    sp.wait_ge(*unit_done(n - WR))
                for half in range(2):
                    sp.dma_start(wring[:, n % WR, 4 * half:4 * half + 4, 0:m], v[half][:, :, c:c + m]
                                 ).then_inc(w_in_s[n % WR], 16)

            sp.dma_start(K[:, :], consts).then_inc(c_in, 16)
            for t in range(NQ + 1):
                if t >= 3:
                    sp.wait_ge(xt_ps, 2 * (t - 2))
                src = x_p[0, P * t:P * (t + 1), :] if t < NQ else x_s[:, 0, :]
                sp.dma_start(xs[0:toks(t), t % 3, :], src).then_inc(x_in[t % 3], 16)
                if t < WR:
                    load_unit(t)

            for n in range(WR, NU_ATT):
                load_unit(n)
            sp.wait_ge(xt_ps, 2 * (NQ + 1))
            for c in range(2):
                for part in range(2):
                    sp.dma_start(cw2[:, c, :, HD * part:HD * (part + 1)],
                                 cmp_w[0, c, STRIDE * part:STRIDE * (part + 1)].rearrange(
                                     "(q two) d e -> (two d) q e", two=2)).then_inc(cw_in, 16)
                    for half in range(2):
                        sp.dma_start(cw64[HD * half:HD * (half + 1), c, :, HD * part:HD * (part + 1)],
                                     cmp_w[0, c, STRIDE * part:STRIDE * (part + 1)].rearrange("l d e -> d l e")
                                     ).then_inc(cw_in, 16)
                for two in range(2):
                    sp.dma_start(cpos[HD * two:HD * (two + 1), c, :],
                                 cmp_pos[0, c].rearrange("(q two) d -> two d q", two=2)[two],
                                 allow_slow_non_contiguous=True).then_inc(cw_in, 16)
            sp.wait_ge(kt_dve, 3 * (NQ + 1))
            for i, (dst, dst_s) in enumerate(((cmp_p, cmp_s), (sel_p, sel_s))):
                sp.dma_start(dst[0, 0].rearrange("(t p) c g d -> p t (c g d)", p=P),
                             kvtok[:, 0:NQ, 256 * i:256 * (i + 1)]).then_inc(kv_out, 16)
                sp.dma_start(dst_s[0, :, 0].rearrange("b c g d -> b (c g d)"),
                             kvd[:, 256 * i:256 * (i + 1)]).then_inc(kv_out, 16)
            sp.dma_start(win_p[0, 0].rearrange("(t p) c g d -> p t (c g d)", p=P),
                         kvtok[:, NQ - WINDOW // P:NQ, 512:768]).then_inc(kv_out, 16)
            sp.dma_start(win_s[0, :, WINDOW - 1].rearrange("b c g d -> b (c g d)"),
                         kvd[:, 512:768]).then_inc(kv_out, 16)
            sp.dma_start(win_s[0, :, 0:WINDOW - 1].rearrange("b l c g d -> b (l c g d)"),
                         c_win[0, :, 1:WINDOW].rearrange("b l c g d -> b (l c g d)")).then_inc(shift_out, 16)
            sp.wait_ge(cp_ps, 2)
            sp.wait_ge(cp_dve, 3)
            sp.dma_start(kcA[64:65, :, :], kpos[:, SEQ:].rearrange("a (g n) -> a g n", g=2)).then_inc(ka_s, 16)
            for br in range(2):
                for g in range(2):
                    sp.dma_start(kA[64:65, br, g, :], kpos[:, 0:SEQ]).then_inc(ka_s, 16)
            sp.wait_ge(kv_out, 6 * 16)

            for n in range(NU_ATT, NU_ATT + WR):
                load_unit(n)
            sp.wait_ge(ph, 3)
            sp.dma_start(tabi, table.rearrange("b j -> j b"), allow_slow_non_contiguous=True).then_inc(tb_in, 16)
            sp.dma_start(cmpbias, dbias[:, NSEL + NWIN:]).then_inc(tb_in, 16)
            sp.wait_ge(rank_s, 1)
            sp.dma_start(Prow[:, 0:NSEL + NWIN], dbias[:, 0:NSEL + NWIN]).then_inc(bias_in, 16)
            for b in range(NB):
                n = 32 + b
                if b < 2:
                    sp.wait_ge(v_s, 15 + b)
                    sp.wait_ge(d_ps, 2 * 16 * 2 + 2 * (15 + b))
                else:
                    sp.wait_ge(d_ps, 96 + b - 1)
                sp.dma_start(raw[:, b % 2, 0:1024].rearrange("p (l c) -> p l c", l=4),
                             c_win[0, b].rearrange("(p l) c g d -> p l (c g d)", l=4)).then_inc(wraw_in[b % 2], 16)
            sp.wait_ge(d_ps, 96 + NB)
            for b in range(NB):
                sp.dma_start(raww[:, b, :, :],
                             c_win[0, b].rearrange("(p l) c g d -> p l c (g d)", l=4)[:, :, 1, :]).then_inc(wv_in, 16)
            sp.wait_ge(ph, 6)
            for i in range(2):
                sp.dma_start(lbt[:, i, :], lb_logits[i].rearrange("(h p) -> p h", p=P),
                             allow_slow_non_contiguous=True).then_inc(small_in, 16)
            for i in range(2):
                sp.dma_start(ngt[DV * i:DV * (i + 1), :], norm_g.rearrange("a v -> v a"),
                             allow_slow_non_contiguous=True).then_inc(small_in, 16)
            for n in range(NU_ATT + WR, U_H + 2 * HG):
                load_unit(n)
            sp.wait_ge(w_ps, wstep(HG - 1, 8) + 1)
            sp.wait_ge(hg_out, 16 * HG)
            sp.dma_start(stt, state[0].rearrange("b h k v -> k b h v")).then_inc(st_in, 16)
            sp.wait_ge(dg_dve, 3 * NB)
            sp.dma_start(hg_s[0].rearrange("b h k v -> k b h v"), stt).then_inc(hgs_out, 16)
            sp.wait_ge(hgs_out, 16)
            sp.wait_ge(shift_out, 16)
            for n in range(U_M, U_M + WR):
                load_unit(n)
            sp.wait_ge(ph, 9)
            wov = w_out[0].rearrange("(k p) c -> p k c", p=P)
            sp.dma_start(wo[:, 4:8], wov[:, 4:8]).then_inc(wo_in[1], 16)
            for n in range(U_M + WR, U_U):
                load_unit(n)
            sp.wait_ge(g_ps, 4 * (NM - 1) + 2)
            sp.dma_start(wo[:, 0:4], wov[:, 0:4]).then_inc(wo_in[0], 16)
            for n in range(U_U, U_U + WR):
                load_unit(n)
            sp.wait_ge(m_dve2, NM)
            sp.dma_start(lng[:, 0, :], ln1_g.to_broadcast([P, D])).then_inc(ln_in, 16)
            sp.dma_start(lng[:, 1, :], ln1_b.to_broadcast([P, D])).then_inc(ln_in, 16)
            for t in range(NQ + 1):
                if t >= 2:
                    sp.wait_ge(f_dve, t - 1)
                src = x_p[0, P * t:P * (t + 1), :] if t < NQ else x_s[:, 0, :]
                sp.dma_start(xr[0:toks(t), t % 2, :], src).then_inc(xr_in[t % 2], 16)
            for g in range(NG):
                if g == 0:
                    sp.wait_ge(f_ps, NQ + 1)
                if g >= 2:
                    sp.wait_ge(dn_ps, 18 * (g - 1))
                sp.dma_start(wdn[:, g % 2], w_down[0, 2 * P * g:2 * P * (g + 1), :].rearrange("(j p) c -> p j c", p=P)
                             ).then_inc(wd_in[g % 2], 16)
                if g == 0:
                    sp.wait_ge(x1_s, NQ + 1)
                    sp.dma_start(lng[:, 0, :], ln2_g.to_broadcast([P, D])).then_inc(ln2_in, 16)
                    sp.dma_start(lng[:, 1, :], ln2_b.to_broadcast([P, D])).then_inc(ln2_in, 16)
                for n in range(U_U + WR + 2 * g, U_U + WR + 2 * (g + 1)):
                    if n < len(units):
                        load_unit(n)
            for t in range(NQ + 1):
                sp.wait_ge(y_s, t + 1)
                dst = y_p[0, P * t:P * (t + 1), :] if t < NQ else y_s_out[:, 0, :]
                sp.dma_start(dst, x1[0:toks(t), t, :]).then_inc(y_out, 16)
            sp.wait_ge(y_out, 16 * (NQ + 1))

        def split_product(pe, out, wh, wlow, xh, xlow):
            tiles = len(wh)
            for k in range(tiles):
                for i, (w, x) in enumerate(((wh[k], xh[k]), (wh[k], xlow[k]), (wlow[k], xh[k]))):
                    mm = pe.matmul(out, w, x, start=(k == 0 and i == 0), stop=(k == tiles - 1 and i == 2))
            return mm

        def split_high(act, n, dst):
            m = units[n][2]
            act.wait_ge(w_in_s[n % WR], 32 * (n // WR + 1))
            act.activation(dst[:, :, 0:m], wring[:, n % WR, :, 0:m], ACT.Copy).then_inc(wh_act, 1)

        def split_low(dve, n, q, high):
            m = units[n][2]
            dve.wait_ge(wh_act, q + 1)
            dve.tensor_tensor(wl[:, n % WR, :, 0:m], wring[:, n % WR, :, 0:m], high[:, :, 0:m].bitcast(F32), ALU.subtract
                              ).then_inc(wl_dve, 1)

        def unit_matmuls(pe, n):
            v, c, m, _, _ = units[n]
            pe.wait_ge(w_in_s[n % WR], 32 * (n // WR + 1))
            for ci, (c0, cn) in enumerate(CHUNKS):
                x = 3 * n + ci
                if x >= 5:
                    pe.wait_ge(u_act, x - 4)
                if n < NU_ATT:
                    mm = split_product(pe, unit_out(x, m, cn), [whA[:, n % 2, k, 0:m] for k in range(KD)],
                                       [wl[:, n % WR, k, 0:m] for k in range(KD)],
                                       [xhA[:, k, c0:c0 + cn] for k in range(KD)],
                                       [xl[:, k, c0:c0 + cn] for k in range(KD)])
                else:
                    for k in range(KD):
                        mm = pe.matmul(unit_out(x, m, cn), wring[:, n % WR, k, 0:m], xT[:, k, c0:c0 + cn],
                                       start=(k == 0), stop=(k == KD - 1))
                mm.then_inc(u_ps, 1)

        @block.tensor
        def _(pe):
            pe.wait_ge(c_in, 16)
            for t in range(NQ + 1):
                n = toks(t)
                pe.wait_ge(x_in[t % 3], 16 * (t // 3 + 1))
                for half in range(2):
                    if t >= 2:
                        pe.wait_ge(xt_dve, 2 * (t - 2) + half + 1)
                    for j in range(4):
                        k = 4 * half + j
                        mm = pe.transpose(PS[:, 2 * (t % 2) + half, P * j:P * j + n], xs[0:n, t % 3, P * k:P * (k + 1)],
                                          ident[0:n, 0:n])
                    mm.then_inc(xt_ps, 1)
            pe.wait_ge(xt_dve, 2 * (NQ + 1))
            for n in range(NU_ATT):
                pe.wait_ge(wl_dve, n + 1)
                unit_matmuls(pe, n)
            pe.wait_ge(u_act, 3 * NU_ATT)
            for t in range(NQ + 1):
                n = toks(t)
                if t >= 1:
                    pe.wait_ge(kt_dve, 3 * t)
                for j in range(6):
                    mm = pe.transpose(PS[0:n, 6 + j // 4, P * (j % 4):P * (j % 4 + 1)],
                                      hA[:, 4 + j, P * t:P * t + n], ident)
                    if j == 3:
                        mm.then_inc(kt_ps, 1)
                pe.transpose(PS[0:n, 7, 256:280], hG[0:24, P * t:P * t + n], ident[0:24, 0:24]).then_inc(kt_ps, 1)
            pe.wait_ge(cw_in, 16 * 16)
            for c in range(2):
                for g in range(2):
                    for l in range(STRIDE):
                        mm = pe.matmul(PS[:, 4 + g, c * NCMP_P:(c + 1) * NCMP_P],
                                       cw64[HD * g:HD * (g + 1), c, l, :],
                                       hA[HD * g:HD * (g + 1), 4 + c, l:SEQ:STRIDE],
                                       start=(l == 0), stop=(l == STRIDE - 1))
            for c in range(2):
                for half in range(2):
                    for q in range(16):
                        mm = pe.matmul(PS[HD * half:HD * (half + 1), 2, c:c + 1],
                                       cw2[:, c, q % 8, HD * (q // 8):HD * (q // 8 + 1)], cpos[:, c, q:q + 1],
                                       start=(q == 0), stop=(q == 15))
            mm.then_inc(cp_ps, 1)
            pe.wait_ge(cp_dve, 3)
            for g in range(2):
                mm = pe.transpose(PS[0:NCMP_P, 3, HD * g:HD * (g + 1)], cmpK[:, 2 + g, :], ident[0:HD, 0:HD])
            mm.then_inc(cp_ps, 1)

            def scores(j):
                h, i, wc = job(j)
                if j % 16 == 0:
                    pe.wait_ge(q_s, h + 1)
                    pe.wait_ge(q_row, h + 1)
                if j >= 2:
                    pe.wait_ge(e_act, exps(j - 2))
                q = qS[:, h % 2, P * i:P * (i + 1)]
                g = h // 4
                if not wc:
                    spans = [(0, g, k0, min(512, P * (i + 1) - k0), k0) for k0 in range(0, P * (i + 1), 512)]
                else:
                    lo, n = P * max(0, i - 4), P * min(i + 1, 5)
                    spans = [(1, g, lo + k0, min(512, n - k0), k0) for k0 in range(0, n, 512)]
                for br, g, k0, n, col in spans:
                    mm = pe.matmul(PS[:, 2 * wc + col // 512, col % 512:col % 512 + n], q, kA[:, br, g, k0:k0 + n],
                                   start=True, stop=True)
                if wc:
                    mm = pe.matmul(PS[:, 3, 128:128 + NCMP_P], q, kcA[:, g, :], start=True, stop=True)
                mm.then_inc(ss_ps, 1)

            def turn(j, gi):
                h, i, wc = job(j)
                if gi == 0:
                    pe.wait_ge(p_dve, j + 1)
                    if j >= 1:
                        pe.wait_ge(t_act, j)
                else:
                    if second_groups[j] >= 1:
                        pe.wait_ge(t_dve, second_groups[j])
                for b, (br, k0, n, col) in enumerate(groups(j)[gi]):
                    mm = pe.transpose(PS[0:n, 4 + gi, P * b:P * (b + 1)], pr[:, j % 2, col:col + n], ident)
                mm.then_inc(t_ps, 1)

            def pv(j, gi):
                h, i, wc = job(j)
                g = h // 4
                if gi == 0:
                    pe.wait_ge(t_act, j + 1)
                    if j % 2 == 0 and j >= 4:
                        pe.wait_ge(o_act, j // 2 - 1)
                else:
                    pe.wait_ge(t_dve, second_groups[j] + 1)
                last_g = gi == len(groups(j)) - 1
                for b, (br, k0, n, col) in enumerate(groups(j)[gi]):
                    if br == 2:
                        v = vcN[:, g, :]
                    else:
                        at = 384 + 256 * br + HD * g
                        v = kvtok[:, k0 // P, at:at + HD]
                    first = wc == 0 and gi == 0 and b == 0
                    last = wc == 1 and last_g and b == len(groups(j)[gi]) - 1
                    mm = pe.matmul(PS[HD * (h % 2):HD * (h % 2 + 1), 6 + i % 2, 0:P], v[0:n, :], PT[0:n, j % 2, gi, P * b:P * (b + 1)],
                                   start=first, stop=last)
                mm.then_inc(pv_ps, 1)

            pe.wait_ge(ka_s, 16 * 5 + 4)
            scores(0)
            scores(1)
            for j in range(NJ + 1):
                if j + 2 < NJ:
                    scores(j + 2)
                if j < NJ:
                    for gi in range(len(groups(j))):
                        turn(j, gi)
                if j >= 1:
                    for gi in range(len(groups(j - 1))):
                        pv(j - 1, gi)

            pe.drain().then_inc(ph, 1)
            pe.wait_ge(ph, 3)
            pe.wait_ge(dve_r, 1)
            pe.matmul(PS[:, 7, 0:NB], const("pagespread", PAGES), tabf, start=True, stop=True).then_inc(pe_r, 1)
            pe.matmul(PS[0:NROW, 6, 0:24], const("ownT", NB), gates[0:NB, NQ, :], start=True, stop=True).then_inc(pe_r, 1)

            def cmp_turn(n):
                pe.wait_ge(raw_in[n % 2], 16 * (n // 2 + 1))
                for a, (c, par, q) in enumerate((c, par, q) for c in range(2) for par in range(2) for q in range(4)):
                    if a % 4 == 0 and n >= 1:
                        pe.wait_ge((cx_act, cx_dve)[c], 4 * (n - 1) + 2 * (par + 1))
                    at = 256 * (2 * q + par) + P * c
                    mm = pe.transpose(PS[:, a // 4, P * (a % 4):P * (a % 4 + 1)], raw[:, n % 2, at:at + P], ident)
                    if a % 4 == 3:
                        mm.then_inc(d_ps, 1)

            def cmp_products(n):
                b, half = n // 2, n % 2
                pe.wait_ge(cx_act, 4 * (n + 1))
                pe.wait_ge(cx_dve, 4 * (n + 1))
                if half == 0 and b >= 2:
                    pe.wait_ge(vc_s, b - 1)
                for c in range(2):
                    for q in range(4):
                        mm = pe.matmul(PS[:, 4 + 2 * (b % 2) + c, 0:256], cw2[:, c, 4 * half + q, :],
                                       xt2[:, n % 2, 256 * (4 * c + q):256 * (4 * c + q + 1)],
                                       start=(half == 0 and q == 0), stop=(half == 1 and q == 3))
                mm.then_inc(dc_ps, 1)

            pe.wait_ge(dve_r, 3)
            for n in range(18):
                if n < 16:
                    cmp_turn(n)
                if 1 <= n < 17:
                    cmp_products(n - 1)
                if n >= 3 and n % 2:
                    b = (n - 3) // 2
                    pe.wait_ge(kv_d, b + 1)
                    pe.transpose(PS[:, 4 + 2 * (b % 2), 256:384], vct[:, b % 2, :], ident).then_inc(vc_ps, 1)
            pe.wait_ge(kv_d, NB)
            pe.wait_ge(dve_r, 4)
            for b in range(NB):
                mm = pe.matmul(PS[0:NROW, 0, 0:NCMP_S], qbd[:, b, :], kcd[:, b, :], start=(b == 0), stop=(b == NB - 1))
            mm.then_inc(pe_r, 1)
            pe.wait_ge(dve_r, 5)
            pe.matmul(PS[0:16, 1, 0:NCMP_S], const("gsum", NROW), P_cmp, start=True, stop=True).then_inc(pe_r, 1)
            pe.wait_ge(rank_s, 1)
            pe.matmul(PS[0:NROW, 6, 0:NBLK_S], const("gspread", 16), blkm[:, 3, :], start=True, stop=True).then_inc(pe_r, 1)
            pe.wait_ge(dve_r, 6)

            def sel_turn(n):
                m = n - 16
                pe.wait_ge(raw_in[n % 2], 16 * (n // 2 + 1))
                for a in range(8):
                    if a % 4 == 0:
                        if m >= 1:
                            pe.wait_ge((d_act, d_dve)[a // 4], m)
                    mm = pe.transpose(PS[:, 4 + a // 4, P * (a % 4):P * (a % 4 + 1)],
                                      raw[:, n % 2, 256 * a:256 * a + P], ident)
                    if a % 4 == 3:
                        mm.then_inc(d_ps, 1)

            def sel_scores(m):
                b, half = m // 2, m % 2
                for s in range(2):
                    pe.wait_ge((d_act, d_dve)[s], m + 1)
                    pe.matmul(PS[0:NROW, 2 * half + s, :], qbd[:, b, :], ktd[:, s, :], start=(b == 0),
                              stop=(b == NB - 1)).then_inc(sc_ps, 1)

            for n in range(16, 32):
                sel_turn(n)
                sel_scores(n - 16)
            for b in range(NB):
                pe.wait_ge(wraw_in[b % 2], 16 * (b // 2 + 1))
                done, bank = ((d_act, 4), (d_dve, 5))[b % 2]
                pe.wait_ge(done, 16 + b // 2)
                for a in range(4):
                    mm = pe.transpose(PS[:, bank, P * a:P * (a + 1)], raw[:, b % 2, 256 * a:256 * a + P], ident)
                mm.then_inc(d_ps, 1)
                pe.wait_ge(done, 16 + b // 2 + 1)
                pe.matmul(PS[0:NROW, 6, :], qbd[:, b, :], ktd[:, b % 2, :], start=(b == 0), stop=(b == NB - 1)
                          ).then_inc(sc_ps, 1)
            for s in range(2):
                for b in range(NB):
                    mm = pe.matmul(PS[0:NROW, 7, s:s + 1], qbd[:, b, :], knew[:, s, b:b + 1], start=(b == 0),
                                   stop=(b == NB - 1))
            mm.then_inc(sc_ps, 1)
            pe.wait_ge(dve_r, 10)
            for a in range(16):
                pe.transpose(PS[:, a // 8, NROW * (a % 8):NROW * (a % 8 + 1)], P_sel[:, P * a:P * (a + 1)],
                             ident[0:NROW, 0:NROW])
            for a in range(4):
                pe.transpose(PS[:, 2, NROW * a:NROW * (a + 1)], P_win[:, P * a:P * (a + 1)], ident[0:NROW, 0:NROW])
            pe.transpose(PS[:, 2, 4 * NROW:5 * NROW], P_cmp, ident[0:NROW, 0:NROW])
            for s in range(2):
                mm = pe.transpose(PS[0:NB, 3, NROW * s:NROW * (s + 1)], pnew[:, s, :], ident[0:NROW, 0:NROW])
            mm.then_inc(pe_r, 1)
            pe.wait_ge(dve_r, 12)
            pe.wait_ge(v_s, 16)
            pe.wait_ge(wv_in, 16 * NB)
            for s in range(2):
                pe.matmul(PS[:, 4, 0:NROW], kvd[:, 384 + 256 * s:512 + 256 * s], pnewT[:, s, :], start=(s == 0), stop=False,
                          skip_group_check=True)
            for b in range(NB):
                cols = slice(8 * b, 8 * b + 8)
                for a in range(16):
                    pe.matmul(PS[:, 4, cols], vall[:, b, a, :], ptdv[:, a, cols], start=False, stop=False,
                              skip_group_check=True)
                for a in range(4):
                    pe.matmul(PS[:, 4, cols], raww[:, b, a, :], ptdv[:, 16 + a, cols], start=False, stop=False,
                              skip_group_check=True)
                mm = pe.matmul(PS[:, 4, cols], vcd[:, b, :], ptdv[:, 20, cols], start=False, stop=(b == NB - 1),
                               skip_group_check=True)
            mm.then_inc(pe_r, 1)
            pe.drain().then_inc(ph, 1)
            pe.wait_ge(ph, 6)
            for n in range(U_IB, U_IB + 4):
                unit_matmuls(pe, n)
            unit_matmuls(pe, U_IB + 4)
            for t in range(NQ + 1):
                n = toks(t)
                if t >= 3:
                    pe.wait_ge(vt_dve, t - 2)
                pe.wait_ge(u_act, 3 * (U_IB + 4))
                for j in range(4):
                    mm = pe.transpose(PS[0:n, 5 + t % 3, P * j:P * (j + 1)], ibT[:, j, P * t:P * t + n], ident)
                mm.then_inc(vt_ps, 1)
            for n in range(U_IB + 5, U_H):
                unit_matmuls(pe, n)
            unit_matmuls(pe, U_H)
            unit_matmuls(pe, U_H + 1)
            pe.wait_ge(vt_dve, NQ + 1)

            def wbank(h, s):
                i = wstep(h, s)
                if i >= 3:
                    pe.wait_ge(*copied(i - 3))
                return 5 + i % 3

            def turn_out(h):
                pe.wait_ge(on_s, h + 1)
                for s in (9, 10):
                    bank = wbank(h, s)
                    for j in range(4):
                        mm = pe.transpose(PS[:, bank, P * j:P * (j + 1)], onb[:, 4 * (s - 9) + j, :], ident)
                    mm.then_inc(w_ps, 1)

            for h in range(HG):
                if h + 1 < HG:
                    unit_matmuls(pe, U_H + 2 * (h + 1))
                if h >= 1 and h % 2 == 0:
                    turn_out(h - 1)
                pe.wait_ge(hk, h + 1)
                for s in (0, 1):
                    bank = wbank(h, s)
                    for j in range(4):
                        t = 4 * s + j
                        mm = pe.transpose(PS[:, bank, P * j:P * (j + 1)], lcb[:, P * t:P * (t + 1)], ident)
                    mm.then_inc(w_ps, 1)
                for s in (2, 3):
                    bank = wbank(h, s)
                    for j in range(4):
                        t = 4 * (s - 2) + j
                        mm = pe.matmul(PS[:, bank, P * j:P * (j + 1)], kf[:, P * t:P * (t + 1)],
                                       qT[:, h % 2, P * t:P * (t + 1)], start=True, stop=True)
                    mm.then_inc(w_ps, 1)
                pe.wait_ge(vb_s, 4 * (h + 1))
                pe.wait_ge(*copied(wstep(h, 1)))
                for s in (4, 5, 6, 7):
                    bank = wbank(h, s)
                    for j in range(2):
                        t = 2 * (s - 4) + j
                        mm = pe.matmul(PS[:, bank, 256 * j:256 * (j + 1)], kkt[:, t, :],
                                       vbd[:, t, :, :].rearrange("p j v -> p (j v)"), start=True, stop=True)
                    mm.then_inc(w_ps, 1)
                if h + 1 < HG:
                    unit_matmuls(pe, U_H + 2 * (h + 1) + 1)
                pe.wait_ge(*copied(wstep(h, 3)))
                pe.wait_ge(s_s, NCH * (h + 1) - 1)
                bank = wbank(h, 8)
                for t in range(NQ):
                    out = PS[:, bank, DV * t:DV * (t + 1)]
                    pe.matmul(out, atm[:, t, :], vt[:, t, DV * h:DV * (h + 1)], start=True, stop=False,
                              skip_group_check=True)
                    for j in range(4):
                        c = 4 * t + j
                        if c:
                            mm = pe.matmul(out[CH * j:CH * (j + 1), :], qT[:, h % 2, CH * c:CH * (c + 1)], Sb[:, c - 1, :],
                                           start=False, stop=True, skip_group_check=True)
                mm.then_inc(w_ps, 1)
            turn_out(HG - 1)
            for b in range(NB):
                pe.wait_ge(*copied(len(wsteps) - 1))
                if b >= 3:
                    pe.wait_ge(dg_dve, 3 * (b - 2))
                pe.matmul(PS[:, 5 + b % 3, :], const("rowb", NB).rearrange("p (b n) -> p b n", b=NB)[:, b, :], vdec,
                          start=True, stop=True).then_inc(dg_ps, 1)
            pe.wait_ge(dg_dve, 3 * NB)
            for h in range(HG):
                for b in range(NB):
                    mm = pe.matmul(PS[0:NB, 5, DV * h:DV * (h + 1)], qz[:, h, b, :], stt[:, b, h, :], start=(b == 0),
                                   stop=(b == NB - 1))
            mm.then_inc(dg_ps, 1)
            pe.wait_ge(dg_dve, 3 * NB + 4)
            for j in range(4):
                mm = pe.transpose(PS[:, 6, NB * j:NB * (j + 1)], onb[0:NB, j, :], ident[0:NB, 0:NB])
            mm.then_inc(dg_ps, 1)
            pe.drain().then_inc(ph, 1)
            pe.wait_ge(ph, 9)
            for s in range(NM):
                i, ci = s // 3, s % 3
                c0, cn = CHUNKS[ci]
                if s >= 2:
                    pe.wait_ge(m_dve2, s - 1)
                if s == 0:
                    pe.wait_ge(u_act, 3 * U_M)
                for ab in range(2):
                    n = U_M + 3 * i + ab
                    if ci == 0:
                        pe.wait_ge(wl_dve, SPLITS_M + 2 * i + ab + 1)
                    if s == 0:
                        pe.wait_ge(xl_dve, KD)
                    split_product(pe, PS[:, 4 * (s % 2) + ab, 0:cn], [whM[:, 2 * (i % 2) + ab, k] for k in range(KD)],
                                  [wl[:, n % WR, k] for k in range(KD)], [xhM[:, k, c0:c0 + cn] for k in range(KD)],
                                  [xl[:, k, c0:c0 + cn] for k in range(KD)]).then_inc(g_ps, 1)
                n = U_M + 3 * i + 2
                pe.wait_ge(w_in_s[n % WR], 32 * (n // WR + 1))
                for ab, a in enumerate((aT, rT)):
                    for k in range(4):
                        mm = pe.matmul(PS[:, 4 * (s % 2) + 2 + ab, 0:cn], wring[:, n % WR, 4 * ab + k, :], a[:, k, c0:c0 + cn],
                                       start=(k == 0), stop=(k == 3))
                    mm.then_inc(g_ps, 1)
            pe.wait_ge(m_dve2, NM)

            def turn_x1(t):
                n = toks(t)
                pe.wait_ge(x1_s, t + 1)
                for half in range(2):
                    if t >= 2:
                        pe.wait_ge(x1l_dve, 2 * (t - 2) + half + 1)
                    for j in range(4):
                        k = 4 * half + j
                        mm = pe.transpose(PS[:, 4 + 2 * (t % 2) + half, P * j:P * j + n], x1[0:n, t, P * k:P * (k + 1)],
                                          ident[0:n, 0:n])
                    mm.then_inc(xt1_ps, 1)

            for t in range(NQ + 1):
                n = toks(t)
                if t >= 2:
                    pe.wait_ge(f_dve, t - 1)
                for part in (1, 0):
                    if t == 0:
                        pe.wait_ge(wo_in[part], 16)
                    for half in range(2):
                        for k in range(4 * part, 4 * part + 4):
                            mm = pe.matmul(PS[0:n, 2 * (t % 2) + half, :], mT[:, k, P * t:P * t + n],
                                           wo[:, k, 512 * half:512 * (half + 1)], start=(k == 4), stop=(k == 3))
                mm.then_inc(f_ps, 1)
                if t >= 1:
                    turn_x1(t - 1)
            turn_x1(NQ)
            pe.wait_ge(x1l_dve, 2 * (NQ + 1))

            def up(i):
                n = U_U + i
                pe.wait_ge(wl_dve, SPLITS_U + i + 1)
                for ci, (c0, cn) in enumerate(CHUNKS):
                    x = 3 * i + ci
                    if x >= 5:
                        pe.wait_ge(relu_act, x - 4)
                    split_product(pe, unit_out(x, P, cn), [whM[:, i % 2, k] for k in range(KD)],
                                  [wl[:, n % WR, k] for k in range(KD)], [x1h[:, k, c0:c0 + cn] for k in range(KD)],
                                  [xl[:, k, c0:c0 + cn] for k in range(KD)]).then_inc(u_ps, 1)

            def down(g):
                pe.wait_ge(wdl_dve, g + 1)
                pe.wait_ge(ul_dve, 2 * (g + 1))
                u, w = uR[g % 2], wdl[:, g % 2]
                for t in range(NQ + 1):
                    tk = slice(P * t, P * t + toks(t))
                    for half in range(2):
                        d, cols = 18 * g + 2 * t + half, slice(512 * half, 512 * (half + 1))
                        if d >= 3:
                            pe.wait_ge(dn_dve, d - 2)
                        split_product(pe, PS[0:toks(t), 5 + d % 3, :], [u[:, j, 1, tk] for j in range(2)],
                                      [u[:, j, 0, tk] for j in range(2)], [wdh[:, j, cols] for j in range(2)],
                                      [w[:, j, cols] for j in range(2)]).then_inc(dn_ps, 1)

            for g in range(NG):
                up(2 * g)
                up(2 * g + 1)
                if g >= 1:
                    down(g - 1)
            down(NG - 1)

        @block.scalar
        def _(act):
            for t in range(NQ + 1):
                n = toks(t)
                if t == 2 or t == 4:
                    split_high(act, t // 2 - 1, whA[:, t // 2 - 1])
                for half in range(2):
                    act.wait_ge(xt_ps, 2 * t + half + 1)
                    act.activation(xhA[:, 4 * half:4 * half + 4, P * t:P * t + n],
                                   PS[:, 2 * (t % 2) + half, :].rearrange("p (j n) -> p j n", j=4)[:, :, 0:n], ACT.Copy
                                   ).then_inc(xt_act, 1)

            def unit_copy(n):
                v, c, m, dst, fn = units[n]
                for ci, (c0, cn) in enumerate(CHUNKS):
                    act.wait_ge(u_ps, 3 * n + ci + 1)
                    act.activation(dst[0:m, c0:c0 + cn], unit_out(3 * n + ci, m, cn), fn).then_inc(u_act, 1)
            for n in range(NU_ATT):
                if 1 <= n < NU_ATT - 1:
                    act.wait_ge(u_ps, 3 * n)
                    split_high(act, n + 1, whA[:, (n + 1) % 2])
                unit_copy(n)
            act.wait_ge(cp_ps, 1)
            act.wait_ge(kt_ps, 2 * (NQ + 1))
            act.activation(cmpT.rearrange("p (c g) n -> p g c n", c=2),
                           PS[HD:P, 4:6, 0:2 * NCMP_P].rearrange("p g (c n) -> p g c n", c=2), ACT.Copy
                           ).then_inc(cp_act, 1)

            def exp(j):
                h, i, wc = job(j)
                act.wait_ge(m_dve, j + 1)
                if j >= 2:
                    act.wait_ge(t_ps, first_group[j - 1])
                if not wc:
                    n = P * (i + 1)
                    act.activation(pr[:, 0, 0:n], PS[:, 0:2, :].rearrange("p a n -> p (a n)")[:, 0:n], ACT.Exp,
                                   bias=small[:, 16 * (j % 4):16 * (j % 4) + 1],
                                   accum_out=small[:, 16 * (j % 4) + 4:16 * (j % 4) + 5]).then_inc(e_act, 1)
                else:
                    for w, (c0, n) in enumerate(((0, P * min(i + 1, 5)), (640, NCMP_P))):
                        act.activation(pr[:, 1, c0:c0 + n], PS[:, 2:4, :].rearrange("p a n -> p (a n)")[:, c0:c0 + n],
                                       ACT.Exp, bias=small[:, 16 * (j % 4) + w:16 * (j % 4) + w + 1],
                                       accum_out=small[:, 16 * (j % 4) + 4 + w:16 * (j % 4) + 5 + w]).then_inc(e_act, 1)

            def stage_q(h):
                if h >= 2:
                    act.wait_ge(ss_ps, 16 * (h - 1))
                act.activation(qS[0:HD, h % 2, :], hA[HD * (h % 2):HD * (h % 2 + 1), h // 2, 0:SEQ], ACT.Copy,
                               scale=HD ** -0.5).then_inc(q_s, 1)

            def out(n):
                h, i = heads[n]
                act.wait_ge(pv_ps, first_group[2 * n + 2])
                act.activation(aT[HD * (h % 2):HD * (h % 2 + 1), h // 2, P * i:P * (i + 1)],
                               PS[HD * (h % 2):HD * (h % 2 + 1), 6 + i % 2, 0:P], ACT.Copy).then_inc(o_act, 1)

            act.wait_ge(kt_ps, 2 * (NQ + 1))
            act.wait_ge(cp_ps, 2)
            act.wait_ge(cp_dve, 5)
            stage_q(0)
            exp(0)
            exp(1)
            for j in range(NJ):
                act.wait_ge(t_ps, first_group[j] + 1)
                if j >= 2:
                    act.wait_ge(pv_ps, first_group[j - 1])
                ev = evacuations(groups(j)[0])
                for e, (r, c0, c1) in enumerate(ev):
                    ins = act.activation(PT[0:r, j % 2, 0, c0:c1], PS[0:r, 4, c0:c1], ACT.Copy)
                    if e == len(ev) - 1:
                        ins.then_inc(t_act, 1)
                if j + 2 < NJ:
                    exp(j + 2)
                if j % 2 == 0 and j >= 2:
                    out(j // 2 - 1)
                if j % 16 == 4 and j // 16 + 1 < 8:
                    stage_q(j // 16 + 1)
            out(len(heads) - 1)

            act.drain().then_inc(ph, 1)
            act.wait_ge(ph, 3)

            def part1(b):
                act.wait_ge(dc_ps, 2 * b + 2)
                if b >= 1:
                    act.wait_ge(kv_d, b)
                act.activation(tmp1, PS[HD:P, 4 + 2 * (b % 2):6 + 2 * (b % 2), 0:256].rearrange(
                    "p c (g n) -> p c g n", g=2), ACT.Copy).then_inc(kv_a, 1)

            for n in range(16):
                for s in range(2):
                    act.wait_ge(d_ps, 4 * n + s + 1)
                    if n >= 2:
                        act.wait_ge(dc_ps, n - 1)
                    for g in range(2):
                        act.activation(xt_of(n, 0, s, g), PS[HD * g:HD * (g + 1), s, :].rearrange("p (q n) -> p q n", q=4),
                                       ACT.Copy).then_inc(cx_act, 1)
                if n >= 2 and n % 2 == 0:
                    part1(n // 2 - 1)
            part1(NB - 1)
            act.wait_ge(dve_r, 4)
            ast = Steps(act, act_r)
            act.wait_ge(dst2, 4)
            ast(act.activation(P_cmp, P_cmp, ACT.Exp, bias=dsm[:, 0:1], accum_out=dsm[:, 3:4]))
            for m in range(16):
                act.wait_ge(d_ps, 64 + 2 * m + 1)
                if m >= 1:
                    act.wait_ge(sc_ps, 2 * m - 1)
                act.activation(ktd[:, 0, :], PS[:, 4, :], ACT.Copy).then_inc(d_act, 1)
            for b in range(0, NB, 2):
                act.wait_ge(d_ps, 96 + b + 1)
                act.wait_ge(sc_ps, 31 if b == 0 else 32 + b - 1)
                act.activation(ktd[:, 0, :], PS[:, 4, :], ACT.Copy).then_inc(d_act, 1)
            act.wait_ge(dve_r, 8)
            ast(act.activation(P_sel, P_sel, ACT.Exp, bias=dsm[:, 1:2], accum_out=dsm[:, 4:5]))
            ast(act.activation(P_win, P_win, ACT.Exp, bias=dsm[:, 2:3], accum_out=dsm[:, 5:6]))
            act.drain().then_inc(ph, 1)
            act.wait_ge(ph, 6)
            act.wait_ge(small_in, 64)
            act.wait_ge(hd, 3)
            act.activation(lbt[:, 3, :], lbt[:, 3, :], ACT.Exp).then_inc(lb_act, 1)
            act.activation(lbt[:, 4, :], lbt[:, 4, :], ACT.Exp).then_inc(lb_act, 1)
            for n in range(U_IB, U_H + 2):
                if n == U_H:
                    act.wait_ge(lb_act, 2)
                unit_copy(n)

            def step_copy(h, s):
                i = wstep(h, s)
                act.wait_ge(w_ps, i + 1)
                dst = kkt[:, 4 * s:4 * s + 4, :] if s < 2 else Ub[:, 8 * (s - 4):8 * (s - 3), :]
                if s == 0 and h >= 1:
                    act.wait_ge(w_ps, wstep(h - 1, 7) + 1)
                if s == 4:
                    act.wait_ge(vt_ps, NQ + 1)
                    if h >= 1:
                        act.wait_ge(s_s, NCH * h)
                act.activation(dst, PS[:, 5 + i % 3, :].rearrange("p (a n) -> p a n", n=dst.shape[2]), ACT.Copy
                               ).then_inc(w_act, 1)

            ra = Steps(act, r_act)

            def decay(h):
                act.wait_ge(hf, h + 1)
                if h >= 1:
                    act.wait_ge(hk, h)
                act.activation(lfb, fT[:, h % 2, 0:SEQ], ACT.Ln).then_inc(hl, 1)
                act.wait_ge(hs, h + 1)
                act.activation(lfb, lcb, ACT.Exp, scale=-1.0).then_inc(he, 1)
                act.wait_ge(he, 2 * h + 1)
                act.activation(lcb, lcb, ACT.Exp).then_inc(he, 1)

            decay(0)
            for h in range(HG):
                if h + 1 < HG:
                    if h >= 1:
                        act.wait_ge(hk, h)
                    unit_copy(U_H + 2 * (h + 1))
                for s in (0, 1, 4, 5, 6, 7):
                    step_copy(h, s)
                if h + 1 < HG:
                    if h >= 1:
                        act.wait_ge(w_ps, wstep(h - 1, 8) + 1)
                    unit_copy(U_H + 2 * (h + 1) + 1)
                    decay(h + 1)
                act.wait_ge(lb_s, h + 1)
                ra(act.activation(hsm[:, 8:16], hsm[:, 0:8], ACT.Ln, scale=1.0 / DV, bias=hsm[:, 95:96]))
                ra(act.activation(hsm[:, 16:24], hsm[:, 8:16], ACT.Exp, scale=-0.5))
            act.wait_ge(dg_dve, 3 * NB + 3)
            ra(act.activation(hsm[0:NB, 8:16], hsm[0:NB, 0:8], ACT.Ln, scale=1.0 / DV, bias=hsm[0:NB, 95:96]))
            ra(act.activation(hsm[0:NB, 16:24], hsm[0:NB, 8:16], ACT.Exp, scale=-0.5))
            act.drain().then_inc(ph, 1)
            act.wait_ge(ph, 9)
            act.activation(xhM[:, 0, :], xT[:, 0, :], ACT.Copy).then_inc(xh_act, 1)
            for ab in range(2):
                split_high(act, U_M + ab, whM[:, ab])
            for k in range(1, KD):
                act.activation(xhM[:, k, :], xT[:, k, :], ACT.Copy).then_inc(xh_act, 1)
            for s in range(NM):
                cn = CHUNKS[s % 3][1]
                if s % 3 == 1 and s // 3 + 1 < KD:
                    i = s // 3 + 1
                    for ab in range(2):
                        if i >= 2:
                            act.wait_ge(*unit_done(U_M + 3 * (i - 2) + ab))
                        split_high(act, U_M + 3 * i + ab, whM[:, 2 * (i % 2) + ab])
                for ab in range(2):
                    act.wait_ge(g_ps, 4 * s + ab + 1)
                    if s >= 2:
                        act.wait_ge(m_dve2, s - 1)
                    act.activation(sgb[:, s % 2, ab, 0:cn], PS[:, 4 * (s % 2) + ab, 0:cn], ACT.Sigmoid).then_inc(m_act, 1)

            ra2 = Steps(act, ln_r)

            def rstd_of(t, lnum):
                n = toks(t)
                act.wait_ge(ln_v, (NQ + 1) * lnum + t + 1)
                ra2(act.activation(rstd[0:n, 0:1], mv[0:n, 1:2], ACT.Ln, bias=epsb[0:n, :]))
                ra2(act.activation(rstd[0:n, 1:2], rstd[0:n, 0:1], ACT.Exp, scale=-0.5))

            for t in range(NQ + 1):
                n = toks(t)
                rstd_of(t, 0)
                for half in range(2):
                    act.wait_ge(xt1_ps, 2 * t + half + 1)
                    act.activation(x1h[:, 4 * half:4 * half + 4, P * t:P * t + n],
                                   PS[:, 4 + 2 * (t % 2) + half, :].rearrange("p (j n) -> p j n", j=4)[:, :, 0:n], ACT.Copy
                                   ).then_inc(xt1_act, 1)
            act.wait_ge(f_ps, NQ + 1)
            for i in range(2):
                split_high(act, U_U + i, whM[:, i])
            for i in range(F_FF // P):
                g = i // 2
                if g >= 2:
                    act.wait_ge(dn_ps, 18 * (g - 1))
                for ci, (c0, cn) in enumerate(CHUNKS):
                    act.wait_ge(u_ps, 3 * (U_U + i - (U_U - U_M)) + ci + 1)
                    act.activation(uT[g % 2][:, i % 2, 0, c0:c0 + cn], unit_out(3 * i + ci, P, cn), ACT.Relu).then_inc(relu_act, 1)
                act.wait_ge(sq_dve, i + 1)
                act.activation(uR[g % 2][:, i % 2, 1, :], uT[g % 2][:, i % 2, 0, :], ACT.Copy).then_inc(uh_act, 1)
                if i + 2 < F_FF // P:
                    split_high(act, U_U + i + 2, whM[:, i % 2])
                if i % 2 == 1:
                    act.wait_ge(wd_in[g % 2], 16 * (g // 2 + 1))
                    if g >= 1:
                        act.wait_ge(dn_ps, 18 * g)
                    act.activation(wdh[:, :, :], wdn[:, g % 2], ACT.Copy).then_inc(wdh_act, 1)
            for t in range(NQ + 1):
                rstd_of(t, 1)

        @block.vector
        def _(dve):
            for t in range(NQ + 1):
                n = toks(t)
                if t == 2 or t == 4:
                    split_low(dve, t // 2 - 1, t // 2 - 1, whA[:, t // 2 - 1])
                for half in range(2):
                    dve.wait_ge(xt_act, 2 * t + half + 1)
                    s = (slice(None), slice(4 * half, 4 * half + 4), slice(P * t, P * t + n))
                    dve.tensor_tensor(xl[s], PS[:, 2 * (t % 2) + half, :].rearrange("p (j n) -> p j n", j=4)[:, :, 0:n],
                                      xhA[s].bitcast(F32), ALU.subtract).then_inc(xt_dve, 1)
            for n in range(2, NU_ATT):
                split_low(dve, n, n, whA[:, n % 2])
            dve.wait_ge(u_ps, 3 * NU_ATT)
            for k in range(5):
                dve.tensor_tensor(xT[:, k, :], xl[:, k, :].bitcast(F32), xhA[:, k, :].bitcast(F32), ALU.add).then_inc(x_dve, 1)
            dve.wait_ge(x_dve, 5)
            dve.wait_ge(x_pool, KD - 5)
            for t in range(NQ + 1):
                n = toks(t)
                dve.wait_ge(kt_ps, 2 * t + 1)
                kv = kvtok[:, t, :] if t < NQ else kvd
                dve.tensor_copy(kv[0:n, 0:512], PS[0:n, 6, :]).then_inc(kt_dve, 1)
                dve.wait_ge(kt_ps, 2 * t + 2)
                dve.tensor_copy(kv[0:n, 512:768], PS[0:n, 7, 0:256]).then_inc(kt_dve, 1)
                dve.tensor_copy(gates[0:n, t, :], PS[0:n, 7, 256:280]).then_inc(kt_dve, 1)
            cps = Steps(dve, cp_dve)
            dve.wait_ge(cp_act, 1)
            cps(dve.tensor_copy(cb[:, 0:2], PS[:, 2, 0:2]))
            cps(dve.memset(cmpK[:, :, :], 0.0))
            for c in range(2):
                s = slice(2 * c, 2 * c + 2)
                ins = dve.scalar_tensor_tensor(
                    out=cmpK[:, s, 0:NCMP_P - 1],
                    in0=PS[0:HD, 4:6, c * NCMP_P:(c + 1) * NCMP_P - 1],
                    scalar=cb[0:HD, c:c + 1], in1=cmpT[:, s, 1:NCMP_P], op0=ALU.add, op1=ALU.add)
                if c:
                    cps(ins)
            dve.wait_ge(cp_ps, 2)
            cps(dve.tensor_copy(vcN, PS[0:NCMP_P, 3, 0:P].rearrange("p (g e) -> p g e", g=2)))
            cps(dve.tensor_copy(kcA[0:HD, :, :], cmpK[:, 0:2, :]))
            dve.wait_ge(ka_s, 16 * 5)
            for br in range(2):
                for g in range(2):
                    dve.tensor_copy(kA[0:HD, br, g, :], hA[HD * g:HD * (g + 1), 6 + 2 * br, 0:SEQ]).then_inc(ka_s, 1)
            steps = Steps(dve, dch)

            def slope_row(h):
                if h >= 2:
                    dve.wait_ge(ss_ps, 16 * (h - 1))
                dve.memset(qS[64:65, h % 2, :], 2.0 ** -(h + 1)).then_inc(q_row, 1)

            def maxima(j):
                h, i, wc = job(j)
                dve.wait_ge(ss_ps, j + 1)
                sc = PS[:, 2 * wc:2 * wc + 2, :].rearrange("p a n -> p (a n)")
                nm = small[:, 16 * (j % 4):16 * (j % 4) + 4]
                n = P * (i + 1) if not wc else P * min(i + 1, 5)
                own = sc[:, n - P:n]
                steps(dve.tensor_tensor(own, own, const("causal"), ALU.add))
                if wc and i >= 4:
                    steps(dve.tensor_tensor(sc[:, 0:P], sc[:, 0:P], const("winlow"), ALU.add))
                if wc:
                    cm = const("cmpmask").rearrange("p (t n) -> p t n", t=NQ)[:, i, :]
                    steps(dve.tensor_tensor(sc[:, 640:704], sc[:, 640:704], cm, ALU.add))
                    steps(dve.tensor_reduce(nm[:, 1:2], sc[:, 640:704], AX.X, ALU.max, negate=True))
                    if i == 0:
                        steps(dve.tensor_scalar(nm[:, 1:2], nm[:, 1:2], 1e29, None, ALU.min))
                dve.tensor_reduce(nm[:, 0:1], sc[:, 0:n], AX.X, ALU.max, negate=True).then_inc(m_dve, 1)

            def scale(j):
                h, i, wc = job(j)
                dve.wait_ge(e_act, exps(j))
                sm = small[:, 16 * (j % 4):16 * (j % 4) + 16]
                w = 2 if wc else 1
                if wc:
                    steps(dve.tensor_scalar(sm[:, 5:6], sm[:, 5:6], 1e-30, None, ALU.max))
                steps(dve.reciprocal(sm[:, 8:8 + w], sm[:, 4:4 + w]))
                gt = gates[:, i, :].rearrange("p (h c) -> p h c", c=3)[:, h, :]
                gt = gt[:, 1:2] if not wc else gt[:, 2:3]
                steps(dve.tensor_tensor(sm[:, 12:13], sm[:, 8:9], gt, ALU.mult))
                if wc:
                    steps(dve.tensor_tensor(sm[:, 13:14], sm[:, 9:10],
                                            gates[:, i, 3 * h:3 * h + 1], ALU.mult))
                    dve.tensor_scalar(pr[:, 1, 640:704], pr[:, 1, 640:704], sm[:, 13:14], None, ALU.mult)
                n = P * (i + 1) if not wc else P * min(i + 1, 5)
                dve.tensor_scalar(pr[:, wc, 0:n], pr[:, wc, 0:n], sm[:, 12:13], None, ALU.mult).then_inc(p_dve, 1)

            def second(j):
                if len(groups(j)) < 2:
                    return
                dve.wait_ge(t_ps, first_group[j] + 2)
                if j >= 2:
                    dve.wait_ge(pv_ps, first_group[j - 1])
                ev = evacuations(groups(j)[1])
                for e, (r, c0, c1) in enumerate(ev):
                    ins = dve.tensor_copy(PT[0:r, j % 2, 1, c0:c1], PS[0:r, 5, c0:c1])
                    if e == len(ev) - 1:
                        ins.then_inc(t_dve, 1)

            slope_row(0)
            maxima(0)
            maxima(1)
            scale(0)
            for j in range(NJ):
                if j + 2 < NJ:
                    maxima(j + 2)
                second(j)
                if j + 1 < NJ:
                    scale(j + 1)
                if j % 16 == 4 and j // 16 + 1 < 8:
                    slope_row(j // 16 + 1)
            ds = Steps(dve, dst2)
            ds(dve.memset(qbd[:, :, :], 0.0))
            qf = qbd.rearrange("p b r -> p (b r)")
            for g in range(2):
                for r in range(4):
                    h = 4 * g + r
                    dve.tensor_scalar(qf[HD * g:HD * (g + 1), h:h + 72 * (NB - 1) + 1:72],
                                      hA[HD * (h % 2):HD * (h % 2 + 1), h // 2, SEQ:T], HD ** -0.5, None, ALU.mult)
            dve.tensor_copy(knew[:, 0, :], hA[:, 6, SEQ:T])
            dve.tensor_copy(knew[:, 1, :], hA[:, 8, SEQ:T])
            dve.drain().then_inc(ph, 1)
            dve.wait_ge(ph, 3)
            rs = Steps(dve, dve_r)
            dve.wait_ge(tb_in, 32)
            rs(dve.tensor_copy(tabf, tabi))
            for half in range(2):
                dve.wait_ge(pe_r, 1)
                dve.tensor_scalar(idx[:, half, :], PS[:, 7, 0:NB], 16.0, const("half")[:, half:half + 1],
                                  ALU.mult, ALU.add).then_inc(ix_s, 1)
            dve.wait_ge(pe_r, 2)
            rs(dve.tensor_tensor(g64, PS[0:NROW, 6, 0:24],
                                 const("headsel", NROW).unsqueeze(2).to_broadcast([NROW, 8, 3]), ALU.mult))
            rs(dve.tensor_reduce(grow[:, 0:3], g64.rearrange("p (h c) -> p c h", c=3), AX.X, ALU.add))
            dve.memset(kcd[:, :, NCMP_S - 1:NCMP_S], 0.0)
            ds(dve.memset(vct[:, :, NCMP_S - 1:NCMP_S], 0.0))

            def blocks_of(b):
                dve.wait_ge(kv_a, b + 1)
                if b >= 2:
                    dve.wait_ge(vc_ps, b - 1)
                for c in range(2):
                    for g in range(2):
                        dst = kcd[:, b, :] if c == 0 else vct[:, b % 2, :]
                        ins = dve.scalar_tensor_tensor(
                            out=dst[HD * g:HD * (g + 1), 0:NCMP_S - 1],
                            in0=PS[0:HD, 4 + 2 * (b % 2) + c, NCMP_S * g:NCMP_S * (g + 1) - 1],
                            scalar=cb[0:HD, c:c + 1], in1=tmp1[:, c, g, 1:NCMP_S], op0=ALU.add, op1=ALU.add)
                ins.then_inc(kv_d, 1)

            def cmp_v(b):
                dve.wait_ge(vc_ps, b + 1)
                dve.tensor_copy(vcd[:, b, :], PS[:, 4 + 2 * (b % 2), 256:384]).then_inc(vc_s, 1)

            for n in range(18):
                if n < 16:
                    for s in range(2):
                        dve.wait_ge(d_ps, 4 * n + s + 3)
                        if n >= 2:
                            dve.wait_ge(dc_ps, n - 1)
                        for g in range(2):
                            dve.tensor_copy(xt_of(n, 1, s, g), PS[HD * g:HD * (g + 1), 2 + s, :].rearrange(
                                "p (q n) -> p q n", q=4)).then_inc(cx_dve, 1)
                if n >= 2 and n % 2 == 0:
                    blocks_of(n // 2 - 1)
                if n >= 3 and n % 2:
                    cmp_v((n - 3) // 2)
            rs(dve.memset(dsm[:, 31:32], 0.0))
            dve.wait_ge(pe_r, 3)
            dve.wait_ge(tb_in, 32)
            ds(dve.tensor_tensor(P_cmp, PS[0:NROW, 0, 0:NCMP_S], cmpbias, ALU.add))
            ds(dve.tensor_reduce(dsm[:, 0:1], P_cmp, AX.X, ALU.max, negate=True))
            dve.wait_ge(act_r, 1)
            ds(dve.tensor_scalar(dsm[:, 6:7], dsm[:, 3:4], 1e-30, None, ALU.max))
            ds(dve.reciprocal(dsm[:, 7:8], dsm[:, 6:7]))
            rs(dve.tensor_scalar(P_cmp, P_cmp, dsm[:, 7:8], None, ALU.mult))
            dve.wait_ge(pe_r, 4)
            ds(dve.memset(blkm[:, 0, :], 0.0))
            ds(dve.tensor_reduce(blkm[:, 0, 0:NBLK_S - 1], PS[0:16, 1, 0:NCMP_S].rearrange("p (b r) -> p b r", r=4),
                                 AX.X, ALU.add))
            ds(dve.tensor_tensor(blkm[:, 1, :], blkm[:, 0, :], const("free", 16), ALU.mult))
            ds(dve.tensor_tensor(blkm[:, 2, :], blkm[:, 1, :], const("forced", 16), ALU.add))
            other = blkm[:, 2, :].unsqueeze(1).to_broadcast([16, NBLK_S, NBLK_S])
            own_ = blkm[:, 2, :].unsqueeze(2).to_broadcast([16, NBLK_S, NBLK_S])
            ds(dve.tensor_tensor(rk1, other, own_, ALU.is_gt))
            ds(dve.tensor_tensor(rk2, other, own_, ALU.is_equal))
            ds(dve.tensor_tensor(rk2, rk2, const("below", 16).rearrange("p (a b) -> p a b", a=NBLK_S), ALU.mult))
            ds(dve.tensor_tensor(rk1, rk1, rk2, ALU.add))
            ds(dve.tensor_reduce(blkm[:, 1, :], rk1, AX.X, ALU.add))
            dve.tensor_scalar(blkm[:, 3, :], blkm[:, 1, :], N_SELECT - 0.5, NEG, ALU.is_gt, ALU.mult).then_inc(rank_s, 1)
            dve.wait_ge(pe_r, 5)
            rs(dve.tensor_copy(mb64, PS[0:NROW, 6, 0:NBLK_S - 1]))
            for m in range(16):
                dve.wait_ge(d_ps, 64 + 2 * m + 2)
                if m >= 1:
                    dve.wait_ge(sc_ps, 2 * m)
                dve.tensor_copy(ktd[:, 1, :], PS[:, 5, :]).then_inc(d_dve, 1)
            for b in range(1, NB, 2):
                dve.wait_ge(d_ps, 96 + b + 1)
                dve.wait_ge(sc_ps, 32 if b == 1 else 32 + b - 1)
                dve.tensor_copy(ktd[:, 1, :], PS[:, 5, :]).then_inc(d_dve, 1)
            dve.wait_ge(bias_in, 16)
            dve.wait_ge(sc_ps, 32 + NB + 1)
            ds(dve.tensor_tensor(P_sel[:, 0:PAST], P_sel[:, 0:PAST], PS[0:NROW, 0:4, :].rearrange("p a n -> p (a n)"), ALU.add))
            ps4 = P_sel[:, 0:PAST].rearrange("p (l k f) -> p l k f", l=STRIDE, f=4)
            ds(dve.tensor_tensor(ps4, ps4, mb64.unsqueeze(1).unsqueeze(3).to_broadcast([NROW, STRIDE, NBLK_S - 1, 4]), ALU.add))
            ds(dve.tensor_copy(P_sel[:, PAST:NSEL], PS[0:NROW, 7, 0:1]))
            rs(dve.tensor_reduce(dsm[:, 1:2], P_sel, AX.X, ALU.max, negate=True))
            ds(dve.tensor_tensor(P_win[:, 0:WINDOW], P_win[:, 0:WINDOW], PS[0:NROW, 6, :], ALU.add))
            ds(dve.tensor_copy(P_win[:, WINDOW:NWIN], PS[0:NROW, 7, 1:2]))
            rs(dve.tensor_reduce(dsm[:, 2:3], P_win, AX.X, ALU.max, negate=True))
            dve.wait_ge(act_r, 3)
            ds(dve.reciprocal(dsm[:, 8:10], dsm[:, 4:6]))
            ds(dve.tensor_tensor(dsm[:, 10:12], dsm[:, 8:10], grow[:, 1:3], ALU.mult))
            ds(dve.tensor_scalar(P_sel, P_sel, dsm[:, 10:11], None, ALU.mult))
            ds(dve.tensor_scalar(P_win, P_win, dsm[:, 11:12], None, ALU.mult))
            ds(dve.tensor_scalar(pnew[:, 0, :], const("own", NROW), P_sel[:, PAST:NSEL], None, ALU.mult))
            rs(dve.tensor_scalar(pnew[:, 1, :], const("own", NROW), P_win[:, WINDOW:NWIN], None, ALU.mult))
            rs(dve.tensor_scalar(P_cmp, P_cmp, grow[:, 0:1], None, ALU.mult))
            dve.wait_ge(pe_r, 6)
            rs(dve.tensor_copy(ptdv[:, :, :], PS[:, 0:3, :].rearrange("p a n -> p (a n)")[:, 0:21 * NROW].rearrange(
                "p (a n) -> p a n", a=21)))
            rs(dve.tensor_copy(pnewT, PS[0:NB, 3, 0:2 * NROW].rearrange("p (s n) -> p s n", s=2)))
            dve.wait_ge(pe_r, 7)
            acc = PS[:, 4, 0:NROW].rearrange("p (b r) -> p b r", b=NB)
            for g in range(2):
                for r in range(4):
                    h = 4 * g + r
                    ins = dve.tensor_copy(aT[HD * (h % 2):HD * (h % 2 + 1), h // 2, SEQ:T], acc[HD * g:HD * (g + 1), :, h])
            dve.drain().then_inc(ph, 1)
            dve.wait_ge(ph, 6)
            hv = Steps(dve, hd)
            dve.wait_ge(small_in, 64)
            hv(dve.tensor_tensor(lbt[:, 2, :], lbt[:, 0, :], lbt[:, 1, :], ALU.max))
            hv(dve.tensor_tensor(lbt[:, 3, :], lbt[:, 0, :], lbt[:, 2, :], ALU.subtract))
            hv(dve.tensor_tensor(lbt[:, 4, :], lbt[:, 1, :], lbt[:, 2, :], ALU.subtract))
            dve.wait_ge(lb_act, 2)
            hv(dve.tensor_tensor(lbt[:, 5, :], lbt[:, 3, :], lbt[:, 4, :], ALU.add))
            hv(dve.reciprocal(lbt[:, 2, :], lbt[:, 5, :]))
            hv(dve.tensor_tensor(lbt[:, 0, :], lbt[:, 3, :], lbt[:, 2, :], ALU.mult))
            hv(dve.tensor_scalar(lbt[:, 1, :], lbt[:, 0, :], -1.0, 1.0, ALU.mult, ALU.add))
            hv(dve.memset(atm, 0.0))
            hv(dve.memset(qz, 0.0))
            hv(dve.memset(hsm[:, 95:96], LN_EPS))
            for t in range(NQ + 1):
                n = toks(t)
                dve.wait_ge(vt_ps, t + 1)
                dve.tensor_copy(vt[:, t, :] if t < NQ else vdec, PS[0:n, 5 + t % 3, :]).then_inc(vt_dve, 1)
            maskb = const("hgmask").bitcast(U32)

            def turned_out(h):
                for s in (9, 10):
                    i = wstep(h, s)
                    dve.wait_ge(w_ps, i + 1)
                    c0 = 512 * (s - 9)
                    dve.scalar_tensor_tensor(out=rT[:, h // 2, c0:c0 + 512], in0=PS[:, 5 + i % 3, :], scalar=ngt[:, 0:1],
                                             in1=gbs[:, h // 2, c0:c0 + 512], op0=ALU.mult, op1=ALU.mult
                                             ).then_inc(w_dve, 1)

            def prepare(h):
                par = h % 2
                dve.wait_ge(u_act, 3 * (U_H + 2 * h + 1))
                dve.tensor_scalar(fT[:, par, :], fT[:, par, :], lbt[:, 1, h:h + 1], lbt[:, 0, h:h + 1], ALU.mult, ALU.add
                                  ).then_inc(hf, 1)
                dve.wait_ge(hf, h + 1)
                if h >= 1:
                    dve.wait_ge(w_ps, wstep(h - 1, 3) + 1)
                hv(dve.tensor_scalar(kf, fT[:, par, :], -1.0, 1.0, ALU.mult, ALU.add))
                hv(dve.tensor_copy(dfk[:, 0, h, :], fT[:, par, SEQ:T]))
                hv(dve.tensor_copy(dfk[:, 1, h, :], kf[:, SEQ:T]))
                dve.wait_ge(hl, h + 1)
                dve.tensor_tensor_scan(lcb, const("fresh"), lfb, 0.0, ALU.mult, ALU.add).then_inc(hs, 1)
                dve.wait_ge(he, 2 * h + 2)
                dve.wait_ge(u_act, 3 * (U_H + 2 * h + 2))
                hv(dve.tensor_copy(dfk[:, 2, h, :], qT[:, par, SEQ:T]))
                hv(dve.tensor_tensor(qT[:, par, 0:SEQ], qT[:, par, 0:SEQ], lcb, ALU.mult))
                hv(dve.tensor_copy(dec, lcb[:, CH - 1:SEQ:CH]))
                hv(dve.tensor_tensor(kf[:, 0:SEQ], kf[:, 0:SEQ], lfb, ALU.mult))
                dve.tensor_tensor(lcb.rearrange("p (c i) -> p c i", c=NCH), kf[:, 0:SEQ].rearrange("p (c i) -> p c i", c=NCH),
                                  dec.unsqueeze(2).to_broadcast([P, NCH, CH]), ALU.mult).then_inc(hk, 1)
                dve.wait_ge(hk, h + 1)

            prepare(0)
            for h in range(HG):
                if h >= 1 and h % 2 == 0:
                    turned_out(h - 1)
                for s in (2, 3):
                    i = wstep(h, s)
                    dve.wait_ge(w_ps, i + 1)
                    for j in range(4):
                        ins = dve.copy_predicated(atm[:, 4 * (s - 2) + j, :], maskb, PS[:, 5 + i % 3, P * j:P * (j + 1)])
                    ins.then_inc(w_dve, 1)
                for c in range(NCH):
                    if c % 8 == 0:
                        dve.wait_ge(*copied(wstep(h, 4 + c // 8)))
                        if h >= 1 and c == 0:
                            dve.wait_ge(hg_out, 16 * h)
                    if c == 0:
                        ins = dve.tensor_copy(Sb[:, 0, :], Ub[:, 0, :])
                    else:
                        ins = dve.scalar_tensor_tensor(out=Sb[:, c, :], in0=Sb[:, c - 1, :], scalar=dec[:, c:c + 1],
                                                       in1=Ub[:, c, :], op0=ALU.mult, op1=ALU.add)
                    ins.then_inc(s_s, 1)
                    dve.wait_ge(s_s, NCH * h + c + 1)
                if h + 1 < HG:
                    prepare(h + 1)
                i = wstep(h, 8)
                dve.wait_ge(w_ps, i + 1)
                dve.tensor_copy(osb, PS[:, 5 + i % 3, :].rearrange("p (t v) -> p t v", t=NQ)).then_inc(w_dve, 1)
                dve.wait_ge(*copied(i))
                hv(dve.tensor_tensor(sqb, osb, osb, ALU.mult))
                dve.tensor_reduce(hsm[:, 0:8], sqb, AX.X, ALU.add).then_inc(lb_s, 1)
                dve.wait_ge(r_act, 2 * (h + 1))
                if h % 2 == 0 and h >= 2:
                    dve.wait_ge(w_ps, wstep(h - 1, 10) + 1)
                dve.tensor_tensor(onb[:, :, DV * (h % 2):DV * (h % 2 + 1)], osb,
                                  hsm[:, 16:24].unsqueeze(2).to_broadcast([P, NQ, DV]), ALU.mult).then_inc(on_s, 1)
                dve.wait_ge(on_s, h + 1)
            turned_out(HG - 1)
            dv = Steps(dve, dg_dve)
            for h in range(HG):
                dve.tensor_copy(qz[:, h, :, :].rearrange("p a b -> p (a b)")[:, 0:NB * NB:NB + 1], dfk[:, 2, h, :])
            dve.wait_ge(st_in, 16)
            for b in range(NB):
                dve.wait_ge(dg_ps, b + 1)
                dv(dve.tensor_tensor(sqb, PS[:, 5 + b % 3, :].rearrange("p (h v) -> p h v", h=HG),
                                     dfk[:, 1, :, b:b + 1].to_broadcast([P, HG, DV]), ALU.mult))
                dv(dve.tensor_tensor(stt[:, b, :, :], stt[:, b, :, :],
                                     dfk[:, 0, :, b:b + 1].to_broadcast([P, HG, DV]), ALU.mult))
                dv(dve.tensor_tensor(stt[:, b, :, :], stt[:, b, :, :], sqb, ALU.add))
            dve.wait_ge(dg_ps, NB + 1)
            dv(dve.tensor_copy(osb[0:NB], PS[0:NB, 5, :].rearrange("p (t v) -> p t v", t=HG)))
            dv(dve.tensor_tensor(sqb[0:NB], osb[0:NB], osb[0:NB], ALU.mult))
            dv(dve.tensor_reduce(hsm[0:NB, 0:8], sqb[0:NB], AX.X, ALU.add))
            dve.wait_ge(r_act, 2 * HG + 2)
            dve.wait_ge(w_ps, len(wsteps))
            dv(dve.tensor_tensor(onb[0:NB, 0:4, :].rearrange("p a b -> p (a b)").rearrange("p (h v) -> p h v", h=HG), osb[0:NB],
                                 hsm[0:NB, 16:24].unsqueeze(2).to_broadcast([NB, HG, DV]), ALU.mult))
            dve.wait_ge(dg_ps, NB + 2)
            for j in range(4):
                dve.scalar_tensor_tensor(out=rT[:, j, SEQ:T], in0=PS[:, 6, NB * j:NB * (j + 1)], scalar=ngt[:, 0:1],
                                         in1=gbs[:, j, SEQ:T], op0=ALU.mult, op1=ALU.mult)
            dve.drain().then_inc(ph, 1)
            dve.wait_ge(ph, 9)
            ms = Steps(dve, me_s)
            ms(dve.memset(epsb, LN_EPS))

            def x_low(k):
                dve.wait_ge(xh_act, k + 1)
                dve.tensor_tensor(xl[:, k, :], xT[:, k, :], xhM[:, k, :].bitcast(F32), ALU.subtract).then_inc(xl_dve, 1)

            x_low(0)
            for ab in range(2):
                split_low(dve, U_M + ab, SPLITS_M + ab, whM[:, ab])
            for k in range(1, KD):
                x_low(k)
            for s in range(NM):
                i, ci = s // 3, s % 3
                c0, cn = CHUNKS[ci]
                if ci == 1 and i + 1 < KD:
                    for ab in range(2):
                        split_low(dve, U_M + 3 * (i + 1) + ab, SPLITS_M + 2 * (i + 1) + ab, whM[:, 2 * ((i + 1) % 2) + ab])
                dve.wait_ge(m_act, 2 * s + 2)
                dve.wait_ge(g_ps, 4 * s + 4)
                for ab in range(2):
                    ms(dve.tensor_tensor(sgb[:, s % 2, ab, 0:cn], sgb[:, s % 2, ab, 0:cn], PS[:, 4 * (s % 2) + 2 + ab, 0:cn],
                                         ALU.mult))
                dve.tensor_tensor(mT[:, i, c0:c0 + cn], sgb[:, s % 2, 0, 0:cn], sgb[:, s % 2, 1, 0:cn], ALU.add
                                  ).then_inc(m_dve2, 1)
            lc = Steps(dve, ln_c)

            def norm(t, lnum, done):
                n = toks(t)
                y = x1[0:n, t, :]
                lc(dve.bn_stats(stats[0:n, 0, :], y[:, 0:512]))
                lc(dve.bn_stats(stats[0:n, 1, :], y[:, 512:D]))
                dve.bn_aggr(mv[0:n, :], stats[0:n, :, :]).then_inc(ln_v, 1)
                k = (NQ + 1) * lnum + t + 1
                dve.wait_ge(ln_r, 2 * k)
                lc(dve.tensor_scalar(y, y, mv[0:n, 0:1], rstd[0:n, 1:2], ALU.subtract, ALU.mult))
                lc(dve.tensor_tensor(y, y, lng[0:n, 0, :], ALU.mult))
                dve.tensor_tensor(y, y, lng[0:n, 1, :], ALU.add).then_inc(done, 1)

            def x1_low(t):
                for half in range(2):
                    dve.wait_ge(xt1_act, 2 * t + half + 1)
                    at = (slice(None), slice(4 * half, 4 * half + 4), slice(P * t, P * t + toks(t)))
                    dve.tensor_tensor(xl[at], PS[:, 4 + 2 * (t % 2) + half, :].rearrange("p (j n) -> p j n", j=4)[:, :, 0:toks(t)],
                                      x1h[at].bitcast(F32), ALU.subtract).then_inc(x1l_dve, 1)

            dve.wait_ge(ln_in, 32)
            for t in range(NQ + 1):
                n = toks(t)
                dve.wait_ge(f_ps, t + 1)
                dve.wait_ge(xr_in[t % 2], 16 * (t // 2 + 1))
                dve.scalar_tensor_tensor(out=x1[0:n, t, :], in0=xr[0:n, t % 2, :], scalar=ALPHA,
                                         in1=PS[0:n, 2 * (t % 2):2 * (t % 2) + 2, :].rearrange("p a n -> p (a n)"),
                                         op0=ALU.mult, op1=ALU.add).then_inc(f_dve, 1)
                dve.wait_ge(f_dve, t + 1)
                norm(t, 0, x1_s)
                if t >= 1:
                    m = toks(t - 1)
                    x1_low(t - 1)
                    dve.tensor_scalar(x1[0:m, t - 1, :], x1[0:m, t - 1, :], ALPHA, None, ALU.mult).then_inc(x1_sc, 1)
            x1_low(NQ)
            dve.wait_ge(x1_s, NQ + 1)
            dve.tensor_scalar(x1[0:NB, NQ, :], x1[0:NB, NQ, :], ALPHA, None, ALU.mult).then_inc(x1_sc, 1)
            dve.wait_ge(x1_sc, NQ + 1)
            dve.wait_ge(ln2_in, 32)
            for i in range(2):
                split_low(dve, U_U + i, SPLITS_U + i, whM[:, i])

            def hidden(i):
                g, n = i // 2, U_U + i
                u = uT[g % 2][:, i % 2]
                dve.wait_ge(relu_act, 3 * (i + 1))
                dve.tensor_tensor(u[:, 0, :], u[:, 0, :], u[:, 0, :], ALU.mult).then_inc(sq_dve, 1)
                dve.wait_ge(uh_act, i + 1)
                dve.tensor_tensor(uR[g % 2][:, i % 2, 0, :], u[:, 0, :], uR[g % 2][:, i % 2, 1, :].bitcast(F32), ALU.subtract).then_inc(ul_dve, 1)
                if i + 2 < F_FF // P:
                    split_low(dve, n + 2, SPLITS_U + i + 2, whM[:, i % 2])

            for g in range(NG + 1):
                if g < NG:
                    hidden(2 * g)
                    hidden(2 * g + 1)
                if g >= 1:
                    for t in range(NQ + 1):
                        n = toks(t)
                        for half in range(2):
                            d = 18 * (g - 1) + 2 * t + half
                            dve.wait_ge(dn_ps, d + 1)
                            if g > 1:
                                dve.wait_ge(dn_dve, d - 17)
                            y = x1[0:n, t, 512 * half:512 * (half + 1)]
                            dve.tensor_tensor(y, y, PS[0:n, 5 + d % 3, :], ALU.add).then_inc(dn_dve, 1)
                        if g == NG:
                            dve.wait_ge(dn_dve, d + 1)
                            norm(t, 1, y_s)
                            dve.wait_ge(y_s, t + 1)
                if g < NG:
                    dve.wait_ge(wdh_act, g + 1)
                    dve.tensor_tensor(wdl[:, g % 2], wdn[:, g % 2], wdh[:, :, :].bitcast(F32), ALU.subtract
                                      ).then_inc(wdl_dve, 1)

        @block.gpsimd
        def _(pool):
            pool.wait_ge(u_ps, 3 * NU_ATT)
            pool.wait_ge(xt_dve, 2 * (NQ + 1))
            for k in range(5, KD):
                pool.tensor_tensor(xT[:, k, :], xl[:, k, :].bitcast(F32), xhA[:, k, :].bitcast(F32), ALU.add).then_inc(x_pool, 1)
            pool.wait_ge(ix_s, 2)
            for n in range(32):
                src = (c_cmp if n < 16 else c_sel)[0].rearrange("n (r l) c g d -> (n r) (l c g d)", l=8)
                b, half = (n % 16) // 2, n % 2
                if n >= 2:
                    pool.wait_ge(d_ps, 4 * (n - 1) if n <= 17 else 64 + 2 * (n - 17))
                if n >= 18:
                    pool.wait_ge(v_s, n - 17)
                pool.indirect_dma_start(out=raw[:, n % 2, :], out_offset=None, in_=src,
                                        in_offset=bass.IndirectOffsetOnAxis(ap=idx[:, half, b:b + 1], axis=0)
                                        ).then_inc(raw_in[n % 2], 16)
                if n >= 17:
                    m = n - 17
                    pool.wait_ge(raw_in[(m + 16) % 2], 16 * ((m + 16) // 2 + 1))
                    if m == 0:
                        pool.wait_ge(vc_s, NB)
                    pool.tensor_copy(vall[:, m // 2, 8 * (m % 2):8 * (m % 2) + 8, :],
                                     raw[:, m % 2, :].rearrange("p (l c) -> p l c", l=8)[:, :, P:2 * P]).then_inc(v_s, 1)
            m = 15
            pool.wait_ge(raw_in[1], 16 * 16)
            pool.tensor_copy(vall[:, m // 2, 8 * (m % 2):8 * (m % 2) + 8, :],
                             raw[:, m % 2, :].rearrange("p (l c) -> p l c", l=8)[:, :, P:2 * P]).then_inc(v_s, 1)
            pool.wait_ge(ph, 6)
            pool.memset(vbd, 0.0).then_inc(zd, 1)
            pool.wait_ge(zd, 1)
            pool.wait_ge(vt_dve, NQ + 1)
            for h in range(HG + 1):
                if h < HG:
                    if h >= 1:
                        pool.wait_ge(w_ps, wstep(h - 1, 7) + 1)
                    for j in range(4):
                        pool.tensor_copy(vbd[CH * j:CH * (j + 1), :, j, :],
                                         vt[CH * j:CH * (j + 1), :, DV * h:DV * (h + 1)]).then_inc(vb_s, 1)
                if h >= 1:
                    pool.wait_ge(s_s, NCH * h)
                    pool.dma_start(hg_p[0, 0, h - 1], Sb[:, NCH - 1, :]).then_inc(hg_out, 16)


_INS = ['x_prompt', 'x_sample', 'cache_cmp_kv', 'cache_sel_kv', 'cache_win_kv', 'state_hgrn', 'page_table', 'w_in',
        'cmp_w', 'cmp_pos', 'hgrn_lb_logits', 'hgrn_norm_g', 'w_br_a', 'w_br_b', 'w_out', 'ln1_g', 'ln1_b', 'w_up',
        'w_down', 'ln2_g', 'ln2_b']
_KV = (2, GROUPS, HD)
_OUTS = [(1, SEQ, D), (NB, 1, D), (1, 1, SEQ) + _KV, (1, 1, SEQ) + _KV, (1, 1, WINDOW) + _KV, (1, 1, HG, P, DV),
         (1, NB, 1) + _KV, (1, NB, 1) + _KV, (1, NB, WINDOW) + _KV, (1, NB, HG, P, DV)]


def kernel(**inputs):
    import concourse.bacc as _bacc
    from concourse.bass_utils import run_bass_kernel_spmd as _run

    nc = _bacc.Bacc("TRN2", target_bir_lowering=False, num_devices=1)
    arrays, args = {}, []
    given = {name: np.ascontiguousarray(inputs[name]) for name in _INS}
    given["consts"], given["kpos"], given["dbias"] = constants(), positions(), decode_biases()
    for name, a in given.items():
        arrays[f"in_{name}"] = a
        args.append(nc.dram_tensor(f"in_{name}", a.shape, mybir.dt.from_np(a.dtype), kind="ExternalInput").ap())
    for i, shape in enumerate(_OUTS):
        args.append(nc.dram_tensor(f"out_{i}", shape, F32, kind="ExternalOutput").ap())
    hybrid_step(nc, *args)
    r = _run(nc, [arrays], core_ids=[0])
    return tuple(r.results[0][f"out_{i}"] for i in range(len(_OUTS)))
```

```python
from contextlib import ExitStack

import numpy as np

import concourse.bass as bass
from concourse import mybir

F32 = mybir.dt.float32
F32R = mybir.dt.float32r
BF16 = mybir.dt.bfloat16
I32 = mybir.dt.int32
U32 = mybir.dt.uint32
ALU = mybir.AluOpType
ACT = mybir.ActivationFunctionType
AX = mybir.AxisListType

P = 128
D = 1024
KD = D // P
SEQ = 1024
NQ = SEQ // P
NB = 8
T = SEQ + NB
HD = 64
GROUPS = 2
PAGES = 16
PAST = 2048
STRIDE = 16
NCMP_P = SEQ // STRIDE
NCMP_S = PAST // STRIDE
CMP_LEN = 32
WINDOW = 512
SEL_BLOCK = 64
N_SELECT = 16
NBLK_S = PAST // SEL_BLOCK + 1
HG = 8
DV = 64
CH = 32
NCH = SEQ // CH
F_FF = 4096
NEG = -1e30
FORCE = 1e6
LN_EPS = 1e-5
ALPHA = 2.0 ** 0.25
NROW = NB * 8

C_QA, C_GLA, C_QB = 0, 1280, 1304
C_FB, C_IB, C_GB, C_MG = C_QB + 1024, C_QB + 2048, C_QB + 2560, C_QB + 3072

CONSTS = {}


def constants():
    parts = {}

    def put(name, a):
        full = np.zeros((P, int(np.prod(a.shape[1:]))), np.float32)
        full[:a.shape[0]] = a.reshape(a.shape[0], -1)
        parts[name] = full

    p = np.arange(P)
    put("ident", np.eye(P))
    put("causal", np.where(p[None, :] <= p[:, None], 0.0, NEG))
    put("winlow", np.where(p[None, :] > p[:, None], 0.0, NEG))
    n = np.arange(NCMP_P)
    end = STRIDE * n + CMP_LEN - 1
    pos = P * np.arange(NQ)[None, :, None] + p[:, None, None]
    put("cmpmask", np.where((n < NCMP_P - 1) & (end <= pos), 0.0, NEG))
    put("hgmask", ((p[:, None] // CH == p[None, :] // CH) & (p[:, None] <= p[None, :])).astype(np.float32))
    put("fresh", np.broadcast_to((np.arange(SEQ) % CH != 0).astype(np.float32), (P, SEQ)))
    row = np.arange(NROW)
    put("gsum", (row[:, None] // 4 == np.arange(16)[None, :]).astype(np.float32))
    put("gspread", (row[None, :] // 4 == np.arange(16)[:, None]).astype(np.float32))
    b = np.arange(NBLK_S)
    forced = (b == 0) | (b == NBLK_S - 1) | (b == NBLK_S - 2)
    put("free", np.broadcast_to(np.where(forced, 0.0, 1.0), (16, NBLK_S)))
    put("forced", np.broadcast_to(np.where(forced, FORCE, 0.0), (16, NBLK_S)))
    put("ownT", (row[None, :] // 8 == np.arange(NB)[:, None]).astype(np.float32))
    put("headsel", (row[:, None] % 8 == np.arange(8)[None, :]).astype(np.float32))
    put("pagespread", (p[None, :] // 8 == np.arange(PAGES)[:, None]).astype(np.float32))
    put("own", (row[:, None] // 8 == np.arange(NB)[None, :]).astype(np.float32))
    put("rowb", np.repeat(np.eye(NB)[:, :, None], P, axis=2))
    put("half", np.stack([2.0 * (p % 8), 2.0 * (p % 8) + 1], axis=1))
    at, out = 0, []
    for name, a in parts.items():
        CONSTS[name] = (at, a.shape[1])
        at += a.shape[1]
        out.append(a)
    return np.concatenate(out, axis=1)


def positions():
    end = STRIDE * np.arange(NCMP_P) + CMP_LEN - 1
    return np.concatenate([np.arange(SEQ), end, end]).astype(np.float32)[None, :]


def block_order():
    b = np.arange(NBLK_S)
    return np.ascontiguousarray(np.broadcast_to(b[None, None, :] < b[None, :, None], (16, NBLK_S, NBLK_S)), np.float32)


def decode_biases():
    slope = 2.0 ** -(np.arange(NROW) % 8 + 1.0)
    l, c = np.arange(STRIDE), np.arange(NCMP_S)
    sel = slope[:, None, None] * (STRIDE * c[None, None, :] + l[None, :, None] - PAST)
    wpos = PAST - WINDOW + 4 * np.arange(P)[None, None, :] + np.arange(4)[None, :, None]
    win = np.where(PAST - wpos < WINDOW, slope[:, None, None] * (wpos - PAST), NEG)
    cmp = np.where(c < NCMP_S - 1, slope[:, None] * (STRIDE * c + CMP_LEN - 1 - PAST), NEG)
    zero = np.zeros((NROW, 1))
    return np.concatenate([sel.reshape(NROW, -1), zero, win.reshape(NROW, -1), zero, cmp], axis=1).astype(np.float32)


class Steps:

    def __init__(self, eng, sem):
        self.eng, self.sem, self.n = eng, sem, 0

    def __call__(self, ins):
        ins.then_inc(self.sem, 1)
        self.n += 1
        self.eng.wait_ge(self.sem, self.n)


def hybrid_step(nc, x_p, x_s, c_cmp, c_sel, c_win, state, table, w_in, cmp_w, cmp_pos, lb_logits, norm_g,
                w_br_a, w_br_b, w_out, ln1_g, ln1_b, w_up, w_down, ln2_g, ln2_b, consts, kpos, dbias, before_d,
                y_p, y_s_out, cmp_p, sel_p, win_p, hg_p, cmp_s, sel_s, win_s, hg_s):
    with ExitStack() as ctx:
        def sb(name, shape, dt=F32):
            return ctx.enter_context(nc.sbuf_tensor(name, shape, dt))

        def sem(name):
            return ctx.enter_context(nc.semaphore(name))

        NC_ = consts.shape[1]
        K = sb("consts_sb", [P, NC_])

        def const(name, rows=P):
            at, n = CONSTS[name]
            return K[0:rows, at:at + n]

        ident = const("ident")
        at, n = CONSTS["cmpmask"]
        masks = sb("masks", [P, at + n], BF16)

        def mask(name, i=0, n=P):
            at = CONSTS[name][0] + i * n
            return masks[:, at:at + n]

        xT_at = (nc.sbuf_base + 31) // 32 * 32
        xT = sb("xT", [P, KD, T])
        aT_at = (nc.sbuf_base + 31) // 32 * 32
        aT = sb("aT", [P, 4, T])
        WR = 4
        wring_at = (nc.sbuf_base + 31) // 32 * 32
        wring = sb("wring", [P, WR, KD, P])
        ARENA = 32200
        arena_at = (nc.sbuf_base + 31) // 32 * 32
        arena = sb("arena", [P, ARENA])
        PS = ctx.enter_context(nc.psum_tensor("PS", [P, 8, 512], F32))

        def rounded(name, base, at, *dims):
            assert base + 4 * (at + int(np.prod(dims))) <= arena_at + 4 * ARENA
            return nc.alloc_sbuf_tensor_at(name, [P, *dims], F32R, offset=base + 4 * at)

        def view(at, *dims, rows=P):
            n = int(np.prod(dims))
            assert at + n <= ARENA, (at, n)
            v = arena[0:rows, at:at + n]
            names = "abcd"[:len(dims)]
            if len(dims) > 1:
                v = v.rearrange(f"p ({' '.join(names)}) -> p {' '.join(names)}",
                                **{names[i]: dims[i] for i in range(1, len(dims))})
            return v

        o = 0
        gates = view(o, NQ + 1, 24); o += (NQ + 1) * 24
        cw2 = view(o, 2, 8, P); o += 2 * 8 * P
        cpos = view(o, 2, 16); o += 32
        cb = view(o, 2, rows=HD); o += 2
        small = view(o, 64); o += 64
        kvd = view(o, 768, rows=NB); o += 768
        qbd = view(o, NB, NROW); o += NB * NROW
        knew = view(o, 2, NB); o += 2 * NB
        o_kept = o = (o + 7) // 8 * 8
        hA = view(o, 10, T); o += 10 * T
        kvtok = view(o, NQ, 768); o += NQ * 768
        o_kc = o; o += 2 * NCMP_P
        vcN = view(o, 2, HD, rows=NCMP_P); o += 2 * HD
        o_k = o; o += 4 * SEQ
        hG = view(o, T, rows=24)
        cmpT = view(o, 4, NCMP_P, rows=HD)
        cmpK = view(o + 256, 4, NCMP_P, rows=HD)
        posrow = arena[64:65, o:o + SEQ + 2 * NCMP_P]
        PT = [view(o, 2, 512)]
        o += SEQ + 2 * NCMP_P
        o_q = o; o += 2 * SEQ
        cw64 = view(o, 2, STRIDE, P)
        xs = view(o + SEQ, 3, D)
        PT += [view(o, 2, 512)]; o += SEQ
        o_q1 = o; o += SEQ
        pr = view(o, 2, SEQ); o += 2 * SEQ
        o_kvtok = o_kept + 10 * T
        xhA = rounded("x_high_att", arena_at, o_kvtok, KD, T)
        xl = rounded("x_low", xT_at, 0, KD, T)
        whA = rounded("w_high_att", arena_at, o_kvtok + KD * T, 2, KD, P)
        wl = rounded("w_low", wring_at, 0, WR, KD, P)
        k1 = rounded("k_high_twice", arena_at, o_k, 2, 2, SEQ)
        k2 = [[rounded(f"k_low{br}{g}", arena_at, o_kept + tile * T, SEQ) for g, tile in enumerate(tiles)]
              for br, tiles in enumerate(((7, 4), (9, 5)))]
        kc1 = rounded("kc_high_twice", arena_at, o_kc, 2, NCMP_P)
        kc2 = rounded("kc_low", arena_at, o, 2, NCMP_P)
        q1 = [rounded("q_high_low0", arena_at, o_q, SEQ), rounded("q_high_low1", arena_at, o_q1, SEQ)]
        q2 = [rounded("q_high0", arena_at, o_q + SEQ, SEQ), rounded("q_high1", arena_at, o_kept + 6 * T, SEQ)]

        ph = sem("phase_done")
        c_in, mk_act = sem("consts_loaded"), sem("masks_ready")
        x_in = [sem(f"x_in{i}") for i in range(3)]
        xt_ps, xt_act, xt_dve = sem("xt_turned"), sem("xt_copied_act"), sem("xt_copied_dve")
        w_in_s = [sem(f"w_loaded{i}") for i in range(WR)]
        u_ps, u_act = sem("unit_chunk_ready"), sem("unit_chunk_copied")
        wh_act, wl_dve = sem("weight_high_parts"), sem("weight_low_parts")
        x_dve, x_pool = sem("x_whole_again_dve"), sem("x_whole_again_pool")
        kt_ps, kt_dve = sem("kv_turned"), sem("kv_copied")
        kv_out, shift_out = sem("kv_stored"), sem("window_shifted")
        cw_in = sem("cmp_weights_loaded")
        cp_ps, cp_act, cp_dve = sem("cmp_parts_ready"), sem("cmp_copied_act"), sem("cmp_steps_dve")
        kc_act, kc_dve = sem("compressed_k_high"), sem("compressed_k_low")
        ka_act, ka_dve, ka_pool, pos_in = sem("k_high_staged"), sem("k_low_staged"), sem("positions_staged"), sem("positions_loaded")
        q_s, ss_ps, e_act, m_dve, p_dve, q_row = (sem("q_staged"), sem("scores_ready"), sem("exp_done"), sem("max_done"),
                                      sem("probs_scaled"), sem("slope_row_set"))
        dch = sem("dve_steps")
        t_ps, t_act, t_dve, pv_ps, o_act = (sem("probs_turned"), sem("probs_copied_act"), sem("probs_copied_dve"),
                                            sem("pv_groups_done"), sem("attn_out_copied"))

        def toks(t):
            return P if t < NQ else NB

        wv = w_in[0].rearrange("(k p) c -> p k c", p=P)
        wv = (wv[:, 0:4], wv[:, 4:8])
        units = [(wv, C_QA + P * i, P, hA[:, i, :], ACT.Copy) for i in range(10)]
        units += [(wv, C_GLA, 24, hG, ACT.Sigmoid)]
        NU_ATT = len(units)
        CHUNKS = [(T // 3 * i, T // 3) for i in range(3)]

        def unit_out(x, m, cn):
            return PS[0:m, x % 5, 0:cn]

        heads = [(h, i) for h in range(8) for i in range(NQ)]
        NJ = 2 * len(heads)

        def job(j):
            h, i = heads[j // 2]
            return h, i, j % 2

        def blocks(j):
            h, i, wc = job(j)
            if not wc:
                return [(0, P * b, P, P * b) for b in range(i + 1)]
            lo = max(0, i - 4)
            return [(1, P * b, P, P * (b - lo)) for b in range(lo, i + 1)] + [(2, 0, NCMP_P, 640)]

        def groups(j):
            bl = blocks(j)
            return [bl[:4]] + ([bl[4:]] if len(bl) > 4 else [])

        first_group = [0]
        second_groups = [0]
        for j in range(NJ):
            first_group.append(first_group[-1] + len(groups(j)))
            second_groups.append(second_groups[-1] + len(groups(j)) - 1)

        def evacuations(gr):
            full = sum(n == P for _, _, n, _ in gr)
            return [(P, 0, P * full)] * (full > 0) + [(NCMP_P, P * full, P * (full + 1))] * (full < len(gr))

        def exps(j):
            return 3 * (j // 2) + (1 if j % 2 == 0 else 3)

        NSEL, NWIN = PAST + 1, WINDOW + 1
        o = o_kept
        raw = view(o, 2, 8 * 256); o += 2 * 8 * 256
        raww = view(o - 4096, NB, 4, P)
        ktd = view(o, 2, 512); o += 1024
        Prow = view(o, NSEL + NWIN + NCMP_S, rows=NROW)
        rk1 = view(o, NBLK_S, NBLK_S, rows=16)
        rk2 = view(o + NBLK_S * NBLK_S, NBLK_S, NBLK_S, rows=16)
        o += NSEL + NWIN + NCMP_S
        P_sel, P_win, P_cmp = Prow[:, 0:NSEL], Prow[:, NSEL:NSEL + NWIN], Prow[:, NSEL + NWIN:]
        cmpbias = view(o, NCMP_S, rows=NROW); o += NCMP_S
        kcd = view(o, NB, NCMP_S); o += NB * NCMP_S
        vcd = view(o, NB, P); o += NB * P
        g64 = view(o, 24, rows=NROW); o += 24
        grow = view(o, 4, rows=NROW); o += 4
        idx = view(o, 2, NB).bitcast(U32); o += 16
        tabi = view(o, NB, rows=PAGES).bitcast(I32); o += NB
        tabf = view(o, NB, rows=PAGES); o += NB
        dsm = view(o, 32, rows=NROW); o += 32
        blkm = view(o, 4, NBLK_S, rows=16); o += 4 * NBLK_S
        mb64 = view(o, NBLK_S - 1, rows=NROW); o += NBLK_S - 1
        pnew = view(o, 2, NB, rows=NROW); o += 16
        pnewT = view(o, 2, NROW, rows=NB); o += 128
        xt2 = view(o, 2, 2048)
        tmp1 = view(o + 4096, 2, 2, NCMP_S, rows=HD)
        vct = view(o + 4608, 2, NCMP_S)
        vall = view(o, NB, STRIDE, P)
        o += NB * STRIDE * P
        ptdv = view(o, 21, NROW)
        before = view(o, NBLK_S, NBLK_S, rows=16)
        acc8 = view(o_kept + 4096, 2, P)
        pv8_ps, pv8_dve = sem("decode_out_ready"), sem("decode_out_copied")
        tb_in, ix_s = sem("table_loaded"), sem("row_index_ready")
        raw_in = [sem(f"pages_loaded{i}") for i in range(2)]
        cx_act, cx_dve = sem("chunks_copied_act"), sem("chunks_copied_dve")

        def xt_of(n, c, par, g):
            return xt2[HD * par:HD * (par + 1), n % 2, 1024 * c:1024 * (c + 1)].rearrange(
                "p (q g n) -> p q g n", q=4, g=2)[:, :, g, :]

        d_ps, d_act, d_dve = sem("turned_pages"), sem("turned_copied_act"), sem("turned_copied_dve")
        dc_ps, kv_a, kv_d = sem("cmp_products"), sem("cmp_part1_copied"), sem("cmp_blocks_built")
        vc_ps, vc_s = sem("cmp_v_turned"), sem("cmp_v_copied")
        pe_r, act_r, dve_r, v_s = (sem("pe_results"), sem("act_results"), sem("dve_results"), sem("v_copied"))
        bias_in, rank_s, wv_in = sem("bias_loaded"), sem("rank_done"), sem("window_v_loaded")
        wraw_in = [sem(f"window_loaded{i}") for i in range(2)]
        sc_ps, dst2 = sem("decode_scores"), sem("decode_steps")
        o = 0
        rT = view(o, 4, T); o += 4 * T
        gbs = view(o, 4, T); o += 4 * T
        vt = view(o, NQ, 512); o += NQ * 512
        vdec = view(o, 512, rows=NB); o += 512
        fT = view(o, 2, T); o += 2 * T
        qT = view(o, 2, T); o += 2 * T
        stt = view(o, NB, HG, DV)
        kf = view(o, T); o += T
        lfb = view(o, SEQ); o += SEQ
        lcb = view(o, SEQ); o += SEQ
        kkt = view(o, NQ, P); o += NQ * P
        atm = view(o, NQ, P); o += NQ * P
        ibT = view(o, 4, T)
        Ub = view(o, NCH, DV); o += NCH * DV
        Sb = view(o, NCH, DV); o += NCH * DV
        o += 32
        vbd = view(o, NQ, 4, DV); o += NQ * 4 * DV
        onb = view(o, NQ, P); o += NQ * P
        osb = view(o, NQ, DV); o += NQ * DV
        sqb = view(o, NQ, DV); o += NQ * DV
        dec = view(o, NCH); o += NCH
        hsm = view(o, 96); o += 96
        lbt = view(o, 6, HG); o += 6 * HG
        ngt = view(o, 1); o += 1
        dfk = view(o, 3, HG, NB); o += 3 * HG * NB
        qz = view(o, HG, NB, NB); o += HG * NB * NB
        units += [(wv, C_IB + P * i, P, ibT[:, i, :], ACT.Copy) for i in range(4)]
        units += [(wv, C_GB + P * i, P, gbs[:, i, :], ACT.Silu) for i in range(4)]
        for h in range(HG):
            units += [(wv, C_FB + P * h, P, fT[:, h % 2, :], ACT.Sigmoid), (wv, C_QB + P * h, P, qT[:, h % 2, :], ACT.Copy)]
        U_IB, U_H = NU_ATT, NU_ATT + 8
        small_in = sem("hgrn_small_loaded")
        vt_ps, vt_dve = sem("v_turned"), sem("v_tokens_copied")
        hf, hl, hs, he, hk = (sem("forget_ready"), sem("log_done"), sem("cumulated"), sem("decay_exp_done"), sem("keys_ready"))
        w_ps, w_act, w_dve = sem("hgrn_products"), sem("hgrn_copied_act"), sem("hgrn_copied_dve")
        vb_s, s_s, r_act, on_s = sem("v_diagonal_set"), sem("states_done"), sem("rms_done"), sem("normed_out")
        hd, lb_act, lb_s = sem("hgrn_dve_steps"), sem("lb_exp_done"), sem("rms_sum_done")
        st_in, hg_out = sem("states_loaded"), sem("states_stored")
        hgs_out = sem("decode_states_stored")
        zd = sem("diagonal_cleared")
        dg_ps, dg_dve = sem("decode_v_spread"), sem("decode_state_steps")

        BY_ACT = (0, 1, 4, 5, 6, 7)

        def wstep(h, s):
            return 20 * (h // 2) + 9 * (h % 2) + s

        wsteps = [(h, s) for h in range(HG) for s in range(11 if h % 2 else 9)]
        for i, (h, s) in enumerate(wsteps):
            assert wstep(h, s) == i

        def copied(i):
            mine = wsteps[i][1] in BY_ACT
            return (w_act if mine else w_dve), sum((s in BY_ACT) == mine for _, s in wsteps[:i + 1])

        xr = view(0, 2, D)
        mT = view(4 * T, KD, T)
        x1h = rounded("x1_high", arena_at, 4 * T, KD, T)
        o = 4 * T + KD * T
        whM = rounded("w_high_mlp", arena_at, o, 4, KD, P)
        wo = view(o, KD, D)
        wdn = view(o + 2 * KD * P, 2, 2, D)
        wdl = rounded("w_down_low", arena_at, o + 2 * KD * P, 2, 2, D)
        wdh = rounded("w_down_high", arena_at, o + 2 * KD * P + 4 * D, 2, D)
        o += KD * D
        xhM = rounded("x_high_merge", arena_at, o, KD, T)
        sgb = view(o + KD * T, 2, 2, 512)
        x1 = view(o, NQ + 1, D)
        o += (NQ + 1) * D
        lng = view(o, 2, D); o += 2 * D
        o = max(o, 12 * T + KD * D + KD * T + 4 * 512)
        stats = view(o, 2, 6); o += 12
        mv = view(o, 2); o += 2
        rstd = view(o, 2); o += 2
        epsb = view(o, 1); o += 1
        stats2 = view(o, NQ + 1, 2, 6); o += (NQ + 1) * 12
        mv2 = view(o, NQ + 1, 3); o += (NQ + 1) * 3
        rstd2 = view(o, NQ + 1, 3); o += (NQ + 1) * 3
        uT = [aT[:, :, :].rearrange("p (j s) t -> p j s t", s=2), view(0, 2, 2, T)]
        uR = [rounded("hidden0", aT_at, 0, 2, 2, T), rounded("hidden1", arena_at, 0, 2, 2, T)]
        NG = F_FF // (2 * P)
        U_M = len(units)
        wbr = tuple(w[0].rearrange("(k p) c -> p k c", p=P) for w in (w_br_a, w_br_b))
        for i in range(KD):
            units += [(wv, C_MG + P * i, P, None, None), (wv, C_MG + D + P * i, P, None, None),
                      (wbr, P * i, P, None, None)]
        U_U = len(units)
        wupv = w_up[0].rearrange("(k p) c -> p k c", p=P)
        wupv = (wupv[:, 0:4], wupv[:, 4:8])
        for i in range(F_FF // P):
            units += [(wupv, P * i, P, None, None)]
        NM = 3 * KD
        wo_in, g_ps, m_act, m_dve2 = [sem(f"w_out_loaded{i}") for i in range(2)], sem("merge_products"), sem("merge_gates"), sem("merged")
        xh_act, xl_dve = sem("x_high_parts"), sem("x_low_parts")
        me_s = sem("merge_dve_steps")
        ln_in, ln2_in = sem("ln1_loaded"), sem("ln2_loaded")
        xr_in = [sem(f"x_again{i}") for i in range(2)]
        f_ps, f_dve, ln_v, ln_r, ln_c = (sem("mix_ready"), sem("residual_done"), sem("variance_ready"), sem("rstd_ready"),
                                         sem("ln_steps"))
        x1_s, xt1_ps, xt1_act, x1_sc = sem("x1_ready"), sem("x1_turned"), sem("x1_copied"), sem("x1_scaled")
        x1l_dve = sem("x1_low_parts")
        wd_in, wdh_act, wdl_dve = [sem(f"w_down{i}") for i in range(2)], sem("w_down_high"), sem("w_down_low")
        relu_act, sq_dve, uh_act, ul_dve = sem("relu_done"), sem("squared"), sem("hidden_high"), sem("hidden_low")
        dn_ps, dn_dve = sem("mlp_out"), sem("mlp_added")
        y_s, y_out = sem("y_ready"), sem("y_stored")
        l2_v, l2_r, l2_n, l2_g = sem("ln2_variance"), sem("ln2_rstd"), sem("ln2_normed"), sem("ln2_gained")

        def unit_done(n):
            if n < U_M:
                return u_ps, 3 * (n + 1)
            if n < U_U:
                i, part = (n - U_M) // 3, (n - U_M) % 3
                return g_ps, 4 * (3 * i + 2) + (1, 2, 4)[part]
            return u_ps, 3 * (n + 1 - (U_U - U_M))

        SPLITS_M, SPLITS_U = NU_ATT, NU_ATT + 2 * KD

        block = ctx.enter_context(nc.Block())

        @block.sync
        def _(sp):
            def load_unit(n):
                v, c, m, _, _ = units[n]
                if n >= WR:
                    sp.wait_ge(*unit_done(n - WR))
                for half in range(2):
                    sp.dma_start(wring[:, n % WR, 4 * half:4 * half + 4, 0:m], v[half][:, :, c:c + m]
                                 ).then_inc(w_in_s[n % WR], 16)

            sp.dma_start(K[:, :], consts).then_inc(c_in, 16)
            sp.dma_start(posrow, kpos).then_inc(pos_in, 16)
            for t in range(NQ + 1):
                if t >= 3:
                    sp.wait_ge(xt_ps, 2 * (t - 2))
                src = x_p[0, P * t:P * (t + 1), :] if t < NQ else x_s[:, 0, :]
                sp.dma_start(xs[0:toks(t), t % 3, :], src).then_inc(x_in[t % 3], 16)
                if t < WR:
                    load_unit(t)

            for n in range(WR, NU_ATT):
                load_unit(n)
            sp.wait_ge(xt_ps, 2 * (NQ + 1))
            for c in range(2):
                for part in range(2):
                    sp.dma_start(cw2[:, c, :, HD * part:HD * (part + 1)],
                                 cmp_w[0, c, STRIDE * part:STRIDE * (part + 1)].rearrange(
                                     "(q two) d e -> (two d) q e", two=2)).then_inc(cw_in, 16)
                    for half in range(2):
                        sp.dma_start(cw64[HD * half:HD * (half + 1), c, :, HD * part:HD * (part + 1)],
                                     cmp_w[0, c, STRIDE * part:STRIDE * (part + 1)].rearrange("l d e -> d l e")
                                     ).then_inc(cw_in, 16)
                for two in range(2):
                    sp.dma_start(cpos[HD * two:HD * (two + 1), c, :],
                                 cmp_pos[0, c].rearrange("(q two) d -> two d q", two=2)[two],
                                 allow_slow_non_contiguous=True).then_inc(cw_in, 16)
            sp.wait_ge(kt_dve, 3 * (NQ + 1))
            for i, (dst, dst_s) in enumerate(((cmp_p, cmp_s), (sel_p, sel_s))):
                sp.dma_start(dst[0, 0].rearrange("(t p) c g d -> p t (c g d)", p=P),
                             kvtok[:, 0:NQ, 256 * i:256 * (i + 1)]).then_inc(kv_out, 16)
                sp.dma_start(dst_s[0, :, 0].rearrange("b c g d -> b (c g d)"),
                             kvd[:, 256 * i:256 * (i + 1)]).then_inc(kv_out, 16)
            sp.dma_start(win_p[0, 0].rearrange("(t p) c g d -> p t (c g d)", p=P),
                         kvtok[:, NQ - WINDOW // P:NQ, 512:768]).then_inc(kv_out, 16)
            sp.dma_start(win_s[0, :, WINDOW - 1].rearrange("b c g d -> b (c g d)"),
                         kvd[:, 512:768]).then_inc(kv_out, 16)
            sp.dma_start(win_s[0, :, 0:WINDOW - 1].rearrange("b l c g d -> b (l c g d)"),
                         c_win[0, :, 1:WINDOW].rearrange("b l c g d -> b (l c g d)")).then_inc(shift_out, 16)
            sp.wait_ge(kv_out, 6 * 16)

            for n in range(NU_ATT, NU_ATT + WR):
                load_unit(n)
            sp.wait_ge(ph, 3)
            sp.dma_start(tabi, table.rearrange("b j -> j b"), allow_slow_non_contiguous=True).then_inc(tb_in, 16)
            sp.dma_start(before, before_d).then_inc(tb_in, 16)
            sp.dma_start(cmpbias, dbias[:, NSEL + NWIN:]).then_inc(tb_in, 16)
            sp.wait_ge(rank_s, 1)
            sp.dma_start(Prow[:, 0:NSEL + NWIN], dbias[:, 0:NSEL + NWIN]).then_inc(bias_in, 16)
            for b in range(NB):
                n = 32 + b
                if b < 2:
                    sp.wait_ge(v_s, 15 + b)
                    sp.wait_ge(d_ps, 2 * 16 * 2 + 2 * (15 + b))
                else:
                    sp.wait_ge(d_ps, 96 + b - 1)
                sp.dma_start(raw[:, b % 2, 0:1024].rearrange("p (l c) -> p l c", l=4),
                             c_win[0, b].rearrange("(p l) c g d -> p l (c g d)", l=4)).then_inc(wraw_in[b % 2], 16)
            sp.wait_ge(d_ps, 96 + NB)
            for b in range(NB):
                sp.dma_start(raww[:, b, :, :],
                             c_win[0, b].rearrange("(p l) c g d -> p l c (g d)", l=4)[:, :, 1, :]).then_inc(wv_in, 16)
            sp.wait_ge(ph, 6)
            for i in range(2):
                sp.dma_start(lbt[:, i, :], lb_logits[i].rearrange("(h p) -> p h", p=P),
                             allow_slow_non_contiguous=True).then_inc(small_in, 16)
            for i in range(2):
                sp.dma_start(ngt[DV * i:DV * (i + 1), :], norm_g.rearrange("a v -> v a"),
                             allow_slow_non_contiguous=True).then_inc(small_in, 16)
            for n in range(NU_ATT + WR, U_H + 2 * HG):
                load_unit(n)
            sp.wait_ge(w_ps, wstep(HG - 1, 7) + 1)
            sp.dma_start(stt, state[0].rearrange("b h k v -> k b h v")).then_inc(st_in, 16)
            sp.wait_ge(dg_dve, 3 * NB)
            sp.dma_start(hg_s[0].rearrange("b h k v -> k b h v"), stt).then_inc(hgs_out, 16)
            sp.wait_ge(hgs_out, 16)
            sp.wait_ge(hg_out, 16 * HG)
            sp.wait_ge(shift_out, 16)
            for n in range(U_M, U_M + WR):
                load_unit(n)
            sp.wait_ge(ph, 9)
            wov = w_out[0].rearrange("(k p) c -> p k c", p=P)
            sp.dma_start(wo[:, 4:8], wov[:, 4:8]).then_inc(wo_in[1], 16)
            for n in range(U_M + WR, U_U):
                load_unit(n)
            sp.wait_ge(g_ps, 4 * (NM - 1) + 2)
            sp.dma_start(wo[:, 0:4], wov[:, 0:4]).then_inc(wo_in[0], 16)
            for n in range(U_U, U_U + WR):
                load_unit(n)
            sp.wait_ge(m_dve2, NM)
            sp.dma_start(lng[:, 0, :], ln1_g.to_broadcast([P, D])).then_inc(ln_in, 16)
            sp.dma_start(lng[:, 1, :], ln1_b.to_broadcast([P, D])).then_inc(ln_in, 16)
            for t in range(NQ + 1):
                if t >= 2:
                    sp.wait_ge(f_dve, t - 1)
                src = x_p[0, P * t:P * (t + 1), :] if t < NQ else x_s[:, 0, :]
                sp.dma_start(xr[0:toks(t), t % 2, :], src).then_inc(xr_in[t % 2], 16)
            for g in range(NG):
                if g == 0:
                    sp.wait_ge(f_ps, NQ + 1)
                if g >= 2:
                    sp.wait_ge(dn_ps, 18 * (g - 1))
                sp.dma_start(wdn[:, g % 2], w_down[0, 2 * P * g:2 * P * (g + 1), :].rearrange("(j p) c -> p j c", p=P)
                             ).then_inc(wd_in[g % 2], 16)
                if g == 0:
                    sp.wait_ge(x1_s, NQ + 1)
                    sp.dma_start(lng[:, 0, :], ln2_g.to_broadcast([P, D])).then_inc(ln2_in, 16)
                    sp.dma_start(lng[:, 1, :], ln2_b.to_broadcast([P, D])).then_inc(ln2_in, 16)
                for n in range(U_U + WR + 2 * g, U_U + WR + 2 * (g + 1)):
                    if n < len(units):
                        load_unit(n)
            for t in range(NQ + 1):
                sp.wait_ge(y_s, t + 1)
                dst = y_p[0, P * t:P * (t + 1), :] if t < NQ else y_s_out[:, 0, :]
                sp.dma_start(dst, x1[0:toks(t), t, :]).then_inc(y_out, 16)
            sp.wait_ge(y_out, 16 * (NQ + 1))

        def split_product(pe, out, wh, wlow, xh, xlow):
            tiles = len(wh)
            for k in range(tiles):
                for i, (w, x) in enumerate(((wh[k], xh[k]), (wh[k], xlow[k]), (wlow[k], xh[k]))):
                    mm = pe.matmul(out, w, x, start=(k == 0 and i == 0), stop=(k == tiles - 1 and i == 2))
            return mm

        def split_high(act, n, dst):
            m = units[n][2]
            act.wait_ge(w_in_s[n % WR], 32 * (n // WR + 1))
            act.activation(dst[:, :, 0:m], wring[:, n % WR, :, 0:m], ACT.Copy).then_inc(wh_act, 1)

        def split_low(dve, n, q, high):
            m = units[n][2]
            dve.wait_ge(wh_act, q + 1)
            dve.tensor_tensor(wl[:, n % WR, :, 0:m], wring[:, n % WR, :, 0:m], high[:, :, 0:m].bitcast(F32), ALU.subtract
                              ).then_inc(wl_dve, 1)

        def unit_matmuls(pe, n):
            v, c, m, _, _ = units[n]
            pe.wait_ge(w_in_s[n % WR], 32 * (n // WR + 1))
            for ci, (c0, cn) in enumerate(CHUNKS):
                x = 3 * n + ci
                if x >= 5:
                    pe.wait_ge(u_act, x - 4)
                if n < NU_ATT:
                    mm = split_product(pe, unit_out(x, m, cn), [whA[:, n % 2, k, 0:m] for k in range(KD)],
                                       [wl[:, n % WR, k, 0:m] for k in range(KD)],
                                       [xhA[:, k, c0:c0 + cn] for k in range(KD)],
                                       [xl[:, k, c0:c0 + cn] for k in range(KD)])
                else:
                    for k in range(KD):
                        mm = pe.matmul(unit_out(x, m, cn), wring[:, n % WR, k, 0:m], xT[:, k, c0:c0 + cn],
                                       start=(k == 0), stop=(k == KD - 1))
                mm.then_inc(u_ps, 1)

        @block.tensor
        def _(pe):
            pe.wait_ge(c_in, 16)
            for t in range(NQ + 1):
                n = toks(t)
                pe.wait_ge(x_in[t % 3], 16 * (t // 3 + 1))
                for half in range(2):
                    if t >= 2:
                        pe.wait_ge(xt_dve, 2 * (t - 2) + half + 1)
                    for j in range(4):
                        k = 4 * half + j
                        mm = pe.transpose(PS[:, 2 * (t % 2) + half, P * j:P * j + n], xs[0:n, t % 3, P * k:P * (k + 1)],
                                          ident[0:n, 0:n])
                    mm.then_inc(xt_ps, 1)
            pe.wait_ge(xt_dve, 2 * (NQ + 1))
            for n in range(NU_ATT):
                pe.wait_ge(wl_dve, n + 1)
                unit_matmuls(pe, n)
            pe.wait_ge(u_act, 3 * NU_ATT)
            for t in range(NQ + 1):
                n = toks(t)
                if t >= 2:
                    pe.wait_ge(kt_dve, 3 * (t - 1))
                bank = 4 + 2 * (t % 2)
                for j in range(6):
                    mm = pe.transpose(PS[0:n, bank + j // 4, P * (j % 4):P * (j % 4 + 1)],
                                      hA[:, 4 + j, P * t:P * t + n], ident)
                    if j == 3:
                        mm.then_inc(kt_ps, 1)
                pe.transpose(PS[0:n, bank + 1, 256:280], hG[0:24, P * t:P * t + n], ident[0:24, 0:24]).then_inc(kt_ps, 1)
            pe.wait_ge(cw_in, 16 * 16)
            pe.wait_ge(kt_dve, 3 * (NQ + 1))
            for c in range(2):
                for g in range(2):
                    for l in range(STRIDE):
                        mm = pe.matmul(PS[:, 4 + g, c * NCMP_P:(c + 1) * NCMP_P],
                                       cw64[HD * g:HD * (g + 1), c, l, :],
                                       hA[HD * g:HD * (g + 1), 4 + c, l:SEQ:STRIDE],
                                       start=(l == 0), stop=(l == STRIDE - 1))
            for c in range(2):
                for q in range(16):
                    mm = pe.matmul(PS[0:HD, 2, c:c + 1], cw2[:, c, q % 8, HD * (q // 8):HD * (q // 8 + 1)],
                                   cpos[:, c, q:q + 1], start=(q == 0), stop=(q == 15))
            mm.then_inc(cp_ps, 1)
            pe.wait_ge(cp_dve, 3)
            for g in range(2):
                mm = pe.transpose(PS[0:NCMP_P, 3, HD * g:HD * (g + 1)], cmpK[:, 2 + g, :], ident[0:HD, 0:HD])
            mm.then_inc(cp_ps, 1)

            def scores(j):
                h, i, wc = job(j)
                if j % 16 == 0:
                    pe.wait_ge(q_s, 2 * (h + 1))
                    pe.wait_ge(q_row, 2 * (h + 1))
                if j % 64 == 0:
                    pe.wait_ge(ka_act, 2 * (h // 4 + 1))
                    pe.wait_ge(ka_dve, 4 * (h // 4 + 1))
                    pe.wait_ge(ka_pool, 2 * (h // 4 + 1))
                if j == 0:
                    pe.wait_ge(mk_act, 1)
                if j == 1:
                    pe.wait_ge(kc_act, 1)
                    pe.wait_ge(kc_dve, 2)
                    pe.wait_ge(ka_pool, 5)
                if j >= 2:
                    pe.wait_ge(e_act, exps(j - 2))
                qa, qb = q1[h % 2][:, P * i:P * (i + 1)], q2[h % 2][0:65, P * i:P * (i + 1)]
                g = h // 4
                if not wc:
                    spans = [(0, g, k0, min(512, P * (i + 1) - k0), k0) for k0 in range(0, P * (i + 1), 512)]
                else:
                    lo, n = P * max(0, i - 4), P * min(i + 1, 5)
                    spans = [(1, g, lo + k0, min(512, n - k0), k0) for k0 in range(0, n, 512)]
                n = spans[-1][3] + spans[-1][4]
                adds = [(n - P, mask("causal"))] + ([(0, mask("winlow"))] if wc and i >= 4 else [])
                for br, g, k0, n, col in spans:
                    out = PS[:, 2 * wc + col // 512, col % 512:col % 512 + n]
                    pe.matmul(out, qa, k1[:, br, g, k0:k0 + n], start=True, stop=False)
                    mine = [(c, m) for c, m in adds if col <= c < col + n]
                    mm = pe.matmul(out, qb, k2[br][g][0:65, k0:k0 + n], start=False, stop=True)
                    for c, m in mine:
                        mm = pe.matmul(PS[:, 2 * wc + c // 512, c % 512:c % 512 + P], mask("ident"), m, start=False,
                                       stop=True, skip_group_check=True)
                if wc:
                    pe.matmul(PS[:, 3, 128:128 + NCMP_P], qa, kc1[:, g, :], start=True, stop=False)
                    mm = pe.matmul(PS[:, 3, 128:128 + NCMP_P], qb, kc2[0:65, g, :], start=False, stop=True)
                    mm = pe.matmul(PS[:, 3, 128:128 + NCMP_P], mask("ident"), mask("cmpmask", i, NCMP_P), start=False, stop=True,
                                   skip_group_check=True)
                mm.then_inc(ss_ps, 1)

            def turn(j, gi):
                h, i, wc = job(j)
                if gi == 0:
                    pe.wait_ge(p_dve, j + 1)
                    if j >= 1:
                        pe.wait_ge(t_act, j)
                else:
                    if second_groups[j] >= 1:
                        pe.wait_ge(t_dve, second_groups[j])
                for b, (br, k0, n, col) in enumerate(groups(j)[gi]):
                    mm = pe.transpose(PS[0:n, 4 + gi, P * b:P * (b + 1)], pr[:, j % 2, col:col + n], ident)
                mm.then_inc(t_ps, 1)

            def pv(j, gi):
                h, i, wc = job(j)
                g = h // 4
                if gi == 0:
                    pe.wait_ge(t_act, j + 1)
                    if j % 2 == 0 and j >= 4:
                        pe.wait_ge(o_act, j // 2 - 1)
                else:
                    pe.wait_ge(t_dve, second_groups[j] + 1)
                last_g = gi == len(groups(j)) - 1
                for b, (br, k0, n, col) in enumerate(groups(j)[gi]):
                    if br == 2:
                        v = vcN[:, g, :]
                    else:
                        at = 384 + 256 * br + HD * g
                        v = kvtok[:, k0 // P, at:at + HD]
                    first = wc == 0 and gi == 0 and b == 0
                    last = wc == 1 and last_g and b == len(groups(j)[gi]) - 1
                    mm = pe.matmul(PS[HD * (h % 2):HD * (h % 2 + 1), 6 + i % 2, 0:P], v[0:n, :], PT[j % 2][0:n, gi, P * b:P * (b + 1)],
                                   start=first, stop=last)
                mm.then_inc(pv_ps, 1)

            scores(0)
            scores(1)
            for j in range(NJ + 1):
                if j + 2 < NJ:
                    scores(j + 2)
                if j < NJ:
                    for gi in range(len(groups(j))):
                        turn(j, gi)
                if j >= 1:
                    for gi in range(len(groups(j - 1))):
                        pv(j - 1, gi)

            pe.drain().then_inc(ph, 1)
            pe.wait_ge(ph, 3)
            pe.wait_ge(dve_r, 1)
            pe.matmul(PS[:, 7, 0:NB], const("pagespread", PAGES), tabf, start=True, stop=True).then_inc(pe_r, 1)
            pe.matmul(PS[0:NROW, 6, 0:24], const("ownT", NB), gates[0:NB, NQ, :], start=True, stop=True).then_inc(pe_r, 1)

            def cmp_turn(n):
                pe.wait_ge(raw_in[n % 2], 16 * (n // 2 + 1))
                for a, (c, par, q) in enumerate((c, par, q) for c in range(2) for par in range(2) for q in range(4)):
                    if a % 4 == 0 and n >= 1:
                        pe.wait_ge((cx_act, cx_dve)[c], 4 * (n - 1) + 2 * (par + 1))
                    at = 256 * (2 * q + par) + P * c
                    mm = pe.transpose(PS[:, a // 4, P * (a % 4):P * (a % 4 + 1)], raw[:, n % 2, at:at + P], ident)
                    if a % 4 == 3:
                        mm.then_inc(d_ps, 1)

            def cmp_products(n):
                b, half = n // 2, n % 2
                pe.wait_ge(cx_act, 4 * (n + 1))
                pe.wait_ge(cx_dve, 4 * (n + 1))
                if half == 0 and b >= 2:
                    pe.wait_ge(vc_s, b - 1)
                for c in range(2):
                    for q in range(4):
                        mm = pe.matmul(PS[:, 4 + 2 * (b % 2) + c, 0:256], cw2[:, c, 4 * half + q, :],
                                       xt2[:, n % 2, 256 * (4 * c + q):256 * (4 * c + q + 1)],
                                       start=(half == 0 and q == 0), stop=(half == 1 and q == 3))
                mm.then_inc(dc_ps, 1)

            pe.wait_ge(dve_r, 3)
            for n in range(18):
                if n < 16:
                    cmp_turn(n)
                if 1 <= n < 17:
                    cmp_products(n - 1)
                if n >= 3 and n % 2:
                    b = (n - 3) // 2
                    pe.wait_ge(kv_d, b + 1)
                    pe.transpose(PS[:, 4 + 2 * (b % 2), 256:384], vct[:, b % 2, :], ident).then_inc(vc_ps, 1)
            pe.wait_ge(kv_d, NB)
            pe.wait_ge(dve_r, 4)
            for b in range(NB):
                mm = pe.matmul(PS[0:NROW, 0, 0:NCMP_S], qbd[:, b, :], kcd[:, b, :], start=(b == 0), stop=(b == NB - 1))
            mm.then_inc(pe_r, 1)
            pe.wait_ge(dve_r, 5)
            pe.matmul(PS[0:16, 1, 0:NCMP_S], const("gsum", NROW), P_cmp, start=True, stop=True).then_inc(pe_r, 1)
            pe.wait_ge(rank_s, 1)
            pe.matmul(PS[0:NROW, 6, 0:NBLK_S], const("gspread", 16), blkm[:, 3, :], start=True, stop=True).then_inc(pe_r, 1)
            pe.wait_ge(dve_r, 6)

            def sel_turn(n):
                m = n - 16
                pe.wait_ge(raw_in[n % 2], 16 * (n // 2 + 1))
                for a in range(8):
                    if a % 4 == 0:
                        if m >= 1:
                            pe.wait_ge((d_act, d_dve)[a // 4], m)
                    mm = pe.transpose(PS[:, 4 + a // 4, P * (a % 4):P * (a % 4 + 1)],
                                      raw[:, n % 2, 256 * a:256 * a + P], ident)
                    if a % 4 == 3:
                        mm.then_inc(d_ps, 1)

            def sel_scores(m):
                b, half = m // 2, m % 2
                for s in range(2):
                    pe.wait_ge((d_act, d_dve)[s], m + 1)
                    pe.matmul(PS[0:NROW, 2 * half + s, :], qbd[:, b, :], ktd[:, s, :], start=(b == 0),
                              stop=(b == NB - 1)).then_inc(sc_ps, 1)

            for n in range(16, 32):
                sel_turn(n)
                sel_scores(n - 16)
            for s in range(2):
                for b in range(NB):
                    mm = pe.matmul(PS[0:NROW, 7, s:s + 1], qbd[:, b, :], knew[:, s, b:b + 1], start=(b == 0),
                                   stop=(b == NB - 1))
            mm.then_inc(sc_ps, 1)
            for b in range(NB):
                pe.wait_ge(wraw_in[b % 2], 16 * (b // 2 + 1))
                bank = 4 + b % 2
                pe.wait_ge(d_act, 16 + max(b - 1, 0))
                pe.wait_ge(d_dve, 16)
                for a in range(4):
                    mm = pe.transpose(PS[:, bank, P * a:P * (a + 1)], raw[:, b % 2, 256 * a:256 * a + P], ident)
                mm.then_inc(d_ps, 1)
                pe.wait_ge(d_act, 16 + b + 1)
                pe.matmul(PS[0:NROW, 6, :], qbd[:, b, :], ktd[:, b % 2, :], start=(b == 0), stop=(b == NB - 1)
                          ).then_inc(sc_ps, 1)
            pe.wait_ge(dve_r, 10)
            for a in range(16):
                pe.transpose(PS[:, a // 8, NROW * (a % 8):NROW * (a % 8 + 1)], P_sel[:, P * a:P * (a + 1)],
                             ident[0:NROW, 0:NROW])
            for a in range(4):
                pe.transpose(PS[:, 2, NROW * a:NROW * (a + 1)], P_win[:, P * a:P * (a + 1)], ident[0:NROW, 0:NROW])
            pe.transpose(PS[:, 2, 4 * NROW:5 * NROW], P_cmp, ident[0:NROW, 0:NROW])
            for s in range(2):
                mm = pe.transpose(PS[0:NB, 3, NROW * s:NROW * (s + 1)], pnew[:, s, :], ident[0:NROW, 0:NROW])
            mm.then_inc(pe_r, 1)
            pe.wait_ge(dve_r, 12)
            pe.wait_ge(v_s, 16)
            pe.wait_ge(wv_in, 16 * NB)
            for b in range(NB):
                cols, r0 = slice(8 * b, 8 * b + 8), 32 * (b % 4)
                out = PS[r0:r0 + 8, 4 + b // 4, 0:P]
                for s in range(2):
                    pe.matmul(out, pnewT[:, s, cols], kvd[:, 384 + 256 * s:512 + 256 * s], start=(s == 0), stop=False)
                for a in range(16):
                    pe.matmul(out, ptdv[:, a, cols], vall[:, b, a, :], start=False, stop=False)
                for a in range(4):
                    pe.matmul(out, ptdv[:, 16 + a, cols], raww[:, b, a, :], start=False, stop=False)
                mm = pe.matmul(out, ptdv[:, 20, cols], vcd[:, b, :], start=False, stop=True)
                mm.then_inc(pv8_ps, 1)
            pe.wait_ge(pv8_dve, NB + 1)
            for a in range(2):
                mm = pe.transpose(PS[:, 6, P * a:P * (a + 1)], acc8[:, a, :], ident)
            mm.then_inc(pe_r, 1)
            pe.drain().then_inc(ph, 1)
            pe.wait_ge(ph, 6)
            for n in range(U_IB, U_IB + 4):
                unit_matmuls(pe, n)
            unit_matmuls(pe, U_IB + 4)
            for t in range(NQ + 1):
                n = toks(t)
                if t >= 3:
                    pe.wait_ge(vt_dve, t - 2)
                pe.wait_ge(u_act, 3 * (U_IB + 4))
                for j in range(4):
                    mm = pe.transpose(PS[0:n, 5 + t % 3, P * j:P * (j + 1)], ibT[:, j, P * t:P * t + n], ident)
                mm.then_inc(vt_ps, 1)
            for n in range(U_IB + 5, U_H):
                unit_matmuls(pe, n)
            unit_matmuls(pe, U_H)
            unit_matmuls(pe, U_H + 1)
            pe.wait_ge(vt_dve, NQ + 1)

            def wbank(h, s):
                i = wstep(h, s)
                if i >= 3:
                    pe.wait_ge(*copied(i - 3))
                return 5 + i % 3

            def turn_out(h):
                pe.wait_ge(on_s, h + 1)
                for s in (9, 10):
                    bank = wbank(h, s)
                    for j in range(4):
                        mm = pe.transpose(PS[:, bank, P * j:P * (j + 1)], onb[:, 4 * (s - 9) + j, :], ident)
                    mm.then_inc(w_ps, 1)

            for h in range(HG):
                if h + 1 < HG:
                    unit_matmuls(pe, U_H + 2 * (h + 1))
                if h >= 1 and h % 2 == 0:
                    turn_out(h - 1)
                pe.wait_ge(hk, h + 1)
                for s in (0, 1):
                    bank = wbank(h, s)
                    for j in range(4):
                        t = 4 * s + j
                        mm = pe.transpose(PS[:, bank, P * j:P * (j + 1)], lcb[:, P * t:P * (t + 1)], ident)
                    mm.then_inc(w_ps, 1)
                for s in (2, 3):
                    bank = wbank(h, s)
                    for j in range(4):
                        t = 4 * (s - 2) + j
                        mm = pe.matmul(PS[:, bank, P * j:P * (j + 1)], kf[:, P * t:P * (t + 1)],
                                       qT[:, h % 2, P * t:P * (t + 1)], start=True, stop=True)
                    mm.then_inc(w_ps, 1)
                pe.wait_ge(vb_s, 4 * (h + 1))
                pe.wait_ge(*copied(wstep(h, 1)))
                for s in (4, 5, 6, 7):
                    bank = wbank(h, s)
                    for j in range(2):
                        t = 2 * (s - 4) + j
                        mm = pe.matmul(PS[:, bank, 256 * j:256 * (j + 1)], kkt[:, t, :],
                                       vbd[:, t, :, :].rearrange("p j v -> p (j v)"), start=True, stop=True)
                    mm.then_inc(w_ps, 1)
                if h + 1 < HG:
                    unit_matmuls(pe, U_H + 2 * (h + 1) + 1)
                pe.wait_ge(*copied(wstep(h, 3)))
                pe.wait_ge(s_s, NCH * (h + 1) - 1)
                bank = wbank(h, 8)
                for t in range(NQ):
                    out = PS[:, bank, DV * t:DV * (t + 1)]
                    pe.matmul(out, atm[:, t, :], vt[:, t, DV * h:DV * (h + 1)], start=True, stop=False,
                              skip_group_check=True)
                    for j in range(4):
                        c = 4 * t + j
                        if c:
                            mm = pe.matmul(out[CH * j:CH * (j + 1), :], qT[:, h % 2, CH * c:CH * (c + 1)], Sb[:, c - 1, :],
                                           start=False, stop=True, skip_group_check=True)
                mm.then_inc(w_ps, 1)
            turn_out(HG - 1)
            for b in range(NB):
                pe.wait_ge(*copied(len(wsteps) - 1))
                if b >= 3:
                    pe.wait_ge(dg_dve, 3 * (b - 2))
                pe.matmul(PS[:, 5 + b % 3, :], const("rowb", NB).rearrange("p (b n) -> p b n", b=NB)[:, b, :], vdec,
                          start=True, stop=True).then_inc(dg_ps, 1)
            pe.wait_ge(dg_dve, 3 * NB)
            for h in range(HG):
                for b in range(NB):
                    mm = pe.matmul(PS[0:NB, 5, DV * h:DV * (h + 1)], qz[:, h, b, :], stt[:, b, h, :], start=(b == 0),
                                   stop=(b == NB - 1))
            mm.then_inc(dg_ps, 1)
            pe.wait_ge(dg_dve, 3 * NB + 4)
            for j in range(4):
                mm = pe.transpose(PS[:, 6, NB * j:NB * (j + 1)], onb[0:NB, j, :], ident[0:NB, 0:NB])
            mm.then_inc(dg_ps, 1)
            pe.drain().then_inc(ph, 1)
            pe.wait_ge(ph, 9)
            for s in range(NM):
                i, ci = s // 3, s % 3
                c0, cn = CHUNKS[ci]
                if s >= 2:
                    pe.wait_ge(m_dve2, s - 1)
                if s == 0:
                    pe.wait_ge(u_act, 3 * U_M)
                for ab in range(2):
                    n = U_M + 3 * i + ab
                    if ci == 0:
                        pe.wait_ge(wl_dve, SPLITS_M + 2 * i + ab + 1)
                    if s == 0:
                        pe.wait_ge(xl_dve, KD)
                    split_product(pe, PS[:, 4 * (s % 2) + ab, 0:cn], [whM[:, 2 * (i % 2) + ab, k] for k in range(KD)],
                                  [wl[:, n % WR, k] for k in range(KD)], [xhM[:, k, c0:c0 + cn] for k in range(KD)],
                                  [xl[:, k, c0:c0 + cn] for k in range(KD)]).then_inc(g_ps, 1)
                n = U_M + 3 * i + 2
                pe.wait_ge(w_in_s[n % WR], 32 * (n // WR + 1))
                for ab, a in enumerate((aT, rT)):
                    for k in range(4):
                        mm = pe.matmul(PS[:, 4 * (s % 2) + 2 + ab, 0:cn], wring[:, n % WR, 4 * ab + k, :], a[:, k, c0:c0 + cn],
                                       start=(k == 0), stop=(k == 3))
                    mm.then_inc(g_ps, 1)
            pe.wait_ge(m_dve2, NM)

            def turn_x1(t):
                n = toks(t)
                pe.wait_ge(x1_s, t + 1)
                for half in range(2):
                    if t >= 2:
                        pe.wait_ge(x1l_dve, 2 * (t - 2) + half + 1)
                    for j in range(4):
                        k = 4 * half + j
                        mm = pe.transpose(PS[:, 4 + 2 * (t % 2) + half, P * j:P * j + n], x1[0:n, t, P * k:P * (k + 1)],
                                          ident[0:n, 0:n])
                    mm.then_inc(xt1_ps, 1)

            for t in range(NQ + 1):
                n = toks(t)
                if t >= 2:
                    pe.wait_ge(f_dve, t - 1)
                for part in (1, 0):
                    if t == 0:
                        pe.wait_ge(wo_in[part], 16)
                    for half in range(2):
                        for k in range(4 * part, 4 * part + 4):
                            mm = pe.matmul(PS[0:n, 2 * (t % 2) + half, :], mT[:, k, P * t:P * t + n],
                                           wo[:, k, 512 * half:512 * (half + 1)], start=(k == 4), stop=(k == 3))
                mm.then_inc(f_ps, 1)
                if t >= 1:
                    turn_x1(t - 1)
            turn_x1(NQ)
            pe.wait_ge(x1l_dve, 2 * (NQ + 1))

            def up(i):
                n = U_U + i
                pe.wait_ge(wl_dve, SPLITS_U + i + 1)
                for ci, (c0, cn) in enumerate(CHUNKS):
                    x = 3 * i + ci
                    if x >= 5:
                        pe.wait_ge(relu_act, x - 4)
                    split_product(pe, unit_out(x, P, cn), [whM[:, i % 2, k] for k in range(KD)],
                                  [wl[:, n % WR, k] for k in range(KD)], [x1h[:, k, c0:c0 + cn] for k in range(KD)],
                                  [xl[:, k, c0:c0 + cn] for k in range(KD)]).then_inc(u_ps, 1)

            def down(g):
                pe.wait_ge(wdl_dve, g + 1)
                pe.wait_ge(ul_dve, 2 * (g + 1))
                u, w = uR[g % 2], wdl[:, g % 2]
                for t in range(NQ + 1):
                    tk = slice(P * t, P * t + toks(t))
                    for half in range(2):
                        d, cols = 18 * g + 2 * t + half, slice(512 * half, 512 * (half + 1))
                        if d >= 3:
                            pe.wait_ge(dn_dve, d - 2)
                        split_product(pe, PS[0:toks(t), 5 + d % 3, :], [u[:, j, 1, tk] for j in range(2)],
                                      [u[:, j, 0, tk] for j in range(2)], [wdh[:, j, cols] for j in range(2)],
                                      [w[:, j, cols] for j in range(2)]).then_inc(dn_ps, 1)

            for g in range(NG):
                up(2 * g)
                up(2 * g + 1)
                if g >= 1:
                    down(g - 1)
            down(NG - 1)

        @block.scalar
        def _(act):
            act.wait_ge(c_in, 16)
            act.activation(masks[:, :], K[:, 0:masks.shape[1]], ACT.Copy).then_inc(mk_act, 1)
            for t in range(NQ + 1):
                n = toks(t)
                if t == 2 or t == 4:
                    split_high(act, t // 2 - 1, whA[:, t // 2 - 1])
                for half in range(2):
                    act.wait_ge(xt_ps, 2 * t + half + 1)
                    act.activation(xhA[:, 4 * half:4 * half + 4, P * t:P * t + n],
                                   PS[:, 2 * (t % 2) + half, :].rearrange("p (j n) -> p j n", j=4)[:, :, 0:n], ACT.Copy
                                   ).then_inc(xt_act, 1)

            def unit_copy(n):
                v, c, m, dst, fn = units[n]
                for ci, (c0, cn) in enumerate(CHUNKS):
                    act.wait_ge(u_ps, 3 * n + ci + 1)
                    act.activation(dst[0:m, c0:c0 + cn], unit_out(3 * n + ci, m, cn), fn).then_inc(u_act, 1)
            for n in range(NU_ATT):
                if 1 <= n < NU_ATT - 1:
                    act.wait_ge(u_ps, 3 * n)
                    split_high(act, n + 1, whA[:, (n + 1) % 2])
                unit_copy(n)
            def stage_q(h):
                if h >= 2:
                    act.wait_ge(ss_ps, 16 * (h - 1))
                q = hA[HD * (h % 2):HD * (h % 2 + 1), h // 2, 0:SEQ]
                act.activation(q1[h % 2][HD * (h % 2):HD * (h % 2 + 1), :], q, ACT.Copy, scale=HD ** -0.5).then_inc(q_s, 1)
                if h == 1:
                    act.wait_ge(ka_dve, 8)
                act.activation(q2[h % 2][0:HD, :], q, ACT.Copy, scale=HD ** -0.5).then_inc(q_s, 1)

            def stage_k(g):
                for br in range(2):
                    act.activation(k1[0:HD, br, g, :], hA[HD * g:HD * (g + 1), 6 + 2 * br, 0:SEQ], ACT.Copy
                                   ).then_inc(ka_act, 1)

            act.wait_ge(kt_ps, 2 * (NQ + 1))
            stage_k(0)
            stage_q(0)
            act.wait_ge(cp_ps, 1)
            act.wait_ge(kt_ps, 2 * (NQ + 1))
            act.activation(cmpT.rearrange("p (c g) n -> p g c n", c=2),
                           PS[HD:P, 4:6, 0:2 * NCMP_P].rearrange("p g (c n) -> p g c n", c=2), ACT.Copy
                           ).then_inc(cp_act, 1)

            def exp(j):
                h, i, wc = job(j)
                act.wait_ge(m_dve, j + 1)
                if j >= 2:
                    act.wait_ge(t_ps, first_group[j - 1])
                if not wc:
                    n = P * (i + 1)
                    act.activation(pr[:, 0, 0:n], PS[:, 0:2, :].rearrange("p a n -> p (a n)")[:, 0:n], ACT.Exp,
                                   bias=small[:, 16 * (j % 4):16 * (j % 4) + 1],
                                   accum_out=small[:, 16 * (j % 4) + 4:16 * (j % 4) + 5]).then_inc(e_act, 1)
                else:
                    for w, (c0, n) in enumerate(((0, P * min(i + 1, 5)), (640, NCMP_P))):
                        act.activation(pr[:, 1, c0:c0 + n], PS[:, 2:4, :].rearrange("p a n -> p (a n)")[:, c0:c0 + n],
                                       ACT.Exp, bias=small[:, 16 * (j % 4) + w:16 * (j % 4) + w + 1],
                                       accum_out=small[:, 16 * (j % 4) + 4 + w:16 * (j % 4) + 5 + w]).then_inc(e_act, 1)

            def out(n):
                h, i = heads[n]
                act.wait_ge(pv_ps, first_group[2 * n + 2])
                act.activation(aT[HD * (h % 2):HD * (h % 2 + 1), h // 2, P * i:P * (i + 1)],
                               PS[HD * (h % 2):HD * (h % 2 + 1), 6 + i % 2, 0:P], ACT.Copy).then_inc(o_act, 1)

            act.wait_ge(kt_ps, 2 * (NQ + 1))
            act.wait_ge(cp_ps, 2)
            act.wait_ge(cp_dve, 4)
            act.activation(kc1[0:HD, :, :], cmpK[:, 0:2, :], ACT.Copy).then_inc(kc_act, 1)
            exp(0)
            exp(1)
            for j in range(NJ):
                act.wait_ge(t_ps, first_group[j] + 1)
                if j >= 2:
                    act.wait_ge(pv_ps, first_group[j - 1])
                ev = evacuations(groups(j)[0])
                for e, (r, c0, c1) in enumerate(ev):
                    ins = act.activation(PT[j % 2][0:r, 0, c0:c1], PS[0:r, 4, c0:c1], ACT.Copy)
                    if e == len(ev) - 1:
                        ins.then_inc(t_act, 1)
                if j + 2 < NJ:
                    exp(j + 2)
                if j % 2 == 0 and j >= 2:
                    out(j // 2 - 1)
                if j == 2:
                    stage_k(1)
                if j % 16 == 4 and j // 16 + 1 < 8:
                    stage_q(j // 16 + 1)
            out(len(heads) - 1)

            act.drain().then_inc(ph, 1)
            act.wait_ge(ph, 3)

            def part1(b):
                act.wait_ge(dc_ps, 2 * b + 2)
                if b >= 1:
                    act.wait_ge(kv_d, b)
                act.activation(tmp1, PS[HD:P, 4 + 2 * (b % 2):6 + 2 * (b % 2), 0:256].rearrange(
                    "p c (g n) -> p c g n", g=2), ACT.Copy).then_inc(kv_a, 1)

            for n in range(16):
                for s in range(2):
                    act.wait_ge(d_ps, 4 * n + s + 1)
                    if n >= 2:
                        act.wait_ge(dc_ps, n - 1)
                    for g in range(2):
                        act.activation(xt_of(n, 0, s, g), PS[HD * g:HD * (g + 1), s, :].rearrange("p (q n) -> p q n", q=4),
                                       ACT.Copy).then_inc(cx_act, 1)
                if n >= 2 and n % 2 == 0:
                    part1(n // 2 - 1)
            part1(NB - 1)
            act.wait_ge(dve_r, 4)
            ast = Steps(act, act_r)
            act.wait_ge(dst2, 4)
            ast(act.activation(P_cmp, P_cmp, ACT.Exp, bias=dsm[:, 0:1], accum_out=dsm[:, 3:4]))
            act.wait_ge(vc_s, NB)
            for m in range(16):
                act.wait_ge(raw_in[m % 2], 16 * ((m + 16) // 2 + 1))
                act.activation(vall[:, m // 2, 8 * (m % 2):8 * (m % 2) + 8, :],
                               raw[:, m % 2, :].rearrange("p (l c) -> p l c", l=8)[:, :, P:2 * P], ACT.Copy).then_inc(v_s, 1)
                act.wait_ge(d_ps, 64 + 2 * m + 1)
                if m >= 1:
                    act.wait_ge(sc_ps, 2 * m - 1)
                act.activation(ktd[:, 0, :], PS[:, 4, :], ACT.Copy).then_inc(d_act, 1)
            for b in range(NB):
                act.wait_ge(d_ps, 96 + b + 1)
                act.wait_ge(sc_ps, (31, 32)[b] if b < 2 else 33 + b - 1)
                act.activation(ktd[:, b % 2, :], PS[:, 4 + b % 2, :], ACT.Copy).then_inc(d_act, 1)
            act.wait_ge(dve_r, 7)
            ast(act.activation(P_sel, P_sel, ACT.Exp, bias=dsm[:, 1:2], accum_out=dsm[:, 4:5]))
            act.wait_ge(dve_r, 8)
            ast(act.activation(P_win, P_win, ACT.Exp, bias=dsm[:, 2:3], accum_out=dsm[:, 5:6]))
            act.drain().then_inc(ph, 1)
            act.wait_ge(ph, 6)
            act.wait_ge(small_in, 64)
            act.wait_ge(hd, 3)
            act.activation(lbt[:, 3, :], lbt[:, 3, :], ACT.Exp).then_inc(lb_act, 1)
            act.activation(lbt[:, 4, :], lbt[:, 4, :], ACT.Exp).then_inc(lb_act, 1)
            for n in range(U_IB, U_H + 2):
                if n == U_H:
                    act.wait_ge(lb_act, 2)
                unit_copy(n)

            def step_copy(h, s):
                i = wstep(h, s)
                act.wait_ge(w_ps, i + 1)
                dst = kkt[:, 4 * s:4 * s + 4, :] if s < 2 else Ub[:, 8 * (s - 4):8 * (s - 3), :]
                if s == 0 and h >= 1:
                    act.wait_ge(w_ps, wstep(h - 1, 7) + 1)
                if s == 4:
                    act.wait_ge(vt_ps, NQ + 1)
                    if h >= 1:
                        act.wait_ge(s_s, NCH * h)
                act.activation(dst, PS[:, 5 + i % 3, :].rearrange("p (a n) -> p a n", n=dst.shape[2]), ACT.Copy
                               ).then_inc(w_act, 1)

            ra = Steps(act, r_act)

            def decay(h):
                act.wait_ge(hf, h + 1)
                if h >= 1:
                    act.wait_ge(hk, h)
                act.activation(lfb, fT[:, h % 2, 0:SEQ], ACT.Ln).then_inc(hl, 1)
                act.wait_ge(hs, h + 1)
                act.activation(lfb, lcb, ACT.Exp, scale=-1.0).then_inc(he, 1)
                act.wait_ge(he, 2 * h + 1)
                act.activation(lcb, lcb, ACT.Exp).then_inc(he, 1)

            decay(0)
            for h in range(HG):
                if h + 1 < HG:
                    if h >= 1:
                        act.wait_ge(hk, h)
                    unit_copy(U_H + 2 * (h + 1))
                for s in (0, 1, 4, 5, 6, 7):
                    step_copy(h, s)
                if h + 1 < HG:
                    if h >= 1:
                        act.wait_ge(w_ps, wstep(h - 1, 8) + 1)
                    unit_copy(U_H + 2 * (h + 1) + 1)
                    decay(h + 1)
                act.wait_ge(lb_s, h + 1)
                ra(act.activation(hsm[:, 8:16], hsm[:, 0:8], ACT.Ln, scale=1.0 / DV, bias=hsm[:, 95:96]))
                ra(act.activation(hsm[:, 16:24], hsm[:, 8:16], ACT.Exp, scale=-0.5))
            act.wait_ge(dg_dve, 3 * NB + 3)
            ra(act.activation(hsm[0:NB, 8:16], hsm[0:NB, 0:8], ACT.Ln, scale=1.0 / DV, bias=hsm[0:NB, 95:96]))
            ra(act.activation(hsm[0:NB, 16:24], hsm[0:NB, 8:16], ACT.Exp, scale=-0.5))
            act.drain().then_inc(ph, 1)
            act.wait_ge(ph, 9)
            act.wait_ge(hgs_out, 16)
            act.activation(xhM[:, 0, :], xT[:, 0, :], ACT.Copy).then_inc(xh_act, 1)
            for ab in range(2):
                split_high(act, U_M + ab, whM[:, ab])
            for k in range(1, KD):
                act.activation(xhM[:, k, :], xT[:, k, :], ACT.Copy).then_inc(xh_act, 1)
            for s in range(NM):
                cn = CHUNKS[s % 3][1]
                if s % 3 == 1 and s // 3 + 1 < KD:
                    i = s // 3 + 1
                    for ab in range(2):
                        if i >= 2:
                            act.wait_ge(*unit_done(U_M + 3 * (i - 2) + ab))
                        split_high(act, U_M + 3 * i + ab, whM[:, 2 * (i % 2) + ab])
                for ab in range(2):
                    act.wait_ge(g_ps, 4 * s + ab + 1)
                    if s >= 2:
                        act.wait_ge(m_dve2, s - 1)
                    act.activation(sgb[:, s % 2, ab, 0:cn], PS[:, 4 * (s % 2) + ab, 0:cn], ACT.Sigmoid).then_inc(m_act, 1)

            ra2 = Steps(act, ln_r)

            def rstd_of(t):
                n = toks(t)
                act.wait_ge(ln_v, t + 1)
                ra2(act.activation(rstd[0:n, 0:1], mv[0:n, 1:2], ACT.Ln, bias=epsb[0:n, :]))
                ra2(act.activation(rstd[0:n, 1:2], rstd[0:n, 0:1], ACT.Exp, scale=-0.5))

            for t in range(NQ + 1):
                n = toks(t)
                rstd_of(t)
                for half in range(2):
                    act.wait_ge(xt1_ps, 2 * t + half + 1)
                    act.activation(x1h[:, 4 * half:4 * half + 4, P * t:P * t + n],
                                   PS[:, 4 + 2 * (t % 2) + half, :].rearrange("p (j n) -> p j n", j=4)[:, :, 0:n], ACT.Copy
                                   ).then_inc(xt1_act, 1)
            act.wait_ge(f_ps, NQ + 1)
            for i in range(2):
                split_high(act, U_U + i, whM[:, i])
            for i in range(F_FF // P):
                g = i // 2
                if g >= 2:
                    act.wait_ge(dn_ps, 18 * (g - 1))
                for ci, (c0, cn) in enumerate(CHUNKS):
                    act.wait_ge(u_ps, 3 * (U_U + i - (U_U - U_M)) + ci + 1)
                    act.activation(uT[g % 2][:, i % 2, 0, c0:c0 + cn], unit_out(3 * i + ci, P, cn), ACT.Relu).then_inc(relu_act, 1)
                act.wait_ge(sq_dve, i + 1)
                act.activation(uR[g % 2][:, i % 2, 1, :], uT[g % 2][:, i % 2, 0, :], ACT.Copy).then_inc(uh_act, 1)
                if i + 2 < F_FF // P:
                    split_high(act, U_U + i + 2, whM[:, i % 2])
                if i % 2 == 1:
                    act.wait_ge(wd_in[g % 2], 16 * (g // 2 + 1))
                    if g >= 1:
                        act.wait_ge(dn_ps, 18 * g)
                    act.activation(wdh[:, :, :], wdn[:, g % 2], ACT.Copy).then_inc(wdh_act, 1)
            rn = Steps(act, l2_r)
            for t in range(NQ + 1):
                n = toks(t)
                act.wait_ge(l2_v, t + 1)
                rn(act.activation(rstd2[0:n, t, 0:1], mv2[0:n, t, 1:2], ACT.Ln, bias=epsb[0:n, :]))
                rn(act.activation(rstd2[0:n, t, 1:2], rstd2[0:n, t, 0:1], ACT.Exp, scale=-0.5))
                rn(act.activation(rstd2[0:n, t, 2:3], mv2[0:n, t, 2:3], ACT.Copy, scale=rstd2[0:n, t, 1:2]))
                act.activation(x1[0:n, t, :], x1[0:n, t, :], ACT.Identity, scale=rstd2[0:n, t, 1:2],
                               bias=rstd2[0:n, t, 2:3]).then_inc(l2_n, 1)

        @block.vector
        def _(dve):
            for t in range(NQ + 1):
                n = toks(t)
                if t == 2 or t == 4:
                    split_low(dve, t // 2 - 1, t // 2 - 1, whA[:, t // 2 - 1])
                for half in range(2):
                    dve.wait_ge(xt_act, 2 * t + half + 1)
                    s = (slice(None), slice(4 * half, 4 * half + 4), slice(P * t, P * t + n))
                    dve.tensor_tensor(xl[s], PS[:, 2 * (t % 2) + half, :].rearrange("p (j n) -> p j n", j=4)[:, :, 0:n],
                                      xhA[s].bitcast(F32), ALU.subtract).then_inc(xt_dve, 1)
            for n in range(2, NU_ATT):
                split_low(dve, n, n, whA[:, n % 2])
            dve.wait_ge(u_ps, 3 * NU_ATT)
            for k in range(5):
                dve.tensor_tensor(xT[:, k, :], xl[:, k, :].bitcast(F32), xhA[:, k, :].bitcast(F32), ALU.add).then_inc(x_dve, 1)
            dve.wait_ge(x_dve, 5)
            dve.wait_ge(x_pool, KD - 5)
            for t in range(NQ + 1):
                n = toks(t)
                dve.wait_ge(kt_ps, 2 * t + 1)
                kv = kvtok[:, t, :] if t < NQ else kvd
                dve.tensor_copy(kv[0:n, 0:512], PS[0:n, 4 + 2 * (t % 2), :]).then_inc(kt_dve, 1)
                dve.wait_ge(kt_ps, 2 * t + 2)
                dve.tensor_copy(kv[0:n, 512:768], PS[0:n, 5 + 2 * (t % 2), 0:256]).then_inc(kt_dve, 1)
                dve.tensor_copy(gates[0:n, t, :], PS[0:n, 5 + 2 * (t % 2), 256:280]).then_inc(kt_dve, 1)
            def low_k(g):
                for br in range(2):
                    k = hA[HD * g:HD * (g + 1), 6 + 2 * br, 0:SEQ]
                    dve.tensor_copy(k1[HD:P, br, g, :], k).then_inc(ka_dve, 1)
                    dve.wait_ge(ka_act, 2 * g + br + 1)
                    dve.wait_ge(ka_dve, 4 * g + 2 * br + 1)
                    dve.tensor_tensor(k2[br][g][0:HD, :], k, k1[HD * g:HD * (g + 1), br, g, :].bitcast(F32), ALU.subtract
                                      ).then_inc(ka_dve, 1)

            def slope_row(h):
                if h >= 2:
                    dve.wait_ge(ss_ps, 16 * (h - 1))
                if h == 1:
                    dve.wait_ge(ka_act, 4)
                dve.tensor_scalar(q2[h % 2][64:65, :], const("fresh")[64:65, :], 0.0, 2.0 ** -(h + 1), ALU.mult, ALU.add
                                  ).then_inc(q_row, 1)
                dve.wait_ge(q_s, 2 * h + 1)
                at, to = slice(HD * (h % 2), HD * (h % 2 + 1)), slice(HD * (1 - h % 2), HD * (2 - h % 2))
                dve.scalar_tensor_tensor(out=q1[h % 2][to, :], in0=hA[at, h // 2, 0:SEQ], scalar=HD ** -0.5,
                                         in1=q1[h % 2][at, :].bitcast(F32), op0=ALU.mult, op1=ALU.subtract).then_inc(q_row, 1)

            dve.wait_ge(kt_ps, 2 * (NQ + 1))
            low_k(0)
            slope_row(0)
            cps = Steps(dve, cp_dve)
            dve.wait_ge(cp_act, 1)
            cps(dve.tensor_copy(cb[:, 0:2], PS[0:HD, 2, 0:2]))
            cps(dve.memset(cmpK[:, :, :], 0.0))
            for c in range(2):
                s = slice(2 * c, 2 * c + 2)
                ins = dve.scalar_tensor_tensor(
                    out=cmpK[:, s, 0:NCMP_P - 1],
                    in0=PS[0:HD, 4:6, c * NCMP_P:(c + 1) * NCMP_P - 1],
                    scalar=cb[0:HD, c:c + 1], in1=cmpT[:, s, 1:NCMP_P], op0=ALU.add, op1=ALU.add)
                if c:
                    cps(ins)
            dve.wait_ge(cp_ps, 2)
            cps(dve.tensor_copy(vcN, PS[0:NCMP_P, 3, 0:P].rearrange("p (g e) -> p g e", g=2)))
            dve.tensor_copy(kc1[HD:P, :, :], cmpK[:, 0:2, :]).then_inc(kc_dve, 1)
            dve.wait_ge(kc_act, 1)
            dve.tensor_tensor(kc2[0:HD, :, :], cmpK[:, 0:2, :], kc1[0:HD, :, :].bitcast(F32), ALU.subtract).then_inc(kc_dve, 1)

            steps = Steps(dve, dch)

            def mark(ins):
                ins.then_inc(dch, 1)
                steps.n += 1

            def maxima(j):
                h, i, wc = job(j)
                dve.wait_ge(ss_ps, j + 1)
                sc = PS[:, 2 * wc:2 * wc + 2, :].rearrange("p a n -> p (a n)")
                nm = small[:, 16 * (j % 4):16 * (j % 4) + 4]
                n = P * (i + 1) if not wc else P * min(i + 1, 5)
                if wc:
                    ins = dve.tensor_reduce(nm[:, 1:2], sc[:, 640:704], AX.X, ALU.max, negate=True)
                    if i == 0:
                        steps(ins)
                        steps(dve.tensor_scalar(nm[:, 1:2], nm[:, 1:2], 1e29, None, ALU.min))
                    else:
                        mark(ins)
                dve.tensor_reduce(nm[:, 0:1], sc[:, 0:n], AX.X, ALU.max, negate=True).then_inc(m_dve, 1)

            def scale(j):
                h, i, wc = job(j)
                dve.wait_ge(e_act, exps(j))
                sm = small[:, 16 * (j % 4):16 * (j % 4) + 16]
                w = 2 if wc else 1
                if wc and i == 0:
                    steps(dve.tensor_scalar(sm[:, 5:6], sm[:, 5:6], 1e-30, None, ALU.max))
                steps(dve.reciprocal(sm[:, 8:8 + w], sm[:, 4:4 + w]))
                gt = gates[:, i, 3 * h:3 * h + 3]
                if wc:
                    mark(dve.tensor_scalar(pr[:, 1, 640:704], pr[:, 1, 640:704], sm[:, 9:10], gt[:, 0:1], ALU.mult, ALU.mult))
                n = P * (i + 1) if not wc else P * min(i + 1, 5)
                dve.tensor_scalar(pr[:, wc, 0:n], pr[:, wc, 0:n], sm[:, 8:9], gt[:, 1 + wc:2 + wc], ALU.mult, ALU.mult
                                  ).then_inc(p_dve, 1)

            def second(j):
                if len(groups(j)) < 2:
                    return
                dve.wait_ge(t_ps, first_group[j] + 2)
                if j >= 2:
                    dve.wait_ge(pv_ps, first_group[j - 1])
                ev = evacuations(groups(j)[1])
                for e, (r, c0, c1) in enumerate(ev):
                    ins = dve.tensor_copy(PT[j % 2][0:r, 1, c0:c1], PS[0:r, 5, c0:c1])
                    if e == len(ev) - 1:
                        ins.then_inc(t_dve, 1)

            maxima(0)
            maxima(1)
            scale(0)
            for j in range(NJ):
                if j + 2 < NJ:
                    maxima(j + 2)
                if j + 1 < NJ:
                    scale(j + 1)
                second(j)
                if j == 2:
                    low_k(1)
                if j % 16 == 4 and j // 16 + 1 < 8:
                    slope_row(j // 16 + 1)
            ds = Steps(dve, dst2)
            ds(dve.memset(qbd[:, :, :], 0.0))
            qf = qbd.rearrange("p b r -> p (b r)")
            for g in range(2):
                for r in range(4):
                    h = 4 * g + r
                    dve.tensor_scalar(qf[HD * g:HD * (g + 1), h:h + 72 * (NB - 1) + 1:72],
                                      hA[HD * (h % 2):HD * (h % 2 + 1), h // 2, SEQ:T], HD ** -0.5, None, ALU.mult)
            dve.tensor_copy(knew[:, 0, :], hA[:, 6, SEQ:T])
            dve.tensor_copy(knew[:, 1, :], hA[:, 8, SEQ:T])
            dve.drain().then_inc(ph, 1)
            dve.wait_ge(ph, 3)
            rs = Steps(dve, dve_r)
            dve.wait_ge(tb_in, 48)
            rs(dve.tensor_copy(tabf, tabi))
            for half in range(2):
                dve.wait_ge(pe_r, 1)
                dve.tensor_scalar(idx[:, half, :], PS[:, 7, 0:NB], 16.0, const("half")[:, half:half + 1],
                                  ALU.mult, ALU.add).then_inc(ix_s, 1)
            dve.wait_ge(pe_r, 2)
            rs(dve.tensor_tensor(g64, PS[0:NROW, 6, 0:24],
                                 const("headsel", NROW).unsqueeze(2).to_broadcast([NROW, 8, 3]), ALU.mult))
            rs(dve.tensor_reduce(grow[:, 0:3], g64.rearrange("p (h c) -> p c h", c=3), AX.X, ALU.add))
            dve.memset(kcd[:, :, NCMP_S - 1:NCMP_S], 0.0)
            ds(dve.memset(vct[:, :, NCMP_S - 1:NCMP_S], 0.0))

            def blocks_of(b):
                dve.wait_ge(kv_a, b + 1)
                if b >= 2:
                    dve.wait_ge(vc_ps, b - 1)
                for c in range(2):
                    for g in range(2):
                        dst = kcd[:, b, :] if c == 0 else vct[:, b % 2, :]
                        ins = dve.scalar_tensor_tensor(
                            out=dst[HD * g:HD * (g + 1), 0:NCMP_S - 1],
                            in0=PS[0:HD, 4 + 2 * (b % 2) + c, NCMP_S * g:NCMP_S * (g + 1) - 1],
                            scalar=cb[0:HD, c:c + 1], in1=tmp1[:, c, g, 1:NCMP_S], op0=ALU.add, op1=ALU.add)
                ins.then_inc(kv_d, 1)

            def cmp_v(b):
                dve.wait_ge(vc_ps, b + 1)
                dve.tensor_copy(vcd[:, b, :], PS[:, 4 + 2 * (b % 2), 256:384]).then_inc(vc_s, 1)

            for n in range(18):
                if n < 16:
                    for s in range(2):
                        dve.wait_ge(d_ps, 4 * n + s + 3)
                        if n >= 2:
                            dve.wait_ge(dc_ps, n - 1)
                        for g in range(2):
                            dve.tensor_copy(xt_of(n, 1, s, g), PS[HD * g:HD * (g + 1), 2 + s, :].rearrange(
                                "p (q n) -> p q n", q=4)).then_inc(cx_dve, 1)
                if n >= 2 and n % 2 == 0:
                    blocks_of(n // 2 - 1)
                if n >= 3 and n % 2:
                    cmp_v((n - 3) // 2)
            rs(dve.memset(dsm[:, 31:32], 0.0))
            dve.wait_ge(pe_r, 3)
            dve.wait_ge(tb_in, 48)
            ds(dve.tensor_tensor(P_cmp, PS[0:NROW, 0, 0:NCMP_S], cmpbias, ALU.add))
            ds(dve.tensor_reduce(dsm[:, 0:1], P_cmp, AX.X, ALU.max, negate=True))
            dve.wait_ge(act_r, 1)
            ds(dve.tensor_scalar(dsm[:, 6:7], dsm[:, 3:4], 1e-30, None, ALU.max))
            ds(dve.reciprocal(dsm[:, 7:8], dsm[:, 6:7]))
            rs(dve.tensor_scalar(P_cmp, P_cmp, dsm[:, 7:8], None, ALU.mult))
            dve.wait_ge(pe_r, 4)
            ds(dve.memset(blkm[:, 0, :], 0.0))
            ds(dve.tensor_reduce(blkm[:, 0, 0:NBLK_S - 1], PS[0:16, 1, 0:NCMP_S].rearrange("p (b r) -> p b r", r=4),
                                 AX.X, ALU.add))
            ds(dve.tensor_tensor(blkm[:, 1, :], blkm[:, 0, :], const("free", 16), ALU.mult))
            ds(dve.tensor_tensor(blkm[:, 2, :], blkm[:, 1, :], const("forced", 16), ALU.add))
            other = blkm[:, 2, :].unsqueeze(1).to_broadcast([16, NBLK_S, NBLK_S])
            own_ = blkm[:, 2, :].unsqueeze(2).to_broadcast([16, NBLK_S, NBLK_S])
            ds(dve.tensor_tensor(rk1, other, own_, ALU.is_gt))
            ds(dve.tensor_tensor(rk2, other, own_, ALU.is_equal))
            ds(dve.tensor_tensor(rk2, rk2, before, ALU.mult))
            ds(dve.tensor_tensor(rk1, rk1, rk2, ALU.add))
            ds(dve.tensor_reduce(blkm[:, 1, :], rk1, AX.X, ALU.add))
            dve.tensor_scalar(blkm[:, 3, :], blkm[:, 1, :], N_SELECT - 0.5, NEG, ALU.is_gt, ALU.mult).then_inc(rank_s, 1)
            dve.wait_ge(pe_r, 5)
            rs(dve.tensor_copy(mb64, PS[0:NROW, 6, 0:NBLK_S - 1]))
            for m in range(16):
                dve.wait_ge(d_ps, 64 + 2 * m + 2)
                if m >= 1:
                    dve.wait_ge(sc_ps, 2 * m)
                dve.tensor_copy(ktd[:, 1, :], PS[:, 5, :]).then_inc(d_dve, 1)
            dve.wait_ge(bias_in, 16)
            dve.wait_ge(sc_ps, 32)
            ds(dve.tensor_tensor(P_sel[:, 0:PAST], P_sel[:, 0:PAST], PS[0:NROW, 0:4, :].rearrange("p a n -> p (a n)"), ALU.add))
            ps4 = P_sel[:, 0:PAST].rearrange("p (l k f) -> p l k f", l=STRIDE, f=4)
            ds(dve.tensor_tensor(ps4, ps4, mb64.unsqueeze(1).unsqueeze(3).to_broadcast([NROW, STRIDE, NBLK_S - 1, 4]), ALU.add))
            dve.wait_ge(sc_ps, 33)
            ds(dve.tensor_copy(P_sel[:, PAST:NSEL], PS[0:NROW, 7, 0:1]))
            rs(dve.tensor_reduce(dsm[:, 1:2], P_sel, AX.X, ALU.max, negate=True))
            dve.wait_ge(sc_ps, 33 + NB)
            ds(dve.tensor_tensor(P_win[:, 0:WINDOW], P_win[:, 0:WINDOW], PS[0:NROW, 6, :], ALU.add))
            ds(dve.tensor_copy(P_win[:, WINDOW:NWIN], PS[0:NROW, 7, 1:2]))
            rs(dve.tensor_reduce(dsm[:, 2:3], P_win, AX.X, ALU.max, negate=True))
            dve.wait_ge(act_r, 3)
            ds(dve.reciprocal(dsm[:, 8:10], dsm[:, 4:6]))
            ds(dve.tensor_tensor(dsm[:, 10:12], dsm[:, 8:10], grow[:, 1:3], ALU.mult))
            ds(dve.tensor_scalar(P_sel, P_sel, dsm[:, 10:11], None, ALU.mult))
            ds(dve.tensor_scalar(P_win, P_win, dsm[:, 11:12], None, ALU.mult))
            ds(dve.tensor_scalar(pnew[:, 0, :], const("own", NROW), P_sel[:, PAST:NSEL], None, ALU.mult))
            rs(dve.tensor_scalar(pnew[:, 1, :], const("own", NROW), P_win[:, WINDOW:NWIN], None, ALU.mult))
            rs(dve.tensor_scalar(P_cmp, P_cmp, grow[:, 0:1], None, ALU.mult))
            dve.wait_ge(pe_r, 6)
            rs(dve.tensor_copy(ptdv[:, :, :], PS[:, 0:3, :].rearrange("p a n -> p (a n)")[:, 0:21 * NROW].rearrange(
                "p (a n) -> p a n", a=21)))
            rs(dve.tensor_copy(pnewT, PS[0:NB, 3, 0:2 * NROW].rearrange("p (s n) -> p s n", s=2)))
            dve.memset(acc8, 0.0).then_inc(pv8_dve, 1)
            dve.wait_ge(pv8_dve, 1)
            for b in range(NB):
                r0 = 32 * (b % 4)
                dve.wait_ge(pv8_ps, b + 1)
                dve.tensor_copy(acc8[r0:r0 + 8, b // 4, :], PS[r0:r0 + 8, 4 + b // 4, 0:P]).then_inc(pv8_dve, 1)
            dve.wait_ge(pe_r, 7)
            acc = PS[:, 6, 0:2 * P].rearrange("p (a j r) -> p a j r", a=2, j=4)
            for h in range(8):
                g = h // 4
                dve.tensor_copy(aT[HD * (h % 2):HD * (h % 2 + 1), h // 2, SEQ:T].rearrange("p (a j) -> p a j", a=2),
                                acc[HD * g:HD * (g + 1), :, :, h])
            dve.drain().then_inc(ph, 1)
            dve.wait_ge(ph, 6)
            hv = Steps(dve, hd)
            dve.wait_ge(small_in, 64)
            hv(dve.tensor_tensor(lbt[:, 2, :], lbt[:, 0, :], lbt[:, 1, :], ALU.max))
            hv(dve.tensor_tensor(lbt[:, 3, :], lbt[:, 0, :], lbt[:, 2, :], ALU.subtract))
            hv(dve.tensor_tensor(lbt[:, 4, :], lbt[:, 1, :], lbt[:, 2, :], ALU.subtract))
            dve.wait_ge(lb_act, 2)
            hv(dve.tensor_tensor(lbt[:, 5, :], lbt[:, 3, :], lbt[:, 4, :], ALU.add))
            hv(dve.reciprocal(lbt[:, 2, :], lbt[:, 5, :]))
            hv(dve.tensor_tensor(lbt[:, 0, :], lbt[:, 3, :], lbt[:, 2, :], ALU.mult))
            hv(dve.tensor_scalar(lbt[:, 1, :], lbt[:, 0, :], -1.0, 1.0, ALU.mult, ALU.add))
            hv(dve.memset(atm, 0.0))
            hv(dve.memset(qz, 0.0))
            hv(dve.memset(hsm[:, 95:96], LN_EPS))
            for t in range(NQ + 1):
                n = toks(t)
                dve.wait_ge(vt_ps, t + 1)
                dve.tensor_copy(vt[:, t, :] if t < NQ else vdec, PS[0:n, 5 + t % 3, :]).then_inc(vt_dve, 1)
            maskb = const("hgmask").bitcast(U32)

            def turned_out(h):
                for s in (9, 10):
                    i = wstep(h, s)
                    dve.wait_ge(w_ps, i + 1)
                    c0 = 512 * (s - 9)
                    dve.scalar_tensor_tensor(out=rT[:, h // 2, c0:c0 + 512], in0=PS[:, 5 + i % 3, :], scalar=ngt[:, 0:1],
                                             in1=gbs[:, h // 2, c0:c0 + 512], op0=ALU.mult, op1=ALU.mult
                                             ).then_inc(w_dve, 1)

            def prepare(h):
                par = h % 2
                dve.wait_ge(u_act, 3 * (U_H + 2 * h + 1))
                dve.tensor_scalar(fT[:, par, :], fT[:, par, :], lbt[:, 1, h:h + 1], lbt[:, 0, h:h + 1], ALU.mult, ALU.add
                                  ).then_inc(hf, 1)
                dve.wait_ge(hf, h + 1)
                if h >= 1:
                    dve.wait_ge(w_ps, wstep(h - 1, 3) + 1)
                hv(dve.tensor_scalar(kf, fT[:, par, :], -1.0, 1.0, ALU.mult, ALU.add))
                hv(dve.tensor_copy(dfk[:, 0, h, :], fT[:, par, SEQ:T]))
                hv(dve.tensor_copy(dfk[:, 1, h, :], kf[:, SEQ:T]))
                dve.wait_ge(hl, h + 1)
                dve.tensor_tensor_scan(lcb, const("fresh"), lfb, 0.0, ALU.mult, ALU.add).then_inc(hs, 1)
                dve.wait_ge(he, 2 * h + 2)
                dve.wait_ge(u_act, 3 * (U_H + 2 * h + 2))
                hv(dve.tensor_copy(dfk[:, 2, h, :], qT[:, par, SEQ:T]))
                hv(dve.tensor_tensor(qT[:, par, 0:SEQ], qT[:, par, 0:SEQ], lcb, ALU.mult))
                hv(dve.tensor_copy(dec, lcb[:, CH - 1:SEQ:CH]))
                hv(dve.tensor_tensor(kf[:, 0:SEQ], kf[:, 0:SEQ], lfb, ALU.mult))
                dve.tensor_tensor(lcb.rearrange("p (c i) -> p c i", c=NCH), kf[:, 0:SEQ].rearrange("p (c i) -> p c i", c=NCH),
                                  dec.unsqueeze(2).to_broadcast([P, NCH, CH]), ALU.mult).then_inc(hk, 1)
                dve.wait_ge(hk, h + 1)

            prepare(0)
            for h in range(HG):
                if h >= 1 and h % 2 == 0:
                    turned_out(h - 1)
                for s in (2, 3):
                    i = wstep(h, s)
                    dve.wait_ge(w_ps, i + 1)
                    for j in range(4):
                        ins = dve.copy_predicated(atm[:, 4 * (s - 2) + j, :], maskb, PS[:, 5 + i % 3, P * j:P * (j + 1)])
                    ins.then_inc(w_dve, 1)
                for c in range(NCH):
                    if c % 8 == 0:
                        dve.wait_ge(*copied(wstep(h, 4 + c // 8)))
                        if h >= 1 and c == 0:
                            dve.wait_ge(hg_out, 16 * h)
                    if c == 0:
                        ins = dve.tensor_copy(Sb[:, 0, :], Ub[:, 0, :])
                    else:
                        ins = dve.scalar_tensor_tensor(out=Sb[:, c, :], in0=Sb[:, c - 1, :], scalar=dec[:, c:c + 1],
                                                       in1=Ub[:, c, :], op0=ALU.mult, op1=ALU.add)
                    ins.then_inc(s_s, 1)
                    dve.wait_ge(s_s, NCH * h + c + 1)
                if h + 1 < HG:
                    prepare(h + 1)
                i = wstep(h, 8)
                dve.wait_ge(w_ps, i + 1)
                dve.tensor_copy(osb, PS[:, 5 + i % 3, :].rearrange("p (t v) -> p t v", t=NQ)).then_inc(w_dve, 1)
                dve.wait_ge(*copied(i))
                hv(dve.tensor_tensor(sqb, osb, osb, ALU.mult))
                dve.tensor_reduce(hsm[:, 0:8], sqb, AX.X, ALU.add).then_inc(lb_s, 1)
                dve.wait_ge(r_act, 2 * (h + 1))
                if h % 2 == 0 and h >= 2:
                    dve.wait_ge(w_ps, wstep(h - 1, 10) + 1)
                dve.tensor_tensor(onb[:, :, DV * (h % 2):DV * (h % 2 + 1)], osb,
                                  hsm[:, 16:24].unsqueeze(2).to_broadcast([P, NQ, DV]), ALU.mult).then_inc(on_s, 1)
                dve.wait_ge(on_s, h + 1)
            turned_out(HG - 1)
            dv = Steps(dve, dg_dve)
            for h in range(HG):
                dve.tensor_copy(qz[:, h, :, :].rearrange("p a b -> p (a b)")[:, 0:NB * NB:NB + 1], dfk[:, 2, h, :])
            dve.wait_ge(st_in, 16)
            for b in range(NB):
                dve.wait_ge(dg_ps, b + 1)
                dv(dve.tensor_tensor(sqb, PS[:, 5 + b % 3, :].rearrange("p (h v) -> p h v", h=HG),
                                     dfk[:, 1, :, b:b + 1].to_broadcast([P, HG, DV]), ALU.mult))
                dv(dve.tensor_tensor(stt[:, b, :, :], stt[:, b, :, :],
                                     dfk[:, 0, :, b:b + 1].to_broadcast([P, HG, DV]), ALU.mult))
                dv(dve.tensor_tensor(stt[:, b, :, :], stt[:, b, :, :], sqb, ALU.add))
            dve.wait_ge(dg_ps, NB + 1)
            dv(dve.tensor_copy(osb[0:NB], PS[0:NB, 5, :].rearrange("p (t v) -> p t v", t=HG)))
            dv(dve.tensor_tensor(sqb[0:NB], osb[0:NB], osb[0:NB], ALU.mult))
            dv(dve.tensor_reduce(hsm[0:NB, 0:8], sqb[0:NB], AX.X, ALU.add))
            dve.wait_ge(r_act, 2 * HG + 2)
            dve.wait_ge(w_ps, len(wsteps))
            dv(dve.tensor_tensor(onb[0:NB, 0:4, :].rearrange("p a b -> p (a b)").rearrange("p (h v) -> p h v", h=HG), osb[0:NB],
                                 hsm[0:NB, 16:24].unsqueeze(2).to_broadcast([NB, HG, DV]), ALU.mult))
            dve.wait_ge(dg_ps, NB + 2)
            for j in range(4):
                dve.scalar_tensor_tensor(out=rT[:, j, SEQ:T], in0=PS[:, 6, NB * j:NB * (j + 1)], scalar=ngt[:, 0:1],
                                         in1=gbs[:, j, SEQ:T], op0=ALU.mult, op1=ALU.mult)
            dve.drain().then_inc(ph, 1)
            dve.wait_ge(ph, 9)
            ms = Steps(dve, me_s)
            ms(dve.memset(epsb, LN_EPS))

            def x_low(k):
                dve.wait_ge(xh_act, k + 1)
                dve.tensor_tensor(xl[:, k, :], xT[:, k, :], xhM[:, k, :].bitcast(F32), ALU.subtract).then_inc(xl_dve, 1)

            x_low(0)
            for ab in range(2):
                split_low(dve, U_M + ab, SPLITS_M + ab, whM[:, ab])
            for k in range(1, KD):
                x_low(k)
            for s in range(NM):
                i, ci = s // 3, s % 3
                c0, cn = CHUNKS[ci]
                if ci == 1 and i + 1 < KD:
                    for ab in range(2):
                        split_low(dve, U_M + 3 * (i + 1) + ab, SPLITS_M + 2 * (i + 1) + ab, whM[:, 2 * ((i + 1) % 2) + ab])
                dve.wait_ge(m_act, 2 * s + 2)
                dve.wait_ge(g_ps, 4 * s + 4)
                for ab in range(2):
                    ms(dve.tensor_tensor(sgb[:, s % 2, ab, 0:cn], sgb[:, s % 2, ab, 0:cn], PS[:, 4 * (s % 2) + 2 + ab, 0:cn],
                                         ALU.mult))
                dve.tensor_tensor(mT[:, i, c0:c0 + cn], sgb[:, s % 2, 0, 0:cn], sgb[:, s % 2, 1, 0:cn], ALU.add
                                  ).then_inc(m_dve2, 1)
            lc = Steps(dve, ln_c)

            def norm(t, done):
                n = toks(t)
                y = x1[0:n, t, :]
                lc(dve.bn_stats(stats[0:n, 0, :], y[:, 0:512]))
                lc(dve.bn_stats(stats[0:n, 1, :], y[:, 512:D]))
                dve.bn_aggr(mv[0:n, :], stats[0:n, :, :]).then_inc(ln_v, 1)
                dve.wait_ge(ln_r, 2 * (t + 1))
                lc(dve.tensor_scalar(y, y, mv[0:n, 0:1], rstd[0:n, 1:2], ALU.subtract, ALU.mult))
                lc(dve.tensor_tensor(y, y, lng[0:n, 0, :], ALU.mult))
                dve.tensor_tensor(y, y, lng[0:n, 1, :], ALU.add).then_inc(done, 1)

            def x1_low(t):
                for half in range(2):
                    dve.wait_ge(xt1_act, 2 * t + half + 1)
                    at = (slice(None), slice(4 * half, 4 * half + 4), slice(P * t, P * t + toks(t)))
                    dve.tensor_tensor(xl[at], PS[:, 4 + 2 * (t % 2) + half, :].rearrange("p (j n) -> p j n", j=4)[:, :, 0:toks(t)],
                                      x1h[at].bitcast(F32), ALU.subtract).then_inc(x1l_dve, 1)

            dve.wait_ge(ln_in, 32)
            for t in range(NQ + 1):
                n = toks(t)
                dve.wait_ge(f_ps, t + 1)
                dve.wait_ge(xr_in[t % 2], 16 * (t // 2 + 1))
                dve.scalar_tensor_tensor(out=x1[0:n, t, :], in0=xr[0:n, t % 2, :], scalar=ALPHA,
                                         in1=PS[0:n, 2 * (t % 2):2 * (t % 2) + 2, :].rearrange("p a n -> p (a n)"),
                                         op0=ALU.mult, op1=ALU.add).then_inc(f_dve, 1)
                dve.wait_ge(f_dve, t + 1)
                norm(t, x1_s)
                if t >= 1:
                    m = toks(t - 1)
                    x1_low(t - 1)
                    dve.tensor_scalar(x1[0:m, t - 1, :], x1[0:m, t - 1, :], ALPHA, None, ALU.mult).then_inc(x1_sc, 1)
            x1_low(NQ)
            dve.wait_ge(x1_s, NQ + 1)
            dve.tensor_scalar(x1[0:NB, NQ, :], x1[0:NB, NQ, :], ALPHA, None, ALU.mult).then_inc(x1_sc, 1)
            dve.wait_ge(x1_sc, NQ + 1)
            dve.wait_ge(ln2_in, 32)
            for i in range(2):
                split_low(dve, U_U + i, SPLITS_U + i, whM[:, i])

            def square(i):
                u = uT[(i // 2) % 2][:, i % 2, 0, :]
                dve.wait_ge(relu_act, 3 * (i + 1))
                dve.tensor_tensor(u, u, u, ALU.mult).then_inc(sq_dve, 1)

            def hidden_low(i):
                g = i // 2
                dve.wait_ge(uh_act, i + 1)
                dve.tensor_tensor(uR[g % 2][:, i % 2, 0, :], uT[g % 2][:, i % 2, 0, :],
                                  uR[g % 2][:, i % 2, 1, :].bitcast(F32), ALU.subtract).then_inc(ul_dve, 1)

            def weights_low(i):
                if i < F_FF // P:
                    split_low(dve, U_U + i, SPLITS_U + i, whM[:, i % 2])

            def moments(t):
                n = toks(t)
                for half in range(2):
                    lc(dve.bn_stats(stats2[0:n, t, half, :], x1[0:n, t, 512 * half:512 * (half + 1)]))
                lc(dve.bn_aggr(mv2[0:n, t, 0:2], stats2[0:n, t, :, :]))
                dve.tensor_scalar(mv2[0:n, t, 2:3], mv2[0:n, t, 0:1], -1.0, None, ALU.mult).then_inc(l2_v, 1)

            def shift(t):
                dve.wait_ge(l2_g, t + 1)
                y = x1[0:toks(t), t, :]
                dve.tensor_tensor(y, y, lng[0:toks(t), 1, :], ALU.add).then_inc(y_s, 1)

            for g in range(NG + 1):
                if g < NG:
                    square(2 * g)
                    hidden_low(2 * g)
                    weights_low(2 * g + 2)
                    square(2 * g + 1)
                if g == 0:
                    hidden_low(1)
                    weights_low(3)
                else:
                    for t in range(NQ + 1):
                        if g < NG and t == 1:
                            hidden_low(2 * g + 1)
                        if g < NG and t == 2:
                            weights_low(2 * g + 3)
                        n = toks(t)
                        for half in range(2):
                            d = 18 * (g - 1) + 2 * t + half
                            dve.wait_ge(dn_ps, d + 1)
                            if g > 1:
                                dve.wait_ge(dn_dve, d - 17)
                            y = x1[0:n, t, 512 * half:512 * (half + 1)]
                            dve.tensor_tensor(y, y, PS[0:n, 5 + d % 3, :], ALU.add).then_inc(dn_dve, 1)
                        if g == NG:
                            dve.wait_ge(dn_dve, d + 1)
                            moments(t)
                            if t >= 2:
                                shift(t - 2)
                if g < NG:
                    dve.wait_ge(wdh_act, g + 1)
                    dve.tensor_tensor(wdl[:, g % 2], wdn[:, g % 2], wdh[:, :, :].bitcast(F32), ALU.subtract
                                      ).then_inc(wdl_dve, 1)
            shift(NQ - 1)
            shift(NQ)

        @block.gpsimd
        def _(pool):
            pool.wait_ge(u_ps, 3 * NU_ATT)
            pool.wait_ge(xt_dve, 2 * (NQ + 1))
            for k in range(5, KD):
                pool.tensor_tensor(xT[:, k, :], xl[:, k, :].bitcast(F32), xhA[:, k, :].bitcast(F32), ALU.add).then_inc(x_pool, 1)
            pool.wait_ge(pos_in, 16)
            pool.wait_ge(kt_ps, 2 * (NQ + 1))
            for g in range(2):
                if g:
                    pool.wait_ge(cp_ps, 1)
                for br in range(2):
                    pool.tensor_copy(k2[br][g][64:65, :], posrow[:, 0:SEQ]).then_inc(ka_pool, 1)
            pool.tensor_copy(kc2[64:65, :, :], posrow[:, SEQ:].rearrange("a (g n) -> a g n", g=2)).then_inc(ka_pool, 1)
            pool.wait_ge(ix_s, 2)
            for n in range(32):
                src = (c_cmp if n < 16 else c_sel)[0].rearrange("n (r l) c g d -> (n r) (l c g d)", l=8)
                b, half = (n % 16) // 2, n % 2
                if n >= 2:
                    pool.wait_ge(d_ps, 4 * (n - 1) if n <= 17 else 64 + 2 * (n - 17))
                if n >= 18:
                    pool.wait_ge(v_s, n - 17)
                pool.indirect_dma_start(out=raw[:, n % 2, :], out_offset=None, in_=src,
                                        in_offset=bass.IndirectOffsetOnAxis(ap=idx[:, half, b:b + 1], axis=0)
                                        ).then_inc(raw_in[n % 2], 16)
            pool.wait_ge(ph, 6)
            pool.memset(vbd, 0.0).then_inc(zd, 1)
            pool.wait_ge(zd, 1)
            pool.wait_ge(vt_dve, NQ + 1)
            for h in range(HG + 1):
                if h < HG:
                    if h >= 1:
                        pool.wait_ge(w_ps, wstep(h - 1, 7) + 1)
                    for j in range(4):
                        pool.tensor_copy(vbd[CH * j:CH * (j + 1), :, j, :],
                                         vt[CH * j:CH * (j + 1), :, DV * h:DV * (h + 1)]).then_inc(vb_s, 1)
                if h >= 1:
                    pool.wait_ge(s_s, NCH * h)
                    pool.dma_start(hg_p[0, 0, h - 1], Sb[:, NCH - 1, :]).then_inc(hg_out, 16)
            pool.wait_ge(ln2_in, 32)
            for t in range(NQ + 1):
                pool.wait_ge(l2_n, t + 1)
                y = x1[0:toks(t), t, :]
                pool.tensor_tensor(y, y, lng[0:toks(t), 0, :], ALU.mult).then_inc(l2_g, 1)


_INS = ['x_prompt', 'x_sample', 'cache_cmp_kv', 'cache_sel_kv', 'cache_win_kv', 'state_hgrn', 'page_table', 'w_in',
        'cmp_w', 'cmp_pos', 'hgrn_lb_logits', 'hgrn_norm_g', 'w_br_a', 'w_br_b', 'w_out', 'ln1_g', 'ln1_b', 'w_up',
        'w_down', 'ln2_g', 'ln2_b']
_KV = (2, GROUPS, HD)
_OUTS = [(1, SEQ, D), (NB, 1, D), (1, 1, SEQ) + _KV, (1, 1, SEQ) + _KV, (1, 1, WINDOW) + _KV, (1, 1, HG, P, DV),
         (1, NB, 1) + _KV, (1, NB, 1) + _KV, (1, NB, WINDOW) + _KV, (1, NB, HG, P, DV)]


def kernel(**inputs):
    import concourse.bacc as _bacc
    from concourse.bass_utils import run_bass_kernel_spmd as _run

    nc = _bacc.Bacc("TRN2", target_bir_lowering=False, num_devices=1)
    arrays, args = {}, []
    given = {name: np.ascontiguousarray(inputs[name]) for name in _INS}
    given["consts"], given["kpos"], given["dbias"], given["before"] = (constants(), positions(), decode_biases(),
                                                                       block_order())
    for name, a in given.items():
        arrays[f"in_{name}"] = a
        args.append(nc.dram_tensor(f"in_{name}", a.shape, mybir.dt.from_np(a.dtype), kind="ExternalInput").ap())
    for i, shape in enumerate(_OUTS):
        args.append(nc.dram_tensor(f"out_{i}", shape, F32, kind="ExternalOutput").ap())
    hybrid_step(nc, *args)
    r = _run(nc, [arrays], core_ids=[0])
    return tuple(r.results[0][f"out_{i}"] for i in range(len(_OUTS)))
```
